# Optimizing a Trainium2 kernel written in Bass

```python
import math
import jax, jax.numpy as jnp
from jax import lax
import numpy as np

D_MODEL = 1024
BATCH = 1
SEQ = 256
DEPTH = 2

HEAD_DIM = 64
N_HEADS_A = 8
A_QK_DIM = 32
A_V_DIM = 2 * A_QK_DIM
N_HEADS_B = 8
N_HEADS_C = 8
N_HEADS_D = 8
A_QK_W = N_HEADS_A * 2 * A_QK_DIM
A_V_W = N_HEADS_A * A_V_DIM
B_W = N_HEADS_B * HEAD_DIM
C_W = N_HEADS_C * HEAD_DIM
D_W = N_HEADS_D * HEAD_DIM
AB_SPLITS = (A_QK_W, A_QK_W, A_V_W, B_W, B_W, B_W)
CD_SPLITS = (C_W, C_W, C_W, D_W, D_W, D_W, N_HEADS_D)
AB_IN = 2 * A_QK_W + A_V_W + 3 * B_W
AB_OUT = A_V_W + B_W
CD_IN = 3 * C_W + 3 * D_W + N_HEADS_D
CD_OUT = C_W + D_W
N_EVEN = (DEPTH + 1) // 2
N_ODD = DEPTH // 2
Q_BLOCK = 128
T5_BUCKETS = 32
T5_MAX_DIST = 128
N_T5_HEADS = 8
DILATED_PATTERNS = ((128, 1), (512, 4), (2048, 16))
PEER_HEADS = 8
PEER_NKEYS = 128
PEER_EXPERTS = PEER_NKEYS * PEER_NKEYS
PEER_DKEY = 256
PEER_TOPK = 16
PEER_TOKEN_BLOCK = 128
DN_ALPHA = (2 * DEPTH) ** 0.25
DN_BETA = (8 * DEPTH) ** -0.25
LN_EPS = 1e-5

kernel_name = "hybrid_diff_stickbreak_dilated_fox_peer"

def layer_norm(x, g, b):
    xf = x.astype(jnp.float32)
    mu = jnp.mean(xf, axis=-1, keepdims=True)
    var = jnp.mean(jnp.square(xf - mu), axis=-1, keepdims=True)
    return ((xf - mu) * lax.rsqrt(var + LN_EPS) * g + b).astype(x.dtype)

def split_cols(t, sizes):
    out, start = [], 0
    for n in sizes:
        out.append(t[..., start:start + n])
        start += n
    return out

def to_heads(t, n_heads):
    B, S, _ = t.shape
    return t.reshape(B, S, n_heads, -1).transpose(0, 2, 1, 3)

def merge_heads(o):
    B, H, S, d = o.shape
    return o.transpose(0, 2, 1, 3).reshape(B, S, H * d)

def to_q_blocks(t):
    B, H, S = t.shape[:3]
    t = t.reshape((B, H, S // Q_BLOCK, Q_BLOCK) + t.shape[3:])
    return jnp.moveaxis(t, 2, 0)

def from_q_blocks(o):
    o = jnp.moveaxis(o, 0, 2)
    return o.reshape(o.shape[0], o.shape[1], -1, o.shape[-1])

def t5_bucket(dist):
    max_exact = T5_BUCKETS // 2
    n = jnp.maximum(dist, 0)
    nf = jnp.maximum(n, 1).astype(jnp.float32)
    large = max_exact + (jnp.log(nf / max_exact) / math.log(T5_MAX_DIST / max_exact)
                         * (T5_BUCKETS - max_exact)).astype(jnp.int32)
    large = jnp.minimum(large, T5_BUCKETS - 1)
    return jnp.where(n < max_exact, n, large)

def diff_attention(q, k, v, t5_bias, lam, lambda_init, subln_g):
    S = q.shape[2]
    scale = A_QK_DIM ** -0.5
    kpos = jnp.arange(S)

    def block(args):
        i, qi = args
        qpos = i * Q_BLOCK + jnp.arange(Q_BLOCK)
        dist = qpos[:, None] - kpos[None, :]
        bias = jnp.moveaxis(t5_bias[t5_bucket(dist)], -1, 0).astype(jnp.float32)
        logits = jnp.einsum('bhqcd,bhscd->bhcqs', qi, k).astype(jnp.float32) * scale
        logits = logits + bias[None, :, None]
        logits = jnp.where(dist >= 0, logits, -jnp.inf)
        p = jax.nn.softmax(logits, axis=-1)
        w = p[:, :, 0] - lam * p[:, :, 1]
        return jnp.einsum('bhqs,bhsd->bhqd', w.astype(v.dtype), v)

    nb = S // Q_BLOCK
    o = from_q_blocks(lax.map(block, (jnp.arange(nb), to_q_blocks(q))))
    of = o.astype(jnp.float32)
    of = of * lax.rsqrt(jnp.mean(jnp.square(of), axis=-1, keepdims=True) + LN_EPS)
    return (of * subln_g * (1.0 - lambda_init)).astype(v.dtype)

def stick_breaking_attention(q, k, v):
    S, d = q.shape[2], q.shape[3]
    scale = d ** -0.5
    kpos = jnp.arange(S)

    def block(args):
        i, qi = args
        qpos = i * Q_BLOCK + jnp.arange(Q_BLOCK)
        past = kpos[None, :] < qpos[:, None]
        z = jnp.einsum('bhqd,bhsd->bhqs', qi, k).astype(jnp.float32) * scale
        log_beta = jax.nn.log_sigmoid(z)
        log_rem = jnp.where(past, jax.nn.log_sigmoid(-z), 0.0)
        after = lax.cumsum(log_rem, axis=3, reverse=True) - log_rem
        w = jnp.where(past, jnp.exp(log_beta + after), 0.0)
        return jnp.einsum('bhqs,bhsd->bhqd', w.astype(v.dtype), v)

    nb = S // Q_BLOCK
    return from_q_blocks(lax.map(block, (jnp.arange(nb), to_q_blocks(q))))

def dilated_attention(q, k, v, t5_bias):
    B, H, S, d = q.shape
    scale = d ** -0.5

    def block(args):
        i, qi = args
        qpos = i * Q_BLOCK + jnp.arange(Q_BLOCK)
        ms, ss, os_ = [], [], []
        for window, dil in DILATED_PATTERNS:
            n_keys = window // dil + 1
            dist = jnp.arange(n_keys) * dil
            kidx = qpos[:, None] - dist[None, :]
            valid = kidx >= 0
            kidx = jnp.maximum(kidx, 0).reshape(-1)
            kg = jnp.take(k, kidx, axis=2).reshape(B, H, Q_BLOCK, n_keys, d)
            vg = jnp.take(v, kidx, axis=2).reshape(B, H, Q_BLOCK, n_keys, d)
            bias = t5_bias[t5_bucket(dist)].T.astype(jnp.float32)
            logits = jnp.einsum('bhqd,bhqjd->bhqj', qi, kg).astype(jnp.float32) * scale
            logits = jnp.where(valid, logits + bias[None, :, None, :], -jnp.inf)
            m = jnp.max(logits, axis=-1)
            e = jnp.exp(logits - m[..., None])
            s = jnp.sum(e, axis=-1)
            o = jnp.einsum('bhqj,bhqjd->bhqd', e, vg.astype(jnp.float32)) / s[..., None]
            ms.append(m)
            ss.append(s)
            os_.append(o)
        m_all = jnp.maximum(jnp.maximum(ms[0], ms[1]), ms[2])
        wts = [s * jnp.exp(m - m_all) for m, s in zip(ms, ss)]
        num = sum(w[..., None] * o for w, o in zip(wts, os_))
        den = sum(wts)
        return (num / den[..., None]).astype(q.dtype)

    nb = S // Q_BLOCK
    return from_q_blocks(lax.map(block, (jnp.arange(nb), to_q_blocks(q))))

def forgetting_attention(q, k, v, log_f):
    S, d = q.shape[2], q.shape[3]
    scale = d ** -0.5
    kpos = jnp.arange(S)
    F = jnp.cumsum(log_f, axis=-1)

    def block(args):
        i, qi, Fi = args
        qpos = i * Q_BLOCK + jnp.arange(Q_BLOCK)
        causal = kpos[None, :] <= qpos[:, None]
        logits = jnp.einsum('bhqd,bhsd->bhqs', qi, k).astype(jnp.float32) * scale
        logits = logits + Fi[..., :, None] - F[:, :, None, :]
        logits = jnp.where(causal, logits, -jnp.inf)
        p = jax.nn.softmax(logits, axis=-1)
        return jnp.einsum('bhqs,bhsd->bhqd', p.astype(v.dtype), v)

    nb = S // Q_BLOCK
    return from_q_blocks(lax.map(block, (jnp.arange(nb), to_q_blocks(q), to_q_blocks(F))))

def ab_mixer(h, t5_bias, w_in, lam_vecs, subln_g, w_out, lambda_init):
    B, S, _ = h.shape
    aq, ak, av, bq, bk, bv = split_cols(h @ w_in, AB_SPLITS)
    aq = aq.reshape(B, S, N_HEADS_A, 2, A_QK_DIM).transpose(0, 2, 1, 3, 4)
    ak = ak.reshape(B, S, N_HEADS_A, 2, A_QK_DIM).transpose(0, 2, 1, 3, 4)
    lv = lam_vecs.astype(jnp.float32)
    lam = jnp.exp(jnp.sum(lv[0] * lv[1])) - jnp.exp(jnp.sum(lv[2] * lv[3])) + lambda_init
    oa = diff_attention(aq, ak, to_heads(av, N_HEADS_A), t5_bias, lam, lambda_init, subln_g)
    ob = stick_breaking_attention(to_heads(bq, N_HEADS_B), to_heads(bk, N_HEADS_B), to_heads(bv, N_HEADS_B))
    return jnp.concatenate([merge_heads(oa), merge_heads(ob)], axis=-1) @ w_out

def cd_mixer(h, t5_bias, w_in, b_f, w_out):
    cq, ck, cv, dq, dk, dv, fg = split_cols(h @ w_in, CD_SPLITS)
    oc = dilated_attention(to_heads(cq, N_HEADS_C), to_heads(ck, N_HEADS_C), to_heads(cv, N_HEADS_C), t5_bias)
    log_f = jax.nn.log_sigmoid(fg.astype(jnp.float32) + b_f).transpose(0, 2, 1)
    od = forgetting_attention(to_heads(dq, N_HEADS_D), to_heads(dk, N_HEADS_D), to_heads(dv, N_HEADS_D), log_f)
    return jnp.concatenate([merge_heads(oc), merge_heads(od)], axis=-1) @ w_out

def peer(x, w_q, sub_keys, u, v):
    B, S, D = x.shape
    xt = x.reshape(B * S // PEER_TOKEN_BLOCK, PEER_TOKEN_BLOCK, D)

    def block(xb):
        q = (xb @ w_q).reshape(PEER_TOKEN_BLOCK, PEER_HEADS, 2, PEER_DKEY // 2)
        sc = jnp.einsum('thcd,hckd->thck', q, sub_keys).astype(jnp.float32)
        top_s, top_i = lax.top_k(sc, PEER_TOPK)
        cand_s = top_s[:, :, 0, :, None] + top_s[:, :, 1, None, :]
        cand_i = top_i[:, :, 0, :, None] * PEER_NKEYS + top_i[:, :, 1, None, :]
        cand_s = cand_s.reshape(PEER_TOKEN_BLOCK, PEER_HEADS, PEER_TOPK * PEER_TOPK)
        cand_i = cand_i.reshape(PEER_TOKEN_BLOCK, PEER_HEADS, PEER_TOPK * PEER_TOPK)
        best_s, pos = lax.top_k(cand_s, PEER_TOPK)
        idx = jnp.take_along_axis(cand_i, pos, axis=-1)
        g = jax.nn.softmax(best_s, axis=-1)
        ug = jnp.take(u, idx, axis=0)
        vg = jnp.take(v, idx, axis=0)
        act = jax.nn.gelu(jnp.einsum('thkd,td->thk', ug, xb), approximate=False)
        return jnp.einsum('thk,thkd->td', (g * act.astype(jnp.float32)).astype(vg.dtype), vg)

    return lax.map(block, xt).reshape(B, S, D)

def _col_scale(sizes, value_slots):
    return jnp.concatenate([jnp.full((n,), DN_BETA if i in value_slots else 1.0, jnp.float32)
                            for i, n in enumerate(sizes)])

def setup_inputs(seed: int = 0) -> dict:
    key = jax.random.key(seed)
    ks = jax.random.split(key, 18)

    def nrm(k, shape, s):
        return jax.random.normal(k, shape, jnp.float32) * s

    x = nrm(ks[0], (BATCH, SEQ, D_MODEL), 1.0)
    t5_bias = nrm(ks[1], (T5_BUCKETS, N_T5_HEADS), 0.5)
    ab_w_in = nrm(ks[2], (N_EVEN, D_MODEL, AB_IN), D_MODEL ** -0.5) * _col_scale(AB_SPLITS, (2, 5))
    ab_lambda = nrm(ks[3], (N_EVEN, 4, A_QK_DIM), 0.1)
    ab_subln_g = 1.0 + nrm(ks[4], (N_EVEN, A_V_DIM), 0.02)
    ab_w_out = nrm(ks[5], (N_EVEN, AB_OUT, D_MODEL), AB_OUT ** -0.5 * DN_BETA)
    cd_w_in = nrm(ks[6], (N_ODD, D_MODEL, CD_IN), D_MODEL ** -0.5) * _col_scale(CD_SPLITS, (2, 5))
    cd_b_f = 3.0 + nrm(ks[7], (N_ODD, N_HEADS_D), 0.1)
    cd_w_out = nrm(ks[8], (N_ODD, CD_OUT, D_MODEL), CD_OUT ** -0.5 * DN_BETA)
    peer_w_q = nrm(ks[9], (DEPTH, D_MODEL, PEER_HEADS * PEER_DKEY), D_MODEL ** -0.5)
    peer_sub_keys = nrm(ks[10], (DEPTH, PEER_HEADS, 2, PEER_NKEYS, PEER_DKEY // 2), (PEER_DKEY // 2) ** -0.5)
    peer_u = nrm(ks[11], (DEPTH, PEER_EXPERTS, D_MODEL), D_MODEL ** -0.5)
    peer_v = nrm(ks[12], (DEPTH, PEER_EXPERTS, D_MODEL), DN_BETA)
    ln_g = 1.0 + nrm(ks[13], (DEPTH, 2, D_MODEL), 0.02)
    ln_b = nrm(ks[14], (DEPTH, 2, D_MODEL), 0.02)
    return {"x": x, "t5_bias": t5_bias, "ab_w_in": ab_w_in, "ab_lambda": ab_lambda,
            "ab_subln_g": ab_subln_g, "ab_w_out": ab_w_out, "cd_w_in": cd_w_in, "cd_b_f": cd_b_f,
            "cd_w_out": cd_w_out, "peer_w_q": peer_w_q, "peer_sub_keys": peer_sub_keys,
            "peer_u": peer_u, "peer_v": peer_v, "ln_g": ln_g, "ln_b": ln_b}

def reference(x, t5_bias, ab_w_in, ab_lambda, ab_subln_g, ab_w_out, cd_w_in, cd_b_f, cd_w_out,
              peer_w_q, peer_sub_keys, peer_u, peer_v, ln_g, ln_b):
    h = x
    for layer in range(DEPTH):
        j = layer // 2
        if layer % 2 == 0:
            lambda_init = 0.8 - 0.6 * math.exp(-0.3 * layer)
            mix = ab_mixer(h, t5_bias, ab_w_in[j], ab_lambda[j], ab_subln_g[j], ab_w_out[j], lambda_init)
        else:
            mix = cd_mixer(h, t5_bias, cd_w_in[j], cd_b_f[j], cd_w_out[j])
        h = layer_norm(DN_ALPHA * h + mix, ln_g[layer, 0], ln_b[layer, 0])
        ffn = peer(h, peer_w_q[layer], peer_sub_keys[layer], peer_u[layer], peer_v[layer])
        h = layer_norm(DN_ALPHA * h + ffn, ln_g[layer, 1], ln_b[layer, 1])
    return h


_drawn_inputs = setup_inputs


def setup_inputs(seed=0):
    import zlib

    import numpy as np

    out = dict(_drawn_inputs(seed))
    spreads = {}
    factors = {'cd_b_f': 48.952}
    for name, (base, spread) in spreads.items():
        noise = np.random.default_rng([zlib.crc32(name.encode()), seed]).standard_normal(out[name].shape)
        drawn = base * np.exp(spread * noise) if base else spread * noise
        out[name] = __import__('jax').numpy.asarray(drawn.astype(out[name].dtype))
    for name, factor in factors.items():
        out[name] = (out[name] * factor).astype(out[name].dtype)
    return out
```

```python
from contextlib import ExitStack

import numpy as np

import concourse.bass as bass
from concourse import mybir

F32 = mybir.dt.float32
F32R = mybir.dt.float32r
U32 = mybir.dt.uint32
ALU = mybir.AluOpType
ACT = mybir.ActivationFunctionType
AX = mybir.AxisListType
ds = bass.ds

P = 128
SEQ = 256
TB = SEQ // P
D = 1024
DC = D // P
LAYERS = 2
HEADS = 8
HD = 64
NKEYS = 128
TOPK = 16
EXPERT_ITEMS = NKEYS
IN_ITEMS = 24
OUT_ITEMS = 8
Q_ITEMS = 16
V_FIRST, V_ITEMS = 8, 8
N_OUT = IN_ITEMS
N_Q = N_OUT + OUT_ITEMS
N_U = N_Q + Q_ITEMS
ITEMS = N_U + EXPERT_ITEMS
EVACS = ITEMS - OUT_ITEMS
RAW = 4
AHEAD = 32
GROUP = 4
GATE_LAG = 2
ALPHA = (2 * LAYERS) ** 0.25
LN_EPS = 1e-5
LAMBDA_INIT = 0.2
NEG = -1.0e30
LOWEST = -3.0e38
REL = 384
W3 = 384

C_KEEP = 2 * P
(C_GE, C_LE, C_NLE, C_ONE, C_NONE, C_STICK, C_PAST, C_CAUSAL) = (
    0, P, 2 * P, 3 * P, 4 * P, 5 * P, 5 * P + W3, 5 * P + 2 * W3)
C_COLS = 5 * P + 3 * W3
SOFT_A, SOFT_C, SOFT_D = 8, 4, 4


def build_program(nc, x, u_stream, v_stream, keys, t5, onehot, relmask, lam_vecs, subln, w_f, b_f,
                  ln_g, ln_b, consts, out):
    scratch = nc.dram_tensor("bias_rows", [LAYERS, HEADS, P, REL], F32, kind="Internal").ap()

    with ExitStack() as ctx:
        def sb(name, shape, dt=F32):
            return ctx.enter_context(nc.sbuf_tensor(name, shape, dt))

        def sem(name):
            return ctx.enter_context(nc.semaphore(name))

        gates = sb("gates", [P, SEQ, NKEYS])
        flat = gates[:, :, :].rearrange("p t j -> p (t j)")
        used = [0]

        def carve(*shape):
            n = int(np.prod(shape))
            a = flat[:, used[0]:used[0] + n]
            used[0] += n
            assert used[0] <= SEQ * NKEYS
            if len(shape) == 2:
                return a.rearrange("p (a b) -> p a b", a=shape[0])
            if len(shape) == 3:
                return a.rearrange("p (a b c) -> p a b c", a=shape[0], b=shape[1])
            return a

        u_raw = sb("u_raw", [P, RAW, DC, P])
        u_hi = sb("u_hi", [P, 2, DC, P], F32R)
        u_lo = sb("u_lo", [P, 2, DC, P], F32R)
        v_raw = sb("v_raw", [P, 2, D])
        v_hi_at = nc.sbuf_base
        v_hi = sb("v_hi", [P, 2, D], F32R)
        v_lo = sb("v_lo", [P, 2, D], F32R)
        xT_hi = sb("xT_hi", [P, DC, SEQ], F32R)
        xT_lo = sb("xT_lo", [P, DC, SEQ], F32R)
        h = sb("h", [P, TB, D])
        act = sb("act", [P, 2, SEQ])
        w_hi_at = nc.sbuf_base
        w_hi = sb("w_hi", [P, 2, SEQ], F32R)
        w_lo = sb("w_lo", [P, 2, SEQ], F32R)
        tabT = sb("tabT", [P, 3, SEQ])
        keep = sb("keep", [P, C_KEEP])
        ident, iota = keep[:, 0:P], keep[:, P:2 * P]
        top_s = sb("top_s", [P, TB, 2 * HEADS, TOPK])
        top_i = sb("top_i", [P, TB, 2 * HEADS, TOPK], U32)
        small = sb("small", [P, 64])
        sc = nc.alloc_sbuf_tensor_at("scores", [P, TB, 2 * HEADS * NKEYS], F32, offset=v_hi_at)
        tmp = nc.alloc_sbuf_tensor_at("tmp", [P, 8, P], F32, offset=w_hi_at)
        tmpu = nc.alloc_sbuf_tensor_at("tmpu", [P, 8, P], U32, offset=w_hi_at)
        qrow = tmp[:, 0:4, :].rearrange("p (e t) k -> p e (t k)", e=2)
        onehots = nc.alloc_sbuf_tensor_at("onehots", [P, 4, 2, GROUP, NKEYS], F32, offset=v_hi_at)
        keysT = v_raw[:, :, :].rearrange("p a (e k) -> p (a e) k", k=NKEYS)

        qkT = carve(16, SEQ)
        vals = carve(TB, 2 * HEADS * HD)
        o = carve(TB, 2 * HEADS * HD)
        bias = carve(HEADS, W3)
        cst = carve(C_COLS)
        logits = [carve(2, W3) for _ in range(2)]
        diffw = [carve(W3) for _ in range(2)]
        probsT = [carve(2, W3) for _ in range(2)]
        z_abs = [carve(W3) for _ in range(2)]
        rem = [carve(W3) for _ in range(2)]
        z_cum = [carve(W3) for _ in range(2)]
        w_stick = [carve(W3) for _ in range(2)]
        sq = carve(TB, HEADS * HD)
        lg, lb = carve(D), carve(D)
        wf = carve(DC, HEADS)
        bfr = carve(HEADS)
        subr = carve(HD)
        lv = carve(2, 2, 32)
        lvp = carve(2, 32)
        t5s = carve(HEADS)
        rowc = carve(3, REL)
        rowb = carve(2, REL)
        ssum = [carve(4) for _ in range(2)]
        nmax = [carve(4) for _ in range(2)]
        rsum = [carve(4) for _ in range(2)]
        fneg = [carve(2) for _ in range(2)]
        lam = carve(4)
        rms = carve(2 * HEADS)
        fgx = carve(2, HEADS)
        fga = carve(2, HEADS)
        logf = carve(2, HEADS)
        fcum = carve(2, HEADS)
        tri_ge, tri_le, ntri_le = (cst[:, a:a + P] for a in (C_GE, C_LE, C_NLE))
        ones, nones = cst[:, C_ONE:C_ONE + P], cst[:, C_NONE:C_NONE + P]
        stick_neg, past_mask, causal = (cst[:, a:a + W3] for a in (C_STICK, C_PAST, C_CAUSAL))

        acc = [ctx.enter_context(nc.psum_tensor(f"acc{i}", [P, 512], F32)) for i in range(4)]
        pu = [ctx.enter_context(nc.psum_tensor(f"pu{i}", [P, 512], F32)) for i in range(2)]
        px = [ctx.enter_context(nc.psum_tensor(f"px{i}", [P, 512], F32)) for i in range(2)]

        s_load = sem("s_load")
        s_bias = sem("s_bias")
        s_cload = sem("s_cload")
        s_lnload = sem("s_lnload")
        s_keys = sem("s_keys")
        s_rows = sem("s_rows")
        u_in = [sem(f"u_in{i}") for i in range(RAW)]
        v_in = [sem(f"v_in{i}") for i in range(2)]
        u_hi_ok = [sem(f"u_hi_ok{f}") for f in range(2)]
        u_lo_ok = [sem(f"u_lo_ok{f}") for f in range(2)]
        u_used = [sem(f"u_used{f}") for f in range(2)]
        evac = sem("evac")
        mixed = sem("mixed")
        v_hi_ok = sem("v_hi_ok")
        v_lo_ok = sem("v_lo_ok")
        v_used = sem("v_used")
        w_hi_ok = sem("w_hi_ok")
        w_ok = sem("w_ok")
        gated = sem("gated")
        rows_ok = sem("rows_ok")
        tr_out = sem("tr_out")
        xT_hi_ok = sem("xT_hi_ok")
        xT_ok = sem("xT_ok")
        s_out = sem("s_out")
        s_read = sem("s_read")
        nmax_ok = sem("nmax_ok")
        exp_ok = sem("exp_ok")
        w_diff_ok = sem("w_diff_ok")
        wT_out = sem("wT_out")
        wT_ok = sem("wT_ok")
        pv_out = sem("pv_out")
        pv_read = sem("pv_read")
        z_out = sem("z_out")
        sp_log_ok = sem("sp_log_ok")
        rem_ok = sem("rem_ok")
        cum_out = sem("cum_out")
        z_cum_ok = sem("z_cum_ok")
        w_stick_ok = sem("w_stick_ok")
        var_ok = sem("var_ok")
        sd_ok = sem("sd_ok")
        t5_out = sem("t5_out")
        rowb_ok = sem("rowb_ok")
        lam_sum = sem("lam_sum")
        lam_exp = sem("lam_exp")
        rms_sum = sem("rms_sum")
        rms_sd = sem("rms_sd")
        f_out = sem("f_out")
        f_abs = sem("f_abs")
        f_log = sem("f_log")
        logf_ok = sem("logf_ok")
        fcum_out = sem("fcum_out")
        fcum_ok = sem("fcum_ok")
        q_out = sem("q_out")
        sc_ok = sem("sc_ok")
        gsub = sem("gsub")
        gexp = sem("gexp")
        tab_ok = sem("tab_ok")
        tabT_out = sem("tabT_out")
        tabT_ok = sem("tabT_ok")
        eq_ok = sem("eq_ok")
        oh_ok = sem("oh_ok")
        g_out = sem("g_out")
        g_mul = sem("g_mul")
        g_copied = sem("g_copied")
        act_step = sem("act_step")
        dve_step = sem("dve_step")
        stored = sem("stored")

        GROUPS = SEQ // GROUP
        layers = range(LAYERS)
        E_ = EXPERT_ITEMS

        def item(L, n):
            return L * ITEMS + n

        def evacs(L, n):
            return L * EVACS + n + 1 - (OUT_ITEMS if n >= N_Q else 0)

        block = ctx.enter_context(nc.Block())

        @block.sync
        def _(sp):
            def load_item(k, i=0):
                if k >= RAW:
                    sp.wait_ge(u_lo_ok[1], k - RAW + 1 + i * RAW)
                src = u_stream[k] if isinstance(i, int) else u_stream[ds(i * RAW + k, 1)].rearrange("o p f -> (o p) f")
                sp.dma_start(u_raw[:, k % RAW].rearrange("p c k -> p (c k)"), src).then_inc(u_in[k % RAW], 16)

            def load_v(j, i=0, step=2):
                if j >= 2:
                    sp.wait_ge(v_lo_ok, (j - 2) * 2 + 2 + i * (2 * step))
                src = v_stream[j] if isinstance(i, int) else v_stream[ds(i * step + j, 1)].rearrange("o p f -> (o p) f")
                sp.dma_start(v_raw[:, j % 2], src).then_inc(v_in[j % 2], 16)

            def load_consts(L):
                sp.dma_start(cst, consts[:, C_KEEP:]).then_inc(s_cload, 16)
                sp.dma_start(wf.rearrange("p c k -> p (c k)"), w_f).then_inc(s_cload, 16)
                sp.dma_start(bfr, b_f.partition_broadcast(P)).then_inc(s_cload, 16)
                sp.dma_start(subr, subln.partition_broadcast(P)).then_inc(s_cload, 16)

            def load_bias(L):
                at = L * HEADS * P * REL + P - 1
                sp.dma_start(bias[:, :, 0:2 * P], bass.AP(scratch.tensor, at, [[REL - 1, P], [P * REL, HEADS], [1, 2 * P]])
                             ).then_inc(s_bias, 16)
                sp.dma_start(bias[:, :, 2 * P:W3], bass.AP(scratch.tensor, at + P, [[REL - 1, P], [P * REL, HEADS], [1, P]])
                             ).then_inc(s_bias, 16)

            def load_norm(q):
                sp.dma_start(lg, ln_g[q].partition_broadcast(P)).then_inc(s_lnload, 16)
                sp.dma_start(lb, ln_b[q].partition_broadcast(P)).then_inc(s_lnload, 16)

            sp.dma_start(h[:, :, :], x.rearrange("(t p) d -> p t d", p=P)).then_inc(s_load, 16)
            sp.dma_start(keep[:, :], consts[:, 0:C_KEEP]).then_inc(s_load, 16)
            for k in range(RAW):
                load_item(k)
            sp.dma_start(t5s[0:32, :], t5).then_inc(s_load, 16)
            sp.dma_start(rowc[0:32, 0, :], onehot).then_inc(s_load, 16)
            sp.dma_start(rowc[0:HEADS, 1:3, :], relmask).then_inc(s_load, 16)
            sp.dma_start(lv.rearrange("p a b c -> p (a b c)"), lam_vecs.partition_broadcast(P)).then_inc(s_load, 16)
            for L in layers:
                if L > 0:
                    sp.wait_ge(w_ok, E_ * L)
                load_consts(L)
                if L == 0:
                    sp.wait_ge(rowb_ok, 1)
                    for m in layers:
                        sp.dma_start(scratch[m], rowb[0:HEADS, m, :].unsqueeze(1).to_broadcast([HEADS, P, REL])
                                     ).then_inc(s_rows, 16)
                    sp.wait_ge(s_rows, 16 * LAYERS)
                load_bias(L)
                if L > 0:
                    load_norm(2 * L - 1)
                for n in range(RAW, N_OUT):
                    load_item(item(L, n))
                if L > 0:
                    sp.wait_ge(rows_ok, 2 * (3 * L - 1) + 2)
                load_norm(2 * L)
                for n in range(N_OUT, N_OUT + 4):
                    load_item(item(L, n))
                if L > 0:
                    sp.wait_ge(v_lo_ok, 2 * E_ * L)
                sp.dma_start(keysT, keys[L]).then_inc(s_keys, 16)
                first = item(L, N_OUT + 4)
                with sp.Fori(0, (OUT_ITEMS - 4 + Q_ITEMS + AHEAD + 4) // RAW) as i:
                    for r in range(RAW):
                        load_item(first + r, i)
                sp.wait_ge(g_out, GROUPS * (L + 1))
                load_v(E_ * L)
                load_v(E_ * L + 1)
                first = item(L, N_U + AHEAD + 4)
                if L + 1 < LAYERS:
                    pairs = E_ - AHEAD
                else:
                    pairs = E_ - AHEAD - 4
                with sp.Fori(0, pairs // RAW) as i:
                    for r in range(RAW):
                        load_item(first + r, i)
                        load_v(E_ * L + 2 + r, i, RAW)
                with sp.Fori(0, (E_ - 2 - pairs) // 2) as i:
                    for r in range(2):
                        load_v(E_ * L + 2 + pairs + r, i)
            sp.wait_ge(w_ok, E_ * LAYERS)
            load_norm(2 * LAYERS - 1)
            for tb in range(TB):
                sp.wait_ge(rows_ok, 2 * (3 * LAYERS - 1) + tb + 1)
                sp.dma_start(out[tb * P:(tb + 1) * P, :], h[:, tb, :]).then_inc(stored, 16)
            sp.wait_ge(stored, 16 * TB)

        @block.gpsimd
        def _(pool):
            def low(k, f, i=0):
                pool.wait_ge(u_hi_ok[f], k + 1 + i * RAW)
                half = slice(f * DC // 2, (f + 1) * DC // 2)
                pool.tensor_tensor(u_lo[:, k % 2, half], u_raw[:, k % RAW, half],
                                   u_hi[:, k % 2, half].bitcast(F32), ALU.subtract).then_inc(u_lo_ok[f], 1)

            def lows(k, n):
                with pool.Fori(0, n // RAW) as i:
                    for r in range(RAW):
                        for f in range(2):
                            low(k + r, f, i)
                for r in range(n // RAW * RAW, n):
                    for f in range(2):
                        low(k + r, f)

            def low_pairs(k, n):
                with pool.Fori(0, n // RAW) as i:
                    for r in range(0, RAW, 2):
                        for f in range(2):
                            low(k + r, f, i)
                            low(k + r + 1, f, i)

            def weigh_onehots(L, q, i=0):
                pool.wait_ge(eq_ok, GROUPS * L + q + 1 + i * 4)
                tok = ds(i * (4 * GROUP) + q * GROUP, GROUP)
                pool.tensor_tensor(onehots[:, q, 1], onehots[:, q, 1],
                                   tabT[:, 2, tok].unsqueeze(2).to_broadcast([P, GROUP, NKEYS]), ALU.mult
                                   ).then_inc(oh_ok, 1)

            for L in layers:
                lows(item(L, 0), V_FIRST)
                low_pairs(item(L, V_FIRST), V_ITEMS)
                lows(item(L, V_FIRST + V_ITEMS), N_OUT - V_FIRST - V_ITEMS)
                low_pairs(item(L, N_OUT), OUT_ITEMS)
                lows(item(L, N_Q), Q_ITEMS + AHEAD + 2)
                with pool.Fori(0, GROUPS // 4) as i:
                    for q in range(4):
                        weigh_onehots(L, q, i)
                for r in (2, 3):
                    for f in range(2):
                        low(item(L, N_U + AHEAD + r), f)
                lows(item(L, N_U + AHEAD + 4), EXPERT_ITEMS - AHEAD - 4)

        @block.scalar
        def _(a):
            steps = [0]

            def step(ins):
                ins.then_inc(act_step, 1)
                steps[0] += 1
                a.wait_ge(act_step, steps[0])

            def round_item(k, i=0, period=RAW):
                a.wait_ge(u_in[k % RAW], 16 * (k // RAW + 1) + i * (16 * period // RAW))
                for f in range(2):
                    round_half(k, f, i, period)

            def round_half(k, f, i=0, period=RAW):
                if k >= 2:
                    a.wait_ge(u_used[f], k - 1 + i * period)
                half = slice(f * DC // 2, (f + 1) * DC // 2)
                a.activation(u_hi[:, k % 2, half], u_raw[:, k % RAW, half], ACT.Copy).then_inc(u_hi_ok[f], 1)

            def round_pair(k):
                for n in (k, k + 1):
                    a.wait_ge(u_in[n % RAW], 16 * (n // RAW + 1))
                for f in range(2):
                    round_half(k, f)
                    round_half(k + 1, f)

            def round_v(j, i=0, period=2):
                a.wait_ge(v_in[j % 2], 16 * (j // 2 + 1) + i * (16 * period // 2))
                for f in range(2):
                    if j >= 2:
                        a.wait_ge(v_used, 2 * (j - 2) + f + 1 + i * (2 * period))
                    half = slice(f * 512, (f + 1) * 512)
                    a.activation(v_hi[:, j % 2, half], v_raw[:, j % 2, half], ACT.Copy).then_inc(v_hi_ok, 1)

            def next_item(k):
                if k + 2 < LAYERS * ITEMS:
                    round_item(k + 2)

            def split_rows(s):
                for g in range(4):
                    tb, half = g // 2, g % 2
                    a.wait_ge(tr_out, 4 * s + g + 1)
                    a.activation(xT_hi[:, 4 * half:4 * half + 4, tb * P:(tb + 1) * P],
                                 px[g % 2][:, :].rearrange("p (c t) -> p c t", c=4), ACT.Copy).then_inc(xT_hi_ok, 1)

            def norm_sd(q):
                for tb in range(TB):
                    a.wait_ge(var_ok, TB * q + tb + 1)
                    a.activation(small[:, 16 + tb:17 + tb], small[:, 14 + tb:15 + tb], ACT.Sqrt).then_inc(sd_ok, 1)

            def take_in(L, n):
                a.wait_ge(u_used[1], item(L, n) + 1)
                tile = n if n < V_FIRST else n - V_ITEMS
                query = n < 4 or 16 <= n < 20
                scale = HD ** -0.5 if query and not (L == 0 and n < 4) else 1.0
                a.activation(qkT[:, tile, :], pu[n % 2][:, 0:SEQ], ACT.Copy, scale=scale).then_inc(evac, 1)

            def take_values(L, n):
                a.wait_ge(u_used[1], item(L, n) + 2)
                m = n - V_FIRST
                for tb in range(TB):
                    ins = a.activation(vals[:, tb, m * P:(m + 2) * P], acc[m % 4 + tb][:, 0:2 * P], ACT.Copy)
                ins.then_inc(evac, 2)

            def exps(su):
                b = su % 2
                a.wait_ge(nmax_ok, su + 1)
                for m in range(2):
                    a.activation(logits[b][:, m, 0:2 * P], logits[b][:, m, 0:2 * P], ACT.Exp,
                                 bias=nmax[b][:, m:m + 1], accum_out=ssum[b][:, 2 * m + 1:2 * m + 2])
                    ins = a.activation(logits[b][:, m, 2 * P:W3], logits[b][:, m, 2 * P:W3], ACT.Exp,
                                       bias=nmax[b][:, 2 + m:3 + m], accum_out=ssum[b][:, 2 * m:2 * m + 1])
                ins.then_inc(exp_ok, 1)

            def take_T(su):
                b = su % 2
                if su < SOFT_A:
                    a.wait_ge(wT_out, su + 1)
                    a.activation(probsT[b][:, 0, :], px[b][:, 0:W3], ACT.Copy).then_inc(wT_ok, 1)
                else:
                    for m in range(2):
                        n = SOFT_A + 2 * (su - SOFT_A) + m + 1
                        a.wait_ge(wT_out, n)
                        a.activation(probsT[b][:, m, :], px[m][:, 0:W3], ACT.Copy).then_inc(wT_ok, 1)

            a.preload_act_table_set("natural_log_exp_and_others")
            a.wait_ge(lam_sum, 1)
            a.activation(lam[:, 2:4], lam[:, 0:2], ACT.Exp).then_inc(lam_exp, 1)
            for L in layers:
                if L == 0:
                    round_item(0)
                    round_item(1)
                split_rows(3 * L)
                n0 = V_FIRST + V_ITEMS
                for n in range(V_FIRST):
                    next_item(item(L, n))
                    take_in(L, n)
                for n in range(V_FIRST, n0, 2):
                    round_pair(item(L, n + 2))
                    take_values(L, n)
                if L == 1:
                    a.preload_act_table_set("natural_log_exp_and_others")
                    a.wait_ge(f_abs, 1)
                    step(a.activation(fga, fga, ACT.Exp))
                    a.activation(fga, fga, ACT.Ln, bias=1.0).then_inc(f_log, 1)
                units = [range(0, SOFT_A), range(SOFT_A, SOFT_A + SOFT_C)][L]
                per = 8 // len(units)
                for i in range(len(units) + 1):
                    if i < len(units):
                        exps(units[i])
                        for n in range(n0 + per * i, n0 + per * i + per):
                            next_item(item(L, n))
                            take_in(L, n)
                    if i > 0:
                        take_T(units[i - 1])
                if L == 0:
                    a.wait_ge(rms_sum, 1)
                    a.activation(rms, rms, ACT.Sqrt).then_inc(rms_sd, 1)
                    a.preload_act_table_set("natural_log_exp_and_others")
                    for b in range(HEADS + 1):
                        if b < HEADS:
                            a.wait_ge(z_out, b + 1)
                            if b >= 2:
                                a.wait_ge(rem_ok, b - 1)
                            step(a.activation(z_abs[b % 2], acc[b % 2][:, 0:W3], ACT.Abs))
                            step(a.activation(z_abs[b % 2], z_abs[b % 2], ACT.Exp, scale=-1.0))
                            a.activation(z_abs[b % 2], z_abs[b % 2], ACT.Ln, bias=1.0).then_inc(sp_log_ok, 1)
                        if b > 0:
                            a.wait_ge(z_cum_ok, b)
                            if b >= 3:
                                a.wait_ge(pv_out, SOFT_A + b - 2)
                            a.activation(w_stick[(b - 1) % 2], z_cum[(b - 1) % 2], ACT.Exp).then_inc(w_stick_ok, 1)
                else:
                    units = range(SOFT_A + SOFT_C, SOFT_A + SOFT_C + SOFT_D)
                    for i in range(len(units) + 1):
                        if i < len(units):
                            exps(units[i])
                        if i > 0:
                            take_T(units[i - 1])
                split_rows(3 * L + 1)
                for n in range(N_OUT, N_Q, 2):
                    round_pair(item(L, n + 2))
                norm_sd(2 * L)
                split_rows(3 * L + 2)
                for e in range(Q_ITEMS + 1):
                    if e < Q_ITEMS:
                        k = item(L, N_Q + e)
                        next_item(k)
                        a.wait_ge(u_used[1], k + 1)
                        if e >= 2:
                            a.wait_ge(q_out, Q_ITEMS * L + e - 1)
                        a.activation(qrow[:, e % 2, :], pu[e % 2][:, 0:SEQ], ACT.Copy).then_inc(evac, 1)
                    if e > 0 and e % 4 == 0:
                        a.wait_ge(q_out, Q_ITEMS * L + e)
                        for tb in range(TB):
                            a.activation(sc[:, tb, (e - 4) * P:e * P], px[tb][:, :], ACT.Copy).then_inc(sc_ok, 1)
                a.preload_act_table(ACT.Gelu)
                with a.Fori(0, AHEAD // RAW) as i:
                    for r in range(RAW):
                        k = item(L, N_U + r)
                        round_item(k + 2, i)
                        a.wait_ge(u_used[1], k + 1 + i * RAW)
                        a.activation(gates[:, :, ds(i * RAW + r, 1)].rearrange("p t o -> p (t o)"),
                                     pu[r % 2][:, 0:SEQ], ACT.Gelu).then_inc(evac, 1)
                for tb in range(TB):
                    a.wait_ge(gsub, TB * L + tb + 1)
                    a.activation(top_s[:, tb, 0:8, :], top_s[:, tb, 0:8, :], ACT.Exp).then_inc(gexp, 1)
                for tb in range(TB):
                    a.wait_ge(tabT_out, TB * L + tb + 1)
                    a.activation(tabT[:, :, tb * P:(tb + 1) * P],
                                 px[tb][:, 0:3 * P].rearrange("p (a t) -> p a t", a=3), ACT.Copy).then_inc(tabT_ok, 1)
                with a.Fori(0, GROUPS // 4) as i:
                    for q in range(4):
                        a.wait_ge(g_mul, GROUPS * L + q + 1 + i * 4)
                        a.activation(gates[:, ds(i * (4 * GROUP) + q * GROUP, GROUP), AHEAD:NKEYS],
                                     acc[q][:, :].rearrange("p (t j) -> p t j", t=GROUP)[:, :, AHEAD:NKEYS],
                                     ACT.Copy).then_inc(g_copied, 1)
                a.preload_act_table(ACT.Gelu)
                round_v(E_ * L)
                round_v(E_ * L + 1)

                def both(i, r, last=False):
                    k = item(L, N_U + AHEAD + r)
                    round_v(E_ * L + 2 + r, i, RAW)
                    if not last:
                        round_item(k + 2, i)
                    a.wait_ge(u_used[1], k + 1 + i * RAW)
                    j = E_ * L + AHEAD + r
                    if L > 0 or r >= 2:
                        a.wait_ge(gated, (E_ - AHEAD) * L + r - 1 + i * RAW)
                    elif not isinstance(i, int):
                        raise AssertionError
                    a.activation(act[:, r % 2, :], pu[r % 2][:, 0:SEQ], ACT.Gelu).then_inc(evac, 1)

                n = E_ - AHEAD
                for r in range(RAW):
                    both(0, r)
                with a.Fori(0, n // RAW - 2) as i:
                    for r in range(RAW):
                        both(i, RAW + r)
                for r in range(RAW):
                    both(0, n - RAW + r, last=(L == LAYERS - 1 and r >= 2))
                with a.Fori(0, (AHEAD - 2) // 2) as i:
                    for r in range(2):
                        round_v(E_ * L + 2 + n + r, i)
                norm_sd(2 * L + 1)

        @block.vector
        def _(v):
            steps = [0]

            def mark(ins):
                ins.then_inc(dve_step, 1)
                steps[0] += 1
                return steps[0]

            def after(n):
                v.wait_ge(dve_step, n)

            def step(ins):
                after(mark(ins))

            def split_rows(s):
                for g in range(4):
                    tb, half = g // 2, g % 2
                    v.wait_ge(xT_hi_ok, 4 * s + g + 1)
                    part = (slice(None), slice(4 * half, 4 * half + 4), slice(tb * P, (tb + 1) * P))
                    v.tensor_tensor(xT_lo[part], px[g % 2][:, :].rearrange("p (c t) -> p c t", c=4),
                                    xT_hi[part].bitcast(F32), ALU.subtract).then_inc(xT_ok, 1)

            def norm(q):
                v.wait_ge(s_lnload, 32 * (q + 1))
                for tb in range(TB):
                    for f in range(2):
                        last = mark(v.bn_stats(small[:, 6 * f:6 * f + 6], h[:, tb, 512 * f:512 * f + 512]))
                    after(last)
                    step(v.bn_aggr(small[:, 12:14], small[:, 0:12].rearrange("p (a b) -> p a b", a=2)))
                    v.tensor_scalar(small[:, 14 + tb:15 + tb], small[:, 13:14], LN_EPS, None, ALU.add).then_inc(var_ok, 1)
                    v.wait_ge(sd_ok, TB * q + tb + 1)
                    step(v.reciprocal(small[:, 18 + tb:19 + tb], small[:, 16 + tb:17 + tb]))
                    step(v.tensor_scalar(h[:, tb, :], h[:, tb, :], small[:, 12:13], small[:, 18 + tb:19 + tb],
                                         ALU.subtract, ALU.mult))
                    step(v.tensor_tensor(h[:, tb, :], h[:, tb, :], lg, ALU.mult))
                    v.tensor_tensor(h[:, tb, :], h[:, tb, :], lb, ALU.add).then_inc(rows_ok, 1)
                v.wait_ge(rows_ok, ROWS[q])

            ROWS = [2 * (3 * (q // 2) + q % 2 + 1) + 2 for q in range(2 * LAYERS)]

            def maps(su):
                b = su % 2
                v.wait_ge(s_out, su + 1)
                if su >= 2:
                    v.wait_ge(wT_out, su - 1 if su - 2 < SOFT_A else SOFT_A + 2 * (su - 1 - SOFT_A))
                for m in range(2):
                    S = acc[m][:, 0:W3]
                    if su < SOFT_A:
                        ins = v.scalar_tensor_tensor(logits[b][:, m, :], S, 32.0 ** -0.5, bias[:, su, :],
                                                     ALU.mult, ALU.add)
                    elif su < SOFT_A + SOFT_C:
                        ins = v.tensor_tensor(logits[b][:, m, :], S, bias[:, 2 * (su - SOFT_A) + m, :], ALU.add)
                    else:
                        hh = 2 * (su - SOFT_A - SOFT_C) + m
                        v.scalar_tensor_tensor(logits[b][:, m, 0:2 * P], acc[m][:, 0:2 * P], fcum[:, 1, hh:hh + 1],
                                               causal[:, 0:2 * P], ALU.add, ALU.add)
                        ins = v.scalar_tensor_tensor(logits[b][:, m, 2 * P:W3], acc[m][:, 2 * P:W3],
                                                     fcum[:, 0, hh:hh + 1], causal[:, 2 * P:W3], ALU.add, ALU.add)
                ins.then_inc(s_read, 1)
                v.wait_ge(s_read, su + 1)
                v.tensor_reduce(nmax[b][:, 0:2], logits[b][:, :, 0:2 * P], AX.X, ALU.max, negate=True)
                v.tensor_reduce(nmax[b][:, 2:4], logits[b][:, :, 2 * P:W3], AX.X, ALU.max, negate=True
                                ).then_inc(nmax_ok, 1)

            def weights(su):
                b = su % 2
                v.wait_ge(exp_ok, su + 1)
                if su >= 2:
                    v.wait_ge(pv_read, PV[su - 2])
                step(v.reciprocal(rsum[b], ssum[b]))
                if su < SOFT_A:
                    step(v.scalar_tensor_tensor(fneg[b], ssum[b][:, 0:2], lam[:, 0:1], rsum[b][:, 2:4],
                                                ALU.mult, ALU.mult))
                    v.scalar_tensor_tensor(diffw[b][:, 0:2 * P], logits[b][:, 1, 0:2 * P], fneg[b][:, 1:2],
                                           logits[b][:, 0, 0:2 * P], ALU.mult, ALU.add)
                    v.scalar_tensor_tensor(diffw[b][:, 2 * P:W3], logits[b][:, 1, 2 * P:W3], fneg[b][:, 0:1],
                                           logits[b][:, 0, 2 * P:W3], ALU.mult, ALU.add).then_inc(w_diff_ok, 1)

            def outputs(su):
                b = su % 2
                v.wait_ge(pv_out, PV[su])
                if su < SOFT_A:
                    res = acc[2 + b][:, 0:2 * HD].rearrange("p (t d) -> p t d", t=2)
                    v.tensor_tensor(o[:, :, su * HD:(su + 1) * HD], res,
                                    rsum[b][:, 0:2].unsqueeze(2).to_broadcast([P, 2, HD]), ALU.mult).then_inc(pv_read, 1)
                else:
                    c = (su - SOFT_A) * 2 * HD
                    for m in range(2):
                        res = acc[2 + b][:, m * 2 * HD:(m + 1) * 2 * HD].rearrange("p (t d) -> p t d", t=2)
                        ins = v.tensor_tensor(o[:, :, c + m * HD:c + (m + 1) * HD], res,
                                              rsum[b][:, 2 * m:2 * m + 2].unsqueeze(2).to_broadcast([P, 2, HD]), ALU.mult)
                    ins.then_inc(pv_read, 1)

            PV = [su + 1 if su < SOFT_A else su + 1 + HEADS for su in range(SOFT_A + SOFT_C + SOFT_D)]

            def topk_first(L):
                for grp in range(4):
                    for tb in range(TB):
                        v.wait_ge(sc_ok, 2 * 4 * L + 2 * grp + tb + 1)
                        es = range(4 * grp, 4 * grp + 4)
                        row = {e: sc[:, tb, e * P:(e + 1) * P] for e in es}
                        best = lambda e, f: top_s[:, tb, e, 8 * f:8 * f + 8]
                        n = {e: mark(v.max(best(e, 0), row[e])) for e in es}
                        for f in range(2):
                            for e in es:
                                after(n[e])
                                n[e] = mark(v.max_index(top_i[:, tb, e, 8 * f:8 * f + 8], best(e, f), row[e]))
                            if f == 0:
                                for e in es:
                                    after(n[e])
                                    n[e] = mark(v.match_replace(row[e], best(e, 0), row[e], LOWEST))
                                for e in es:
                                    after(n[e])
                                    n[e] = mark(v.max(best(e, 1), row[e]))
                after(steps[0])

            def topk_second(L, tb):
                cand = sc[:, tb, :].rearrange("p (h a b) -> p h a b", h=HEADS, a=TOPK)
                ts = top_s[:, tb].rearrange("p (h c) k -> p h c k", c=2)
                step(v.tensor_tensor(cand, ts[:, :, 0, :].unsqueeze(3).to_broadcast([P, HEADS, TOPK, TOPK]),
                                     ts[:, :, 1, :].unsqueeze(2).to_broadcast([P, HEADS, TOPK, TOPK]), ALU.add))
                bests = top_s[:, tb, 0:8, :]
                pos = tmpu[:, 0, :].rearrange("p (h k) -> p h k", h=HEADS)
                for g in range(2):
                    hs = range(4 * g, 4 * g + 4)
                    row = {q: sc[:, tb, q * 2 * P:(q + 1) * 2 * P] for q in hs}
                    best = lambda q, f: bests[:, q, 8 * f:8 * f + 8]
                    n = {q: mark(v.max(best(q, 0), row[q])) for q in hs}
                    for f in range(2):
                        for q in hs:
                            after(n[q])
                            n[q] = mark(v.max_index(pos[:, q, 8 * f:8 * f + 8], best(q, f), row[q]))
                        if f == 0:
                            for q in hs:
                                after(n[q])
                                n[q] = mark(v.match_replace(row[q], best(q, 0), row[q], LOWEST))
                            for q in hs:
                                after(n[q])
                                n[q] = mark(v.max(best(q, 1), row[q]))
                after(steps[0])
                v.tensor_single_scalar(tmpu[:, 1, :], tmpu[:, 0, :], 4, ALU.logical_shift_right)
                step(v.tensor_single_scalar(tmpu[:, 2, :], tmpu[:, 0, :], TOPK - 1, ALU.bitwise_and))
                v.tensor_copy(tmp[:, 3, :], tmpu[:, 1, :])
                step(v.tensor_copy(tmp[:, 4, :], tmpu[:, 2, :]))
                work = sc[:, tb, :].rearrange("p (s a) -> p s a", a=TOPK)
                work4 = sc[:, tb, :].rearrange("p (h k a) -> p h k a", h=HEADS, k=TOPK)
                ti = top_i[:, tb].rearrange("p (h c) k -> p h c k", c=2)
                for side in range(2):
                    step(v.tensor_tensor(work, tmp[:, 3 + side, :].unsqueeze(2).to_broadcast([P, P, TOPK]),
                                         iota[:, 0:TOPK].unsqueeze(1).to_broadcast([P, P, TOPK]), ALU.is_equal))
                    step(v.tensor_tensor(work4, work4,
                                         ti[:, :, side, :].unsqueeze(2).to_broadcast([P, HEADS, TOPK, TOPK]), ALU.mult))
                    step(v.tensor_reduce(tmp[:, 5 + side, :], work, AX.X, ALU.add))
                sub = sc[:, tb, 0:P].rearrange("p (h k) -> p h k", h=HEADS)
                step(v.tensor_tensor(sub, bests, bests[:, :, 0:1].to_broadcast([P, HEADS, TOPK]), ALU.subtract))
                v.tensor_copy(bests, sub).then_inc(gsub, 1)
                dst = sc[:, tb, P:3 * P].rearrange("p (a s) -> p a s", a=2)
                step(v.tensor_copy(dst, tmp[:, 5:7, :]))

            def gate_weights(L, tb):
                bests = top_s[:, tb, 0:8, :]
                v.wait_ge(gexp, TB * L + tb + 1)
                step(v.tensor_reduce(small[:, 20:28], bests, AX.X, ALU.add))
                step(v.reciprocal(small[:, 28:36], small[:, 20:28]))
                v.tensor_tensor(sc[:, tb, 3 * P:4 * P].rearrange("p (h k) -> p h k", h=HEADS), bests,
                                small[:, 28:36].unsqueeze(2).to_broadcast([P, HEADS, TOPK]), ALU.mult).then_inc(tab_ok, 1)

            def onehot_group(L, q, i=0):
                if q >= 4 or not isinstance(i, int):
                    v.wait_ge(g_out, GROUPS * L + q - 3 + i * 4)
                tok = ds(i * (4 * GROUP) + q * GROUP, GROUP)
                shape = [P, GROUP, NKEYS]
                for side in (0, 1):
                    ins = v.tensor_tensor(onehots[:, q % 4, side], iota.unsqueeze(1).to_broadcast(shape),
                                          tabT[:, side, tok].unsqueeze(2).to_broadcast(shape), ALU.is_equal)
                ins.then_inc(eq_ok, 1)

            def gate_group(L, q, i=0):
                v.wait_ge(g_out, GROUPS * L + q + 1 + i * 4)
                g = gates[:, ds(i * (4 * GROUP) + q * GROUP, GROUP), 0:AHEAD]
                v.tensor_tensor(g, g, acc[q % 4][:, :].rearrange("p (t j) -> p t j", t=GROUP)[:, :, 0:AHEAD],
                                ALU.mult).then_inc(g_mul, 1)

            v.wait_ge(s_load, 16 * 6)
            step(v.tensor_tensor(lvp, lv[:, :, 0, :], lv[:, :, 1, :], ALU.mult))
            v.tensor_reduce(lam[:, 0:2], lvp, AX.X, ALU.add).then_inc(lam_sum, 1)
            v.wait_ge(t5_out, 1)
            for L in layers:
                ins = v.tensor_tensor(rowb[0:HEADS, L], px[0][0:HEADS, 0:REL], rowc[0:HEADS, 1 + L], ALU.add)
            ins.then_inc(rowb_ok, 1)
            v.wait_ge(lam_exp, 1)
            step(v.scalar_tensor_tensor(lam[:, 0:1], lam[:, 3:4], LAMBDA_INIT, lam[:, 2:3], ALU.subtract, ALU.subtract))

            for L in layers:
                split_rows(3 * L)
                v.wait_ge(s_cload, 64 * (L + 1))
                v.wait_ge(s_bias, 32 * (L + 1))
                if L == 1:
                    v.wait_ge(f_out, 1)
                    step(v.tensor_tensor(fgx, px[0][:, 0:2 * HEADS].rearrange("p (t h) -> p t h", t=2),
                                         bfr.unsqueeze(1).to_broadcast([P, 2, HEADS]), ALU.add))
                    v.scalar_tensor_tensor(fga, fgx, -1.0, fgx, ALU.mult, ALU.min).then_inc(f_abs, 1)
                    v.wait_ge(f_log, 1)
                    v.scalar_tensor_tensor(logf, fgx, 0.0, fga, ALU.min, ALU.subtract).then_inc(logf_ok, 1)
                    v.wait_ge(fcum_out, 1)
                    v.tensor_copy(fcum, px[1][:, 0:2 * HEADS].rearrange("p (t h) -> p t h", t=2)).then_inc(fcum_ok, 1)
                    v.wait_ge(fcum_ok, 1)
                units = [range(0, SOFT_A), range(SOFT_A, SOFT_A + SOFT_C)][L]
                for i in range(len(units) + 2):
                    if i < len(units):
                        maps(units[i])
                    if 1 <= i <= len(units):
                        weights(units[i - 1])
                    if i >= 2:
                        outputs(units[i - 2])
                if L == 0:
                    v.wait_ge(pv_read, SOFT_A)
                    oa = o[:, :, 0:HEADS * HD]
                    heads = lambda t: t.rearrange("p t (h d) -> p t h d", d=HD)
                    step(v.tensor_tensor(sq, oa, oa, ALU.mult))
                    rv = rms.rearrange("p (t h) -> p t h", t=2)
                    step(v.tensor_reduce(rv, heads(sq), AX.X, ALU.add))
                    v.tensor_scalar(rms, rms, 1.0 / HD, LN_EPS, ALU.mult, ALU.add).then_inc(rms_sum, 1)
                    step(v.tensor_scalar(subr, subr, 1.0 - LAMBDA_INIT, None, ALU.mult))
                    v.wait_ge(rms_sd, 1)
                    step(v.reciprocal(rms, rms))
                    for t in range(TB):
                        n = mark(v.tensor_tensor(heads(oa)[:, t], heads(oa)[:, t],
                                                 rv[:, t].unsqueeze(2).to_broadcast([P, HEADS, HD]), ALU.mult))
                    after(n)
                    for t in range(TB):
                        n = mark(v.tensor_tensor(heads(oa)[:, t], heads(oa)[:, t],
                                                 subr.unsqueeze(1).to_broadcast([P, HEADS, HD]), ALU.mult))
                    for i in range(1, HEADS + 3):
                        b = i - 1
                        if 0 <= b < HEADS:
                            z = acc[b % 2][:, 0:W3]
                            v.wait_ge(sp_log_ok, b + 1)
                            step(v.scalar_tensor_tensor(z_abs[b % 2], z, 0.0, z_abs[b % 2], ALU.max, ALU.add))
                            v.tensor_tensor(rem[b % 2], z_abs[b % 2], stick_neg, ALU.mult).then_inc(rem_ok, 1)
                            v.wait_ge(cum_out, b + 1)
                            v.tensor_tensor(z_cum[b % 2], z, past_mask, ALU.add).then_inc(z_cum_ok, 1)
                        b = i - 3
                        if 0 <= b < HEADS:
                            v.wait_ge(pv_out, SOFT_A + b + 1)
                            c = HEADS * HD + b * HD
                            v.tensor_copy(o[:, :, c:c + HD], acc[2 + b % 2][:, 0:2 * HD].rearrange("p (t d) -> p t d", t=2)
                                          ).then_inc(pv_read, 1)
                    v.wait_ge(pv_read, 2 * HEADS)
                    after(n)
                else:
                    units = range(SOFT_A + SOFT_C, SOFT_A + SOFT_C + SOFT_D)
                    for i in range(len(units) + 2):
                        if i < len(units):
                            maps(units[i])
                        if 1 <= i <= len(units):
                            weights(units[i - 1])
                        if i >= 2:
                            outputs(units[i - 2])
                    v.wait_ge(pv_read, 2 * HEADS + SOFT_C + SOFT_D)
                v.engine_nop().then_inc(rows_ok, 2)
                split_rows(3 * L + 1)
                for n in range(0, OUT_ITEMS, 2):
                    v.wait_ge(u_used[1], item(L, N_OUT + n) + 2)
                    for tb in range(TB):
                        part = h[:, tb, n * P:(n + 2) * P]
                        ins = v.scalar_tensor_tensor(part, part, ALPHA, acc[n % 4 + tb][:, 0:2 * P], ALU.mult, ALU.add)
                    ins.then_inc(mixed, 2)
                v.wait_ge(mixed, OUT_ITEMS * (L + 1))
                norm(2 * L)
                split_rows(3 * L + 2)

                topk_first(L)
                for tb in range(TB):
                    topk_second(L, tb)
                for tb in range(TB):
                    gate_weights(L, tb)
                v.wait_ge(tabT_ok, TB * (L + 1))
                v.wait_ge(evac, evacs(L, N_U + AHEAD - 1))
                for q in range(GATE_LAG):
                    onehot_group(L, q)
                for q in range(4):
                    onehot_group(L, q + GATE_LAG)
                    gate_group(L, q)
                with v.Fori(1, GROUPS // 4 - 1) as i:
                    for q in range(4):
                        onehot_group(L, q + GATE_LAG, i)
                        gate_group(L, q, i)
                for q in range(GROUPS - 4, GROUPS):
                    if q + GATE_LAG < GROUPS:
                        onehot_group(L, q + GATE_LAG)
                    gate_group(L, q)
                v.wait_ge(g_mul, GROUPS * (L + 1))
                v.wait_ge(g_copied, GROUPS * (L + 1))

                def low_v(r, i=0, period=2):
                    j = E_ * L + r
                    for f in range(2):
                        v.wait_ge(v_hi_ok, 2 * j + f + 1 + i * (2 * period))
                        half = slice(f * 512, (f + 1) * 512)
                        v.tensor_tensor(v_lo[:, j % 2, half], v_raw[:, j % 2, half], v_hi[:, j % 2, half].bitcast(F32),
                                        ALU.subtract).then_inc(v_lo_ok, 1)

                def split_w(r, i=0, period=2):
                    j = E_ * L + r
                    if j >= 2:
                        v.wait_ge(v_used, 2 * (j - 2) + 2 + i * (2 * period))
                    col = gates[:, :, ds(i * period + r, 1)].rearrange("p t o -> p (t o)")
                    v.tensor_copy(w_hi[:, j % 2], col).then_inc(w_hi_ok, 1)
                    v.wait_ge(w_hi_ok, j + 1 + i * period)
                    v.tensor_tensor(w_lo[:, j % 2], col, w_hi[:, j % 2].bitcast(F32), ALU.subtract).then_inc(w_ok, 1)

                def gate_item(r, i=0):
                    v.wait_ge(evac, evacs(L, N_U + AHEAD + r) + i * RAW)
                    col = gates[:, :, ds(i * RAW + AHEAD + r, 1)].rearrange("p t o -> p (t o)")
                    v.tensor_tensor(col, col, act[:, r % 2], ALU.mult).then_inc(gated, 1)

                split_w(0)
                split_w(1)
                low_v(0)
                low_v(1)
                n = E_ - AHEAD
                with v.Fori(0, n // RAW) as i:
                    v.wait_ge(gated, n * L + i * RAW)
                    for r in range(RAW):
                        low_v(2 + r, i, RAW)
                        split_w(2 + r, i, RAW)
                        gate_item(r, i)
                v.wait_ge(gated, n * (L + 1))
                with v.Fori(0, (AHEAD - 2) // 2) as i:
                    for r in range(2):
                        low_v(2 + n + r, i)
                        split_w(2 + n + r, i)
                v.wait_ge(v_used, 2 * E_ * (L + 1))
                for tb in range(TB):
                    for f in range(2):
                        part = h[:, tb, f * 512:f * 512 + 512]
                        m = mark(v.scalar_tensor_tensor(part, part, ALPHA, acc[2 * tb + f][:, :], ALU.mult, ALU.add))
                after(m)
                norm(2 * L + 1)

        @block.tensor
        def _(pe):
            def passes(out_ap, lhs, rhs, start, stop):
                (lh, ll), (rh, rl) = lhs, rhs
                pe.matmul(out_ap, lh, rh, start=start, stop=False)
                pe.matmul(out_ap, lh, rl, start=False, stop=False)
                return pe.matmul(out_ap, ll, rh, start=False, stop=stop)

            def item_columns(k, bank, i=0, period=2):
                for f in range(2):
                    pe.wait_ge(u_lo_ok[f], k + 1 + i * period)
                    for c in range(f * DC // 2, (f + 1) * DC // 2):
                        ins = passes(bank[:, 0:SEQ], (u_hi[:, k % 2, c], u_lo[:, k % 2, c]),
                                     (xT_hi[:, c, :], xT_lo[:, c, :]), c == 0, c == DC - 1)
                    ins.then_inc(u_used[f], 1)

            def pair_tokens(k, banks):
                for f in range(2):
                    pe.wait_ge(u_lo_ok[f], k + 2)
                    for c in range(f * DC // 2, (f + 1) * DC // 2):
                        for tb in range(TB):
                            t = slice(tb * P, (tb + 1) * P)
                            ins = passes(banks[tb][:, 0:2 * P], (xT_hi[:, c, t], xT_lo[:, c, t]),
                                         (u_hi[:, :, c], u_lo[:, :, c]), c == 0, c == DC - 1)
                    ins.then_inc(u_used[f], 2)

            def in_item(L, n):
                if n >= 2:
                    pe.wait_ge(evac, evacs(L, n - 2))
                item_columns(item(L, n), pu[n % 2])

            def transpose_rows(s, src):
                for g in range(4):
                    tb, half = g // 2, g % 2
                    if s == 0:
                        pe.wait_ge(s_load, 16 * 6)
                        if g == 0:
                            pe.wait_ge(rowb_ok, 1)
                    else:
                        pe.wait_ge(rows_ok, 2 * (s - 1) + tb + 1)
                    if 4 * s + g >= 2:
                        pe.wait_ge(xT_ok, 4 * s + g - 1)
                    for c in range(4):
                        at = (4 * half + c) * P
                        ins = pe.transpose(px[g % 2][:, c * P:(c + 1) * P], src[:, tb, at:at + P], ident)
                    ins.then_inc(tr_out, 1)
                pe.wait_ge(xT_ok, 4 * s + 4)

            def head(tiles, hh, m=None):
                base = (hh % 2) * HD + (0 if m is None else 32 * m)
                n = HD if m is None else 32
                return qkT[base:base + n, tiles + hh // 2, :]

            def products(su):
                if su >= 1:
                    pe.wait_ge(s_read, su)
                for m in range(2):
                    if su < SOFT_A:
                        q, k = head(0, su, m), head(4, su, m)
                    elif su < SOFT_A + SOFT_C:
                        hh = 2 * (su - SOFT_A) + m
                        q, k = head(0, hh), head(4, hh)
                    else:
                        hh = 2 * (su - SOFT_A - SOFT_C) + m
                        q, k = head(8, hh), head(12, hh)
                    forget = su >= SOFT_A + SOFT_C
                    S = acc[m]
                    ins = pe.matmul(S[:, 0:2 * P], q[:, P:2 * P], k[:, 0:2 * P], start=True, stop=True)
                    if forget:
                        f0 = logf[:, 0, hh:hh + 1].to_broadcast([P, P])
                        f1 = logf[:, 1, hh:hh + 1].to_broadcast([P, P])
                        pe.matmul(S[:, 0:P], f0, ntri_le, start=False, stop=True, skip_group_check=True)
                        pe.matmul(S[:, P:2 * P], f0, nones, start=False, stop=True, skip_group_check=True)
                        pe.matmul(S[:, P:2 * P], f1, ntri_le, start=False, stop=True, skip_group_check=True)
                    ins = pe.matmul(S[:, 2 * P:W3], q[:, 0:P], k[:, 0:P], start=True, stop=True)
                    if forget:
                        ins = pe.matmul(S[:, 2 * P:W3], f0, ntri_le, start=False, stop=True, skip_group_check=True)
                ins.then_inc(s_out, 1)

            def weights_T(su):
                b = su % 2
                if su < SOFT_A:
                    pe.wait_ge(w_diff_ok, su + 1)
                    if su >= 2:
                        pe.wait_ge(wT_ok, su - 1)
                    for blk in range(3):
                        ins = pe.transpose(px[b][:, blk * P:(blk + 1) * P], diffw[b][:, blk * P:(blk + 1) * P], ident)
                    ins.then_inc(wT_out, 1)
                else:
                    pe.wait_ge(exp_ok, su + 1)
                    for m in range(2):
                        n = SOFT_A + 2 * (su - SOFT_A) + m
                        pe.wait_ge(wT_ok, n - 1)
                        for blk in range(3):
                            ins = pe.transpose(px[m][:, blk * P:(blk + 1) * P], logits[b][:, m, blk * P:(blk + 1) * P], ident)
                        ins.then_inc(wT_out, 1)

            def weigh(out_ap, wT, col):
                v0, v1 = vals[:, 0, col:col + HD], vals[:, 1, col:col + HD]
                pe.matmul(out_ap[:, 0:HD], wT[2], v0, start=True, stop=True)
                pe.matmul(out_ap[:, HD:2 * HD], wT[0], v0, start=True, stop=False)
                return pe.matmul(out_ap[:, HD:2 * HD], wT[1], v1, start=False, stop=True)

            def attend(su):
                b = su % 2
                reads = su if su < SOFT_A else su + HEADS
                if reads >= 2:
                    pe.wait_ge(pv_read, reads - 1)
                if su < SOFT_A:
                    pe.wait_ge(wT_ok, su + 1)
                    T = [probsT[b][:, 0, k * P:(k + 1) * P] for k in range(3)]
                    weigh(acc[2 + b][:, 0:2 * HD], T, su * HD).then_inc(pv_out, 1)
                else:
                    for m in range(2):
                        pe.wait_ge(wT_ok, SOFT_A + 2 * (su - SOFT_A) + m + 1)
                        T = [probsT[b][:, m, k * P:(k + 1) * P] for k in range(3)]
                        ins = weigh(acc[2 + b][:, m * 2 * HD:(m + 1) * 2 * HD], T, (2 * (su - SOFT_A) + m) * HD)
                    ins.then_inc(pv_out, 1)

            def run_units(units, L=None, per=0):
                for i in range(len(units) + 2):
                    if i < len(units):
                        products(units[i])
                        for n in range(16 + per * i, 16 + per * i + per):
                            in_item(L, n)
                    if 1 <= i <= len(units):
                        weights_T(units[i - 1])
                    if i >= 2:
                        attend(units[i - 2])

            pe.wait_ge(s_load, 16 * 6)
            pe.matmul(px[0][0:HEADS, 0:REL], t5s[0:32, :], rowc[0:32, 0, :], start=True, stop=True).then_inc(t5_out, 1)
            for L in layers:
                transpose_rows(3 * L, h)
                if L == 1:
                    pe.wait_ge(s_cload, 64 * (L + 1))
                    for tb in range(TB):
                        for c in range(DC):
                            for n, part in enumerate((xT_hi, xT_lo)):
                                ins = pe.matmul(px[0][:, tb * HEADS:(tb + 1) * HEADS],
                                                part[:, c, tb * P:(tb + 1) * P].bitcast(F32), wf[:, c, :],
                                                start=(c == 0 and n == 0), stop=(c == DC - 1 and n == 1))
                    ins.then_inc(f_out, 1)
                for n in range(V_FIRST):
                    in_item(L, n)
                for m in range(0, V_ITEMS, 2):
                    if m >= 4:
                        pe.wait_ge(evac, evacs(L, V_FIRST + m - 3))
                    pair_tokens(item(L, V_FIRST + m), acc[m % 4:m % 4 + 2])
                pe.wait_ge(evac, evacs(L, 15))
                pe.wait_ge(s_cload, 64 * (L + 1))
                if L == 0:
                    run_units(range(0, SOFT_A), L, 1)
                    pe.wait_ge(evac, evacs(L, 23))
                    for i in range(HEADS + 3):
                        b = i
                        if b < HEADS:
                            if b >= 2:
                                pe.wait_ge(z_cum_ok, b - 1)
                            elif b == 0:
                                pe.wait_ge(s_read, SOFT_A)
                            z = acc[b % 2]
                            q, k = head(8, b), head(12, b)
                            pe.matmul(z[:, 0:2 * P], k[:, 0:P], q[:, 0:2 * P], start=True, stop=False)
                            pe.matmul(z[:, 2 * P:W3], k[:, P:2 * P], q[:, P:2 * P], start=False, stop=True).then_inc(z_out, 1)
                        b = i - 1
                        if 0 <= b < HEADS:
                            pe.wait_ge(rem_ok, b + 1)
                            z, r = acc[b % 2], rem[b % 2]
                            kw = dict(start=False, skip_group_check=True)
                            pe.matmul(z[:, 0:2 * P], tri_ge, r[:, 0:2 * P], stop=True, **kw)
                            pe.matmul(z[:, P:2 * P], ones, r[:, 2 * P:W3], stop=True, **kw)
                            pe.matmul(z[:, 2 * P:W3], tri_ge, r[:, 2 * P:W3], stop=True, **kw).then_inc(cum_out, 1)
                        b = i - 2
                        if 0 <= b < HEADS:
                            pe.wait_ge(w_stick_ok, b + 1)
                            pe.wait_ge(pv_read, SOFT_A + b - 1)
                            w = w_stick[b % 2]
                            T = [w[:, P:2 * P], w[:, 2 * P:W3], w[:, 0:P]]
                            weigh(acc[2 + b % 2][:, 0:2 * HD], T, (HEADS + b) * HD).then_inc(pv_out, 1)
                else:
                    pe.wait_ge(logf_ok, 1)
                    for tb in range(TB):
                        F = px[1][:, tb * HEADS:(tb + 1) * HEADS]
                        if tb == 0:
                            pe.matmul(F, tri_le, logf[:, 0, :], start=True, stop=True)
                        else:
                            pe.matmul(F, ones, logf[:, 0, :], start=True, stop=False)
                            pe.matmul(F, tri_le, logf[:, 1, :], start=False, stop=True).then_inc(fcum_out, 1)
                    pe.wait_ge(fcum_ok, 1)
                    run_units(range(SOFT_A, SOFT_A + SOFT_C), L, 2)
                    pe.wait_ge(evac, evacs(L, 23))
                    run_units(range(SOFT_A + SOFT_C, SOFT_A + SOFT_C + SOFT_D))
                transpose_rows(3 * L + 1, o)
                for n in range(0, OUT_ITEMS, 2):
                    if n >= 4:
                        pe.wait_ge(mixed, OUT_ITEMS * L + n - 2)
                    pair_tokens(item(L, N_OUT + n), acc[n % 4:n % 4 + 2])
                transpose_rows(3 * L + 2, h)
                pe.wait_ge(s_keys, 16 * (L + 1))
                for e in range(Q_ITEMS + 1):
                    if e < Q_ITEMS:
                        if e >= 2:
                            pe.wait_ge(evac, evacs(L, N_Q + e - 2))
                        item_columns(item(L, N_Q + e), pu[e % 2])
                    if e > 0:
                        b = e - 1
                        pe.wait_ge(evac, evacs(L, N_Q + b))
                        if b % 4 == 0 and b > 0:
                            pe.wait_ge(sc_ok, 8 * L + 2 * (b // 4))
                        for tb in range(TB):
                            ins = pe.matmul(px[tb][:, (b % 4) * P:(b % 4 + 1) * P], qrow[:, b % 2, tb * P:(tb + 1) * P],
                                            keysT[:, b, :], start=True, stop=True)
                        ins.then_inc(q_out, 1)
                with pe.Fori(0, AHEAD // 2) as i:
                    for r in range(2):
                        pe.wait_ge(evac, evacs(L, N_U + r - 2) + i * 2)
                        item_columns(item(L, N_U + r), pu[r], i)
                for tb in range(TB):
                    pe.wait_ge(sc_ok, 8 * (L + 1))
                    pe.wait_ge(tab_ok, TB * L + tb + 1)
                    for n in range(3):
                        ins = pe.transpose(px[tb][:, n * P:(n + 1) * P], sc[:, tb, (n + 1) * P:(n + 2) * P], ident)
                    ins.then_inc(tabT_out, 1)

                def gates_group(q, i=0):
                    pe.wait_ge(oh_ok, GROUPS * L + q + 1 + i * 4)
                    if not isinstance(i, int) or q >= 4:
                        pe.wait_ge(g_copied, GROUPS * L + q - 3 + i * 4)
                    for t in range(GROUP):
                        ins = pe.matmul(acc[q % 4][:, t * NKEYS:(t + 1) * NKEYS], onehots[:, q % 4, 0, t],
                                        onehots[:, q % 4, 1, t], start=True, stop=True)
                    ins.then_inc(g_out, 1)

                for q in range(4):
                    gates_group(q)
                with pe.Fori(1, GROUPS // 4) as i:
                    for q in range(4):
                        gates_group(q, i)

                def v_item(r, i=0, first=False, last=False):
                    j = E_ * L + r
                    pe.wait_ge(w_ok, j + 1 + i * 2)
                    for f in range(2):
                        pe.wait_ge(v_lo_ok, 2 * j + f + 1 + i * 4)
                        half = slice(f * 512, (f + 1) * 512)
                        for tb in range(TB):
                            t = slice(tb * P, (tb + 1) * P)
                            ins = passes(acc[2 * tb + f][:, :], (w_hi[:, j % 2, t], w_lo[:, j % 2, t]),
                                         (v_hi[:, j % 2, half], v_lo[:, j % 2, half]), first, last)
                        ins.then_inc(v_used, 1)

                def u_item(r, i=0):
                    pe.wait_ge(evac, evacs(L, N_U + AHEAD + r - 2) + i * 2)
                    item_columns(item(L, N_U + AHEAD + r), pu[r % 2], i)

                pe.wait_ge(g_copied, GROUPS * (L + 1))
                for r in range(2):
                    v_item(r, first=(r == 0))
                    u_item(r)
                n = E_ - AHEAD
                with pe.Fori(0, n // 2 - 1) as i:
                    for r in range(2):
                        v_item(2 + r, i)
                        u_item(2 + r, i)
                with pe.Fori(0, AHEAD // 2 - 1) as i:
                    for r in range(2):
                        v_item(n + r, i)
                v_item(E_ - 2)
                v_item(E_ - 1, last=True)


def tables():
    p, f = np.arange(P)[:, None], np.arange(P)[None, :]
    ident = (p == f)
    iota = np.broadcast_to(f, (P, P))
    ge, le = (p >= f), (p <= f)
    one = np.ones((P, P))
    q3 = np.concatenate([np.arange(256), np.arange(128)])[None, :]
    past = q3 > p
    k3 = np.concatenate([np.arange(256) - 128, np.arange(128)])[None, :]
    causal = k3 <= p
    cols = [ident, iota, ge, le, -1.0 * le, one, -one, -1.0 * past, np.where(past, 0, NEG), np.where(causal, 0, NEG)]
    consts = np.concatenate([np.asarray(c, np.float32) for c in cols], axis=1)
    dist = 255 - np.arange(REL)
    n = np.maximum(dist, 0)
    nf = np.maximum(n, 1).astype(np.float32)
    large = 16 + (np.log(nf / np.float32(16)) / np.float32(np.log(8.0)) * np.float32(16)).astype(np.int32)
    bucket = np.where(n < 16, n, np.minimum(large, 31))
    onehot = (np.arange(32)[:, None] == bucket[None, :]).astype(np.float32)
    times = sum(((n % dil == 0) & (n <= win)).astype(np.int32) for win, dil in ((128, 1), (512, 4), (2048, 16)))
    dil = np.where((dist >= 0) & (times > 0), np.log(np.maximum(times, 1)), NEG)
    full = np.where(dist >= 0, 0.0, NEG)
    relmask = np.broadcast_to(np.stack([full, dil])[None], (HEADS, 2, REL)).astype(np.float32)
    return consts, onehot, np.ascontiguousarray(relmask)


def lay_out(x, t5_bias, ab_w_in, ab_lambda, ab_subln_g, ab_w_out, cd_w_in, cd_b_f, cd_w_out,
            peer_w_q, peer_sub_keys, peer_u, peer_v, ln_g, ln_b):
    a = {k: np.asarray(v) for k, v in dict(
        x=x, t5=t5_bias, ab_in=ab_w_in, lam=ab_lambda, sub=ab_subln_g, ab_out=ab_w_out, cd_in=cd_w_in, bf=cd_b_f,
        cd_out=cd_w_out, wq=peer_w_q, keys=peer_sub_keys, u=peer_u, v=peer_v, g=ln_g, b=ln_b).items()}

    def tiles(w):
        return w.reshape(DC, P, -1, P).transpose(2, 1, 0, 3).reshape(-1, P, D)

    stream = []
    for L, (w_in, w_out) in enumerate(((a["ab_in"][0], a["ab_out"][0]), (a["cd_in"][0], a["cd_out"][0]))):
        t = tiles(w_in[:, :IN_ITEMS * P])
        stream += [t[0:12], t[20:24], t[12:20], tiles(w_out), tiles(a["wq"][L])]
        u = a["u"][L].reshape(P, NKEYS, DC, P).transpose(1, 3, 2, 0).reshape(NKEYS, P, D)
        stream.append(u)
    consts, onehot, relmask = tables()
    return {
        "x": a["x"][0],
        "u_stream": np.concatenate(stream),
        "v_stream": np.ascontiguousarray(a["v"].reshape(LAYERS, P, NKEYS, D).transpose(0, 2, 1, 3).reshape(-1, P, D)),
        "keys": np.ascontiguousarray(a["keys"].transpose(0, 4, 1, 2, 3).reshape(LAYERS, P, Q_ITEMS, NKEYS)),
        "t5": a["t5"], "onehot": onehot, "relmask": relmask,
        "lam_vecs": a["lam"].reshape(-1), "subln": a["sub"].reshape(-1),
        "w_f": np.ascontiguousarray(a["cd_in"][0][:, IN_ITEMS * P:].reshape(DC, P, HEADS).transpose(1, 0, 2).reshape(P, -1)),
        "b_f": a["bf"].reshape(-1),
        "ln_g": a["g"].reshape(2 * LAYERS, D), "ln_b": a["b"].reshape(2 * LAYERS, D),
        "consts": consts,
    }


def kernel(**inputs):
    import concourse.bacc as bacc
    from concourse.bass_utils import run_bass_kernel_spmd

    arrays = {k: np.ascontiguousarray(v) for k, v in lay_out(**inputs).items()}
    nc = bacc.Bacc("TRN2", target_bir_lowering=False, num_devices=1, dynamic_dma_scratch_size=1024)
    aps = {k: nc.dram_tensor(f"in_{k}", v.shape, mybir.dt.from_np(v.dtype), kind="ExternalInput").ap()
           for k, v in arrays.items()}
    result = nc.dram_tensor("result", (SEQ, D), F32, kind="ExternalOutput").ap()
    build_program(nc, out=result, **aps)
    r = run_bass_kernel_spmd(nc, [{f"in_{k}": v for k, v in arrays.items()}], core_ids=[0])
    return r.results[0]["result"].reshape(1, SEQ, D)
```

```python
from contextlib import ExitStack

import numpy as np

import concourse.bass as bass
from concourse import mybir

F32 = mybir.dt.float32
F32R = mybir.dt.float32r
U32 = mybir.dt.uint32
ALU = mybir.AluOpType
ACT = mybir.ActivationFunctionType
AX = mybir.AxisListType
ds = bass.ds

P = 128
SEQ = 256
TB = SEQ // P
D = 1024
DC = D // P
LAYERS = 2
HEADS = 8
HD = 64
NKEYS = 128
TOPK = 16
EXPERT_ITEMS = NKEYS
IN_ITEMS = 24
OUT_ITEMS = 8
Q_ITEMS = 16
V_FIRST, V_ITEMS = 8, 8
N_OUT = IN_ITEMS
N_Q = N_OUT + OUT_ITEMS
N_U = N_Q + Q_ITEMS
ITEMS = N_U + EXPERT_ITEMS
EVACS = ITEMS - OUT_ITEMS
RAW = 4
AHEAD = 32
LATE = 16
NZ = 4
REST = EXPERT_ITEMS - AHEAD - LATE
GROUP = 4
GATE_LAG = 3
ALPHA = (2 * LAYERS) ** 0.25
LN_EPS = 1e-5
LAMBDA_INIT = 0.2
NEG = -1.0e30
LOWEST = -3.0e38
REL = 384
W3 = 384

C_KEEP = 2 * P
(C_GE, C_LE, C_NLE, C_ONE, C_NONE, C_STICK, C_PAST, C_CAUSAL) = (
    0, P, 2 * P, 3 * P, 4 * P, 5 * P, 5 * P + W3, 5 * P + 2 * W3)
C_COLS = 5 * P + 3 * W3
SOFT_A, SOFT_C, SOFT_D = 8, 4, 4


def build_program(nc, x, u_stream, v_stream, keys, t5, onehot, relmask, lam_vecs, subln, w_f, b_f,
                  ln_g, ln_b, consts, out):
    scratch = nc.dram_tensor("bias_rows", [LAYERS, HEADS, P, REL], F32, kind="Internal").ap()

    with ExitStack() as ctx:
        def sb(name, shape, dt=F32):
            return ctx.enter_context(nc.sbuf_tensor(name, shape, dt))

        def sem(name):
            return ctx.enter_context(nc.semaphore(name))

        gates = sb("gates", [P, SEQ, NKEYS])
        flat = gates[:, :, :].rearrange("p t j -> p (t j)")
        used = [0]

        def carve(*shape):
            n = int(np.prod(shape))
            a = flat[:, used[0]:used[0] + n]
            used[0] += n
            assert used[0] <= SEQ * NKEYS
            if len(shape) == 2:
                return a.rearrange("p (a b) -> p a b", a=shape[0])
            if len(shape) == 3:
                return a.rearrange("p (a b c) -> p a b c", a=shape[0], b=shape[1])
            return a

        u_raw = sb("u_raw", [P, RAW, DC, P])
        u_hi = sb("u_hi", [P, 2, DC, P], F32R)
        u_lo = sb("u_lo", [P, 2, DC, P], F32R)
        v_hi_at = nc.sbuf_base
        v_hi = sb("v_hi", [P, 2, D], F32R)
        v_lo = sb("v_lo", [P, 2, D], F32R)
        late_at = nc.sbuf_base
        v_raw = sb("v_raw", [P, 2, D])
        w_hi_at = nc.sbuf_base
        w_hi = sb("w_hi", [P, 2, SEQ], F32R)
        w_lo = sb("w_lo", [P, 2, SEQ], F32R)
        gain_at = nc.sbuf_base
        top_s = sb("top_s", [P, TB, 2 * HEADS, TOPK])
        top_i = sb("top_i", [P, TB, 2 * HEADS, TOPK], U32)
        xT_hi = sb("xT_hi", [P, DC, SEQ], F32R)
        xT_lo = sb("xT_lo", [P, DC, SEQ], F32R)
        h = sb("h", [P, TB, D])
        shift_at = nc.sbuf_base
        act = sb("act", [P, 2, SEQ])
        wf_hi, wf_lo = (w_hi[:, b, 0:DC * HEADS].rearrange("p (c k) -> p c k", c=DC) for b in range(2))
        tabT = sb("tabT", [P, 3, SEQ])
        keep = sb("keep", [P, C_KEEP])
        ident, iota = keep[:, 0:P], keep[:, P:2 * P]
        small = sb("small", [P, 64])
        sc = nc.alloc_sbuf_tensor_at("scores", [P, TB, 2 * HEADS * NKEYS], F32, offset=v_hi_at)
        tmp = nc.alloc_sbuf_tensor_at("tmp", [P, 8, P], F32, offset=w_hi_at)
        tmpu = nc.alloc_sbuf_tensor_at("tmpu", [P, 8, P], U32, offset=w_hi_at)
        qrow = tmp[:, 0:4, :].rearrange("p (e t) k -> p e (t k)", e=2)
        onehots = nc.alloc_sbuf_tensor_at("onehots", [P, 4, 2, GROUP, NKEYS], F32, offset=v_hi_at)
        gain = nc.alloc_sbuf_tensor_at("gain", [P, D], F32, offset=gain_at)
        shift = nc.alloc_sbuf_tensor_at("shift", [P, D], F32, offset=shift_at)
        late = nc.alloc_sbuf_tensor_at("late", [P, LATE, SEQ], F32, offset=late_at)
        keysT = v_raw[:, :, :].rearrange("p a (e k) -> p (a e) k", k=NKEYS)

        qkT = carve(16, SEQ)
        vals = carve(TB, 2 * HEADS * HD)
        o = carve(TB, 2 * HEADS * HD)
        bias = carve(HEADS, W3)
        cst = carve(C_COLS)
        logits = [carve(2, W3) for _ in range(2)]
        diffw = [carve(W3) for _ in range(2)]
        probsT = [carve(2, W3) for _ in range(2)]
        z_abs, rem, z_cum, w_stick = ([carve(W3) for _ in range(NZ)] for _ in range(4))
        sq = carve(TB, HEADS * HD)
        wf = carve(DC, HEADS)
        bfr = carve(HEADS)
        subr = carve(HD)
        lv = carve(2, 2, 32)
        lvp = carve(2, 32)
        t5s = carve(HEADS)
        rowc = carve(3, REL)
        rowb = carve(2, REL)
        ssum = [carve(4) for _ in range(2)]
        nmax = [carve(4) for _ in range(2)]
        rsum = [carve(4) for _ in range(2)]
        fneg = [carve(2) for _ in range(2)]
        lam = carve(4)
        rms = carve(2 * HEADS)
        fgx = carve(2, HEADS)
        fga = carve(2, HEADS)
        logf = carve(2, HEADS)
        fcum = carve(2, HEADS)
        tri_ge, tri_le, ntri_le = (cst[:, a:a + P] for a in (C_GE, C_LE, C_NLE))
        ones, nones = cst[:, C_ONE:C_ONE + P], cst[:, C_NONE:C_NONE + P]
        stick_neg, past_mask, causal = (cst[:, a:a + W3] for a in (C_STICK, C_PAST, C_CAUSAL))

        acc = [ctx.enter_context(nc.psum_tensor(f"acc{i}", [P, 512], F32)) for i in range(4)]
        pu = [ctx.enter_context(nc.psum_tensor(f"pu{i}", [P, 512], F32)) for i in range(2)]
        px = [ctx.enter_context(nc.psum_tensor(f"px{i}", [P, 512], F32)) for i in range(2)]

        zbank = [acc[0], acc[1], pu[0], pu[1]]

        s_load = sem("s_load")
        s_bias = sem("s_bias")
        s_cload = sem("s_cload")
        s_lnload = sem("s_lnload")
        s_keys = sem("s_keys")
        s_rows = sem("s_rows")
        u_in = [sem(f"u_in{i}") for i in range(RAW)]
        v_in = [[sem(f"v_in{f}_{i}") for i in range(2)] for f in range(2)]
        u_hi_ok = [sem(f"u_hi_ok{f}") for f in range(2)]
        u_lo_ok = [sem(f"u_lo_ok{f}") for f in range(2)]
        u_used = [sem(f"u_used{f}") for f in range(2)]
        evac = sem("evac")
        mixed = sem("mixed")
        v_hi_ok = sem("v_hi_ok")
        v_lo_ok = sem("v_lo_ok")
        v_used = sem("v_used")
        w_hi_ok = sem("w_hi_ok")
        w_ok = sem("w_ok")
        gated = sem("gated")
        rows_ok = sem("rows_ok")
        tr_out = sem("tr_out")
        xT_hi_ok = sem("xT_hi_ok")
        xT_ok = sem("xT_ok")
        s_out = sem("s_out")
        s_read = sem("s_read")
        nmax_ok = sem("nmax_ok")
        exp_ok = sem("exp_ok")
        w_diff_ok = sem("w_diff_ok")
        wT_out = sem("wT_out")
        wT_ok = sem("wT_ok")
        pv_out = sem("pv_out")
        pv_read = sem("pv_read")
        z_out = sem("z_out")
        sp_log_ok = sem("sp_log_ok")
        rem_ok = sem("rem_ok")
        cum_out = sem("cum_out")
        z_cum_ok = sem("z_cum_ok")
        w_stick_ok = sem("w_stick_ok")
        var_ok = sem("var_ok")
        sd_ok = sem("sd_ok")
        t5_out = sem("t5_out")
        rowb_ok = sem("rowb_ok")
        lam_sum = sem("lam_sum")
        lam_exp = sem("lam_exp")
        rms_sum = sem("rms_sum")
        rms_sd = sem("rms_sd")
        wf_hi_ok = sem("wf_hi_ok")
        wf_ok = sem("wf_ok")
        f_out = sem("f_out")
        f_abs = sem("f_abs")
        f_log = sem("f_log")
        logf_ok = sem("logf_ok")
        fcum_out = sem("fcum_out")
        fcum_ok = sem("fcum_ok")
        q_out = sem("q_out")
        sc_ok = sem("sc_ok")
        gsub = sem("gsub")
        gexp = sem("gexp")
        tab_ok = sem("tab_ok")
        tabT_out = sem("tabT_out")
        tabT_ok = sem("tabT_ok")
        eq_ok = sem("eq_ok")
        oh_ok = sem("oh_ok")
        oh_ok_act = sem("oh_ok_act")
        g_out = sem("g_out")
        late_gated = sem("late_gated")
        g_mul = sem("g_mul")
        g_copied = sem("g_copied")
        act_step = sem("act_step")
        dve_step = sem("dve_step")
        stored = sem("stored")

        GROUPS = SEQ // GROUP
        layers = range(LAYERS)
        E_ = EXPERT_ITEMS

        def item(L, n):
            return L * ITEMS + n

        def evacs(L, n):
            return L * EVACS + n + 1 - (OUT_ITEMS if n >= N_Q else 0)

        def score_bank(su, m):
            return zbank[m + (2 * (su % 2) if su >= SOFT_A + SOFT_C else 0)]

        block = ctx.enter_context(nc.Block())

        @block.sync
        def _(sp):
            def load_item(k, i=0):
                if k >= RAW:
                    sp.wait_ge(u_lo_ok[1], k - RAW + 1 + i * RAW)
                src = u_stream[k] if isinstance(i, int) else u_stream[ds(i * RAW + k, 1)].rearrange("o p f -> (o p) f")
                sp.dma_start(u_raw[:, k % RAW].rearrange("p c k -> p (c k)"), src).then_inc(u_in[k % RAW], 16)

            def load_v(j, i=0, step=2):
                src = v_stream[j] if isinstance(i, int) else v_stream[ds(i * step + j, 1)].rearrange("o p f -> (o p) f")
                for f in range(2):
                    if j >= 2:
                        sp.wait_ge(v_lo_ok, (j - 2) * 2 + f + 1 + i * (2 * step))
                    half = slice(f * 512, (f + 1) * 512)
                    sp.dma_start(v_raw[:, j % 2, half], src[:, half]).then_inc(v_in[f][j % 2], 16)

            def load_consts(L):
                sp.dma_start(cst, consts[:, C_KEEP:]).then_inc(s_cload, 16)
                sp.dma_start(wf.rearrange("p c k -> p (c k)"), w_f).then_inc(s_cload, 16)
                sp.dma_start(bfr, b_f.partition_broadcast(P)).then_inc(s_cload, 16)
                sp.dma_start(subr, subln.partition_broadcast(P)).then_inc(s_cload, 16)

            def load_bias(L):
                at = L * HEADS * P * REL + P - 1
                sp.dma_start(bias[:, :, 0:2 * P], bass.AP(scratch.tensor, at, [[REL - 1, P], [P * REL, HEADS], [1, 2 * P]])
                             ).then_inc(s_bias, 16)
                sp.dma_start(bias[:, :, 2 * P:W3], bass.AP(scratch.tensor, at + P, [[REL - 1, P], [P * REL, HEADS], [1, P]])
                             ).then_inc(s_bias, 16)

            def store_rows(L):
                sp.dma_start(scratch[L], rowb[0:HEADS, L, :].unsqueeze(1).to_broadcast([HEADS, P, REL])
                             ).then_inc(s_rows, 16)

            def load_norm(q):
                sp.dma_start(gain[:, :], ln_g[q].partition_broadcast(P)).then_inc(s_lnload, 16)
                sp.dma_start(shift[:, :], ln_b[q].partition_broadcast(P)).then_inc(s_lnload, 16)

            sp.dma_start(h[:, :, :], x.rearrange("(t p) d -> p t d", p=P)).then_inc(s_load, 16)
            sp.dma_start(keep[:, :], consts[:, 0:C_KEEP]).then_inc(s_load, 16)
            for k in range(RAW):
                load_item(k)
            sp.dma_start(t5s[0:32, :], t5).then_inc(s_load, 16)
            sp.dma_start(rowc[0:32, 0, :], onehot).then_inc(s_load, 16)
            sp.dma_start(rowc[0:HEADS, 1:3, :], relmask).then_inc(s_load, 16)
            sp.dma_start(lv.rearrange("p a b c -> p (a b c)"), lam_vecs.partition_broadcast(P)).then_inc(s_load, 16)
            for L in layers:
                if L > 0:
                    sp.wait_ge(w_ok, E_ * L)
                if L > 0:
                    sp.wait_ge(s_rows, 16 * (L + 1))
                    load_bias(L)
                load_consts(L)
                if L == 0:
                    sp.wait_ge(rowb_ok, 1)
                    store_rows(0)
                    sp.wait_ge(s_rows, 16)
                    load_bias(L)
                for n in range(RAW, N_OUT):
                    load_item(item(L, n))
                if L > 0:
                    sp.wait_ge(rows_ok, 4 * 3 * L)
                load_norm(2 * L)
                for n in range(N_OUT, N_OUT + 4):
                    load_item(item(L, n))
                if L == 0:
                    for m in range(1, LAYERS):
                        store_rows(m)
                if L > 0:
                    sp.wait_ge(v_lo_ok, 2 * E_ * L)
                sp.dma_start(keysT, keys[L]).then_inc(s_keys, 16)
                first = item(L, N_OUT + 4)
                with sp.Fori(0, (OUT_ITEMS - 4 + Q_ITEMS + AHEAD + LATE + 4) // RAW) as i:
                    for r in range(RAW):
                        load_item(first + r, i)
                for r in range(2):
                    sp.wait_ge(late_gated, LATE * L + 4 * (r + 1))
                    load_v(E_ * L + r)
                first = item(L, N_U + AHEAD + LATE + 4)
                if L + 1 < LAYERS:
                    pairs = REST
                else:
                    pairs = REST - 4
                with sp.Fori(0, pairs // RAW) as i:
                    for r in range(RAW):
                        load_item(first + r, i)
                        load_v(E_ * L + 2 + r, i, RAW)
                for r in range(8):
                    load_v(E_ * L + 2 + pairs + r)
                sp.wait_ge(gated, REST * (L + 1))
                load_norm(2 * L + 1)
                with sp.Fori(0, (E_ - 10 - pairs) // 2) as i:
                    for r in range(2):
                        load_v(E_ * L + 10 + pairs + r, i)
            for tb in range(TB):
                sp.wait_ge(rows_ok, 4 * (3 * LAYERS - 1) + 2 * tb + 2)
                sp.dma_start(out[tb * P:(tb + 1) * P, :], h[:, tb, :]).then_inc(stored, 16)
            sp.wait_ge(stored, 16 * TB)

        @block.gpsimd
        def _(pool):
            def low(k, f, i=0):
                pool.wait_ge(u_hi_ok[f], k + 1 + i * RAW)
                half = slice(f * DC // 2, (f + 1) * DC // 2)
                pool.tensor_tensor(u_lo[:, k % 2, half], u_raw[:, k % RAW, half],
                                   u_hi[:, k % 2, half].bitcast(F32), ALU.subtract).then_inc(u_lo_ok[f], 1)

            def lows(k, n):
                with pool.Fori(0, n // RAW) as i:
                    for r in range(RAW):
                        for f in range(2):
                            low(k + r, f, i)
                for r in range(n // RAW * RAW, n):
                    for f in range(2):
                        low(k + r, f)

            def low_pairs(k, n):
                with pool.Fori(0, n // RAW) as i:
                    for r in range(0, RAW, 2):
                        for f in range(2):
                            low(k + r, f, i)
                            low(k + r + 1, f, i)

            def weigh_onehots(L, q, i=0):
                pool.wait_ge(eq_ok, GROUPS * L + q + 1 + i * 16)
                tok = ds(i * (16 * GROUP) + q * GROUP, GROUP)
                pool.tensor_tensor(onehots[:, q % 4, 1], onehots[:, q % 4, 1],
                                   tabT[:, 2, tok].unsqueeze(2).to_broadcast([P, GROUP, NKEYS]), ALU.mult
                                   ).then_inc(oh_ok, 1)

            for L in layers:
                lows(item(L, 0), V_FIRST)
                low_pairs(item(L, V_FIRST), V_ITEMS)
                lows(item(L, V_FIRST + V_ITEMS), N_OUT - V_FIRST - V_ITEMS)
                low_pairs(item(L, N_OUT), OUT_ITEMS)
                lows(item(L, N_Q), Q_ITEMS + AHEAD + 2)
                weigh_onehots(L, 0)
                weigh_onehots(L, 1)

                def beside(r, i=0, last=False):
                    k = item(L, N_U + AHEAD + 2 + r)
                    weigh_onehots(L, 4 * r + 2, i)
                    low(k, 0, i)
                    if not last:
                        weigh_onehots(L, 4 * r + 4, i)
                        weigh_onehots(L, 4 * r + 5, i)
                    low(k, 1, i)

                with pool.Fori(0, LATE // RAW - 1) as i:
                    for r in range(RAW):
                        beside(r, i)
                for r in range(LATE - RAW, LATE):
                    beside(r, last=(r == LATE - 1))
                lows(item(L, N_U + AHEAD + LATE + 2), REST - 2)

        @block.scalar
        def _(a):
            steps = [0]

            def step(ins):
                ins.then_inc(act_step, 1)
                steps[0] += 1
                a.wait_ge(act_step, steps[0])

            def round_item(k, i=0, period=RAW):
                a.wait_ge(u_in[k % RAW], 16 * (k // RAW + 1) + i * (16 * period // RAW))
                for f in range(2):
                    round_half(k, f, i, period)

            def round_half(k, f, i=0, period=RAW):
                if k >= 2:
                    a.wait_ge(u_used[f], k - 1 + i * period)
                half = slice(f * DC // 2, (f + 1) * DC // 2)
                a.activation(u_hi[:, k % 2, half], u_raw[:, k % RAW, half], ACT.Copy).then_inc(u_hi_ok[f], 1)

            def round_pair(k):
                for n in (k, k + 1):
                    a.wait_ge(u_in[n % RAW], 16 * (n // RAW + 1))
                for f in range(2):
                    round_half(k, f)
                    round_half(k + 1, f)

            def round_v(j, i=0, period=2):
                for f in range(2):
                    a.wait_ge(v_in[f][j % 2], 16 * (j // 2 + 1) + i * (16 * period // 2))
                    if j >= 2:
                        a.wait_ge(v_used, 2 * (j - 2) + f + 1 + i * (2 * period))
                    half = slice(f * 512, (f + 1) * 512)
                    a.activation(v_hi[:, j % 2, half], v_raw[:, j % 2, half], ACT.Copy).then_inc(v_hi_ok, 1)

            def next_item(k):
                if k + 2 < LAYERS * ITEMS:
                    round_item(k + 2)

            def split_rows(s):
                for g in range(4):
                    tb, half = g // 2, g % 2
                    a.wait_ge(tr_out, 4 * s + g + 1)
                    a.activation(xT_hi[:, 4 * half:4 * half + 4, tb * P:(tb + 1) * P],
                                 px[g % 2][:, :].rearrange("p (c t) -> p c t", c=4), ACT.Copy).then_inc(xT_hi_ok, 1)

            def norm_sd(q):
                for tb in range(TB):
                    a.wait_ge(var_ok, TB * q + tb + 1)
                    a.activation(small[:, 16 + tb:17 + tb], small[:, 14 + tb:15 + tb], ACT.Sqrt).then_inc(sd_ok, 1)

            def take_in(L, n):
                a.wait_ge(u_used[1], item(L, n) + 1)
                tile = n if n < V_FIRST else n - V_ITEMS
                query = n < 4 or 16 <= n < 20
                scale = HD ** -0.5 if query and not (L == 0 and n < 4) else 1.0
                a.activation(qkT[:, tile, :], pu[n % 2][:, 0:SEQ], ACT.Copy, scale=scale).then_inc(evac, 1)

            def take_values(L, n):
                a.wait_ge(u_used[1], item(L, n) + 2)
                m = n - V_FIRST
                for tb in range(TB):
                    ins = a.activation(vals[:, tb, m * P:(m + 2) * P], acc[m % 4 + tb][:, 0:2 * P], ACT.Copy)
                ins.then_inc(evac, 2)

            def exps(su):
                b = su % 2
                a.wait_ge(nmax_ok, su + 1)
                for m in range(2):
                    a.activation(logits[b][:, m, 0:2 * P], logits[b][:, m, 0:2 * P], ACT.Exp,
                                 bias=nmax[b][:, m:m + 1], accum_out=ssum[b][:, 2 * m + 1:2 * m + 2])
                    ins = a.activation(logits[b][:, m, 2 * P:W3], logits[b][:, m, 2 * P:W3], ACT.Exp,
                                       bias=nmax[b][:, 2 + m:3 + m], accum_out=ssum[b][:, 2 * m:2 * m + 1])
                ins.then_inc(exp_ok, 1)

            def take_T(su):
                b = su % 2
                if su < SOFT_A:
                    a.wait_ge(wT_out, su + 1)
                    a.activation(probsT[b][:, 0, :], px[b][:, 0:W3], ACT.Copy).then_inc(wT_ok, 1)
                else:
                    for m in range(2):
                        n = SOFT_A + 2 * (su - SOFT_A) + m + 1
                        a.wait_ge(wT_out, n)
                        a.activation(probsT[b][:, m, :], px[m][:, 0:W3], ACT.Copy).then_inc(wT_ok, 1)

            a.preload_act_table_set("natural_log_exp_and_others")
            a.wait_ge(lam_sum, 1)
            a.activation(lam[:, 2:4], lam[:, 0:2], ACT.Exp).then_inc(lam_exp, 1)
            for L in layers:
                if L == 0:
                    round_item(0)
                    round_item(1)
                split_rows(3 * L)
                n0 = V_FIRST + V_ITEMS
                for n in range(V_FIRST):
                    next_item(item(L, n))
                    take_in(L, n)
                for n in range(V_FIRST, n0, 2):
                    round_pair(item(L, n + 2))
                    take_values(L, n)
                if L == 1:
                    a.preload_act_table_set("natural_log_exp_and_others")
                    a.wait_ge(f_abs, 1)
                    step(a.activation(fga, fga, ACT.Exp))
                    a.activation(fga, fga, ACT.Ln, bias=1.0).then_inc(f_log, 1)
                units = [range(0, SOFT_A), range(SOFT_A, SOFT_A + SOFT_C)][L]
                per = 8 // len(units)
                for i in range(len(units) + 1):
                    if i < len(units):
                        exps(units[i])
                        for n in range(n0 + per * i, n0 + per * i + per):
                            next_item(item(L, n))
                            take_in(L, n)
                    if i > 0:
                        take_T(units[i - 1])
                if L == 0:
                    for i in range(HEADS + 3):
                        if i < HEADS:
                            b = i % NZ
                            a.wait_ge(z_out, i + 1)
                            if i >= NZ:
                                a.wait_ge(rem_ok, i - NZ + 1)
                            a.activation(z_abs[b], zbank[b][:, 0:W3], ACT.Abs).then_inc(act_step, 1)
                            steps[0] += 1
                        if i == 4:
                            a.wait_ge(rms_sum, 1)
                            a.activation(rms, rms, ACT.Sqrt).then_inc(rms_sd, 1)
                            a.preload_act_table_set("natural_log_exp_and_others")
                        m = i - 3
                        if m >= 0:
                            a.wait_ge(z_cum_ok, m + 1)
                            if m >= NZ:
                                a.wait_ge(pv_out, SOFT_A + m - NZ + 1)
                            a.activation(w_stick[m % NZ], z_cum[m % NZ], ACT.Exp).then_inc(w_stick_ok, 1)
                        if i < HEADS:
                            a.wait_ge(act_step, steps[0])
                            step(a.activation(z_abs[b], z_abs[b], ACT.Exp, scale=-1.0))
                            a.activation(z_abs[b], z_abs[b], ACT.Ln, bias=1.0).then_inc(sp_log_ok, 1)
                else:
                    units = range(SOFT_A + SOFT_C, SOFT_A + SOFT_C + SOFT_D)
                    for i in range(len(units) + 1):
                        if i < len(units):
                            exps(units[i])
                        if i > 0:
                            take_T(units[i - 1])
                split_rows(3 * L + 1)
                a.preload_act_table(ACT.Sqrt)
                for n in range(N_OUT, N_Q, 2):
                    round_pair(item(L, n + 2))
                norm_sd(2 * L)
                split_rows(3 * L + 2)
                for e in range(Q_ITEMS + 1):
                    if e < Q_ITEMS:
                        k = item(L, N_Q + e)
                        next_item(k)
                        a.wait_ge(u_used[1], k + 1)
                        if e >= 2:
                            a.wait_ge(q_out, Q_ITEMS * L + e - 1)
                        a.activation(qrow[:, e % 2, :], pu[e % 2][:, 0:SEQ], ACT.Copy).then_inc(evac, 1)
                    if e > 0 and e % 4 == 0:
                        a.wait_ge(q_out, Q_ITEMS * L + e)
                        for tb in range(TB):
                            a.activation(sc[:, tb, (e - 4) * P:e * P], px[tb][:, :], ACT.Copy).then_inc(sc_ok, 1)
                a.wait_ge(s_rows, 16 * LAYERS)
                a.preload_act_table(ACT.Gelu)
                with a.Fori(0, AHEAD // RAW) as i:
                    for r in range(RAW):
                        k = item(L, N_U + r)
                        round_item(k + 2, i)
                        a.wait_ge(u_used[1], k + 1 + i * RAW)
                        a.activation(gates[:, :, ds(i * RAW + r, 1)].rearrange("p t o -> p (t o)"),
                                     pu[r % 2][:, 0:SEQ], ACT.Gelu).then_inc(evac, 1)
                for tb in range(TB):
                    a.wait_ge(gsub, TB * L + tb + 1)
                    a.activation(top_s[:, tb, 0:8, :], top_s[:, tb, 0:8, :], ACT.Exp).then_inc(gexp, 1)
                for tb in range(TB):
                    a.wait_ge(tabT_out, TB * L + tb + 1)
                    a.activation(tabT[:, :, tb * P:(tb + 1) * P],
                                 px[tb][:, 0:3 * P].rearrange("p (a t) -> p a t", a=3), ACT.Copy).then_inc(tabT_ok, 1)

                def copy_gates(q, i):
                    a.wait_ge(g_mul, GROUPS * L + q + 1 + i * 16)
                    a.activation(gates[:, ds(i * (16 * GROUP) + q * GROUP, GROUP), AHEAD:NKEYS],
                                 acc[q % 4][:, :].rearrange("p (t j) -> p t j", t=GROUP)[:, :, AHEAD:NKEYS],
                                 ACT.Copy).then_inc(g_copied, 1)

                def weigh_onehots(q, i):
                    a.wait_ge(eq_ok, GROUPS * L + q + 1 + i * 16)
                    for t in range(GROUP):
                        row = onehots[:, q % 4, 1, t]
                        tok = ds(i * (16 * GROUP) + q * GROUP + t, 1)
                        ins = a.activation(row, row, ACT.Copy, scale=tabT[:, 2, tok])
                    ins.then_inc(oh_ok_act, 1)

                a.preload_act_table(ACT.Gelu)
                with a.Fori(0, LATE // RAW) as i:
                    for r in range(RAW):
                        k = item(L, N_U + AHEAD + r)
                        copy_gates(4 * r, i)
                        weigh_onehots(4 * r + 3, i)
                        copy_gates(4 * r + 1, i)
                        a.wait_ge(u_in[(k + 2) % RAW], 16 * ((k + 2) // RAW + 1) + i * 16)
                        round_half(k + 2, 0, i)
                        copy_gates(4 * r + 2, i)
                        copy_gates(4 * r + 3, i)
                        round_half(k + 2, 1, i)
                        a.wait_ge(u_used[1], k + 1 + i * RAW)
                        a.activation(late[:, ds(i * RAW + r, 1)].rearrange("p o t -> p (o t)"),
                                     pu[r % 2][:, 0:SEQ], ACT.Gelu).then_inc(evac, 1)

                def both(i, s, last=False):
                    k = item(L, N_U + AHEAD + LATE + s)
                    if s >= 2:
                        round_v(E_ * L + s, i, RAW)
                    if not last:
                        round_item(k + 2, i)
                    a.wait_ge(u_used[1], k + 1 + i * RAW)
                    if L > 0 or s >= 2:
                        a.wait_ge(gated, REST * L + s - 1 + i * RAW)
                    a.activation(act[:, s % 2, :], pu[s % 2][:, 0:SEQ], ACT.Gelu).then_inc(evac, 1)
                    if s < 2:
                        round_v(E_ * L + s)

                n = REST
                for r in range(RAW):
                    both(0, r)
                with a.Fori(0, n // RAW - 2) as i:
                    for r in range(RAW):
                        both(i, RAW + r)
                for r in range(RAW):
                    both(0, n - RAW + r, last=(L == LAYERS - 1 and r >= 2))
                a.preload_act_table(ACT.Sqrt)
                with a.Fori(0, (E_ - n) // 2) as i:
                    for r in range(2):
                        round_v(E_ * L + n + r, i)
                norm_sd(2 * L + 1)

        @block.vector
        def _(v):
            steps = [0]

            def mark(ins):
                ins.then_inc(dve_step, 1)
                steps[0] += 1
                return steps[0]

            def after(n):
                v.wait_ge(dve_step, n)

            def step(ins):
                after(mark(ins))

            def split_rows(s):
                for g in range(4):
                    tb, half = g // 2, g % 2
                    v.wait_ge(xT_hi_ok, 4 * s + g + 1)
                    part = (slice(None), slice(4 * half, 4 * half + 4), slice(tb * P, (tb + 1) * P))
                    v.tensor_tensor(xT_lo[part], px[g % 2][:, :].rearrange("p (c t) -> p c t", c=4),
                                    xT_hi[part].bitcast(F32), ALU.subtract).then_inc(xT_ok, 1)

            def norm(q):
                stats = lambda tb: small[:, 36 + 2 * tb:38 + 2 * tb]
                for tb in range(TB):
                    for f in range(2):
                        part = h[:, tb, 512 * f:512 * f + 512]
                        if q % 2 == 1:
                            step(v.scalar_tensor_tensor(part, part, ALPHA, acc[2 * tb + f][:, :], ALU.mult, ALU.add))
                        last = mark(v.bn_stats(small[:, 6 * f:6 * f + 6], part))
                    after(last)
                    step(v.bn_aggr(stats(tb), small[:, 0:12].rearrange("p (a b) -> p a b", a=2)))
                    v.tensor_scalar(small[:, 14 + tb:15 + tb], stats(tb)[:, 1:2], LN_EPS, None, ALU.add).then_inc(var_ok, 1)
                v.wait_ge(s_lnload, 32 * (q + 1))
                for tb in range(TB):
                    v.wait_ge(sd_ok, TB * q + tb + 1)
                    step(v.reciprocal(small[:, 18 + tb:19 + tb], small[:, 16 + tb:17 + tb]))
                    halves = [slice(0, 512), slice(512, 1024)]
                    n = [mark(v.scalar_tensor_tensor(h[:, tb, c], h[:, tb, c], stats(tb)[:, 0:1], gain[:, c],
                                                     ALU.subtract, ALU.mult)) for c in halves]
                    for c, m in zip(halves, n):
                        after(m)
                        v.scalar_tensor_tensor(h[:, tb, c], h[:, tb, c], small[:, 18 + tb:19 + tb], shift[:, c],
                                               ALU.mult, ALU.add).then_inc(rows_ok, 1)
                v.wait_ge(rows_ok, ROWS[q])

            ROWS = [4 * (3 * (q // 2) + q % 2 + 2) for q in range(2 * LAYERS)]

            def maps(su):
                b = su % 2
                v.wait_ge(s_out, su + 1)
                if su >= 2:
                    v.wait_ge(wT_out, su - 1 if su - 2 < SOFT_A else SOFT_A + 2 * (su - 1 - SOFT_A))
                for m in range(2):
                    S = score_bank(su, m)[:, 0:W3]
                    if su < SOFT_A:
                        ins = v.scalar_tensor_tensor(logits[b][:, m, :], S, 32.0 ** -0.5, bias[:, su, :],
                                                     ALU.mult, ALU.add)
                    elif su < SOFT_A + SOFT_C:
                        ins = v.tensor_tensor(logits[b][:, m, :], S, bias[:, 2 * (su - SOFT_A) + m, :], ALU.add)
                    else:
                        hh = 2 * (su - SOFT_A - SOFT_C) + m
                        v.scalar_tensor_tensor(logits[b][:, m, 0:2 * P], S[:, 0:2 * P], fcum[:, 1, hh:hh + 1],
                                               causal[:, 0:2 * P], ALU.add, ALU.add)
                        ins = v.scalar_tensor_tensor(logits[b][:, m, 2 * P:W3], S[:, 2 * P:W3],
                                                     fcum[:, 0, hh:hh + 1], causal[:, 2 * P:W3], ALU.add, ALU.add)
                ins.then_inc(s_read, 1)
                v.wait_ge(s_read, su + 1)
                v.tensor_reduce(nmax[b][:, 0:2], logits[b][:, :, 0:2 * P], AX.X, ALU.max, negate=True)
                v.tensor_reduce(nmax[b][:, 2:4], logits[b][:, :, 2 * P:W3], AX.X, ALU.max, negate=True
                                ).then_inc(nmax_ok, 1)

            def weights(su):
                b = su % 2
                v.wait_ge(exp_ok, su + 1)
                if su >= 2:
                    v.wait_ge(pv_read, PV[su - 2])
                step(v.reciprocal(rsum[b], ssum[b]))
                if su < SOFT_A:
                    step(v.scalar_tensor_tensor(fneg[b], ssum[b][:, 0:2], lam[:, 0:1], rsum[b][:, 2:4],
                                                ALU.mult, ALU.mult))
                    v.scalar_tensor_tensor(diffw[b][:, 0:2 * P], logits[b][:, 1, 0:2 * P], fneg[b][:, 1:2],
                                           logits[b][:, 0, 0:2 * P], ALU.mult, ALU.add)
                    v.scalar_tensor_tensor(diffw[b][:, 2 * P:W3], logits[b][:, 1, 2 * P:W3], fneg[b][:, 0:1],
                                           logits[b][:, 0, 2 * P:W3], ALU.mult, ALU.add).then_inc(w_diff_ok, 1)

            def outputs(su):
                b = su % 2
                v.wait_ge(pv_out, PV[su])
                if su < SOFT_A:
                    res = acc[2 + b][:, 0:2 * HD].rearrange("p (t d) -> p t d", t=2)
                    v.tensor_tensor(o[:, :, su * HD:(su + 1) * HD], res,
                                    rsum[b][:, 0:2].unsqueeze(2).to_broadcast([P, 2, HD]), ALU.mult).then_inc(pv_read, 1)
                else:
                    c = (su - SOFT_A) * 2 * HD
                    for m in range(2):
                        res = acc[2 + b][:, m * 2 * HD:(m + 1) * 2 * HD].rearrange("p (t d) -> p t d", t=2)
                        ins = v.tensor_tensor(o[:, :, c + m * HD:c + (m + 1) * HD], res,
                                              rsum[b][:, 2 * m:2 * m + 2].unsqueeze(2).to_broadcast([P, 2, HD]), ALU.mult)
                    ins.then_inc(pv_read, 1)

            PV = [su + 1 if su < SOFT_A else su + 1 + HEADS for su in range(SOFT_A + SOFT_C + SOFT_D)]

            def topk_first(L):
                for grp in range(4):
                    for tb in range(TB):
                        v.wait_ge(sc_ok, 2 * 4 * L + 2 * grp + tb + 1)
                        es = range(4 * grp, 4 * grp + 4)
                        row = {e: sc[:, tb, e * P:(e + 1) * P] for e in es}
                        best = lambda e, f: top_s[:, tb, e, 8 * f:8 * f + 8]
                        n = {e: mark(v.max(best(e, 0), row[e])) for e in es}
                        for f in range(2):
                            for e in es:
                                after(n[e])
                                n[e] = mark(v.max_index(top_i[:, tb, e, 8 * f:8 * f + 8], best(e, f), row[e]))
                            if f == 0:
                                for e in es:
                                    after(n[e])
                                    n[e] = mark(v.match_replace(row[e], best(e, 0), row[e], LOWEST))
                                for e in es:
                                    after(n[e])
                                    n[e] = mark(v.max(best(e, 1), row[e]))
                after(steps[0])

            def topk_second(L, tb):
                cand = sc[:, tb, :].rearrange("p (h a b) -> p h a b", h=HEADS, a=TOPK)
                ts = top_s[:, tb].rearrange("p (h c) k -> p h c k", c=2)
                step(v.tensor_tensor(cand, ts[:, :, 0, :].unsqueeze(3).to_broadcast([P, HEADS, TOPK, TOPK]),
                                     ts[:, :, 1, :].unsqueeze(2).to_broadcast([P, HEADS, TOPK, TOPK]), ALU.add))
                bests = top_s[:, tb, 0:8, :]
                pos = tmpu[:, 0, :].rearrange("p (h k) -> p h k", h=HEADS)
                for g in range(2):
                    hs = range(4 * g, 4 * g + 4)
                    row = {q: sc[:, tb, q * 2 * P:(q + 1) * 2 * P] for q in hs}
                    best = lambda q, f: bests[:, q, 8 * f:8 * f + 8]
                    n = {q: mark(v.max(best(q, 0), row[q])) for q in hs}
                    for f in range(2):
                        for q in hs:
                            after(n[q])
                            n[q] = mark(v.max_index(pos[:, q, 8 * f:8 * f + 8], best(q, f), row[q]))
                        if f == 0:
                            for q in hs:
                                after(n[q])
                                n[q] = mark(v.match_replace(row[q], best(q, 0), row[q], LOWEST))
                            for q in hs:
                                after(n[q])
                                n[q] = mark(v.max(best(q, 1), row[q]))
                after(steps[0])
                v.tensor_single_scalar(tmpu[:, 1, :], tmpu[:, 0, :], 4, ALU.logical_shift_right)
                step(v.tensor_single_scalar(tmpu[:, 2, :], tmpu[:, 0, :], TOPK - 1, ALU.bitwise_and))
                v.tensor_copy(tmp[:, 3, :], tmpu[:, 1, :])
                step(v.tensor_copy(tmp[:, 4, :], tmpu[:, 2, :]))
                work = sc[:, tb, :].rearrange("p (s a) -> p s a", a=TOPK)
                work4 = sc[:, tb, :].rearrange("p (h k a) -> p h k a", h=HEADS, k=TOPK)
                ti = top_i[:, tb].rearrange("p (h c) k -> p h c k", c=2)
                for side in range(2):
                    step(v.tensor_tensor(work, tmp[:, 3 + side, :].unsqueeze(2).to_broadcast([P, P, TOPK]),
                                         iota[:, 0:TOPK].unsqueeze(1).to_broadcast([P, P, TOPK]), ALU.is_equal))
                    step(v.tensor_tensor(work4, work4,
                                         ti[:, :, side, :].unsqueeze(2).to_broadcast([P, HEADS, TOPK, TOPK]), ALU.mult))
                    step(v.tensor_reduce(tmp[:, 5 + side, :], work, AX.X, ALU.add))
                sub = sc[:, tb, 0:P].rearrange("p (h k) -> p h k", h=HEADS)
                step(v.tensor_tensor(sub, bests, bests[:, :, 0:1].to_broadcast([P, HEADS, TOPK]), ALU.subtract))
                v.tensor_copy(bests, sub).then_inc(gsub, 1)
                dst = sc[:, tb, P:3 * P].rearrange("p (a s) -> p a s", a=2)
                step(v.tensor_copy(dst, tmp[:, 5:7, :]))

            def gate_weights(L, tb):
                bests = top_s[:, tb, 0:8, :]
                v.wait_ge(gexp, TB * L + tb + 1)
                step(v.tensor_reduce(small[:, 20:28], bests, AX.X, ALU.add))
                step(v.reciprocal(small[:, 28:36], small[:, 20:28]))
                v.tensor_tensor(sc[:, tb, 3 * P:4 * P].rearrange("p (h k) -> p h k", h=HEADS), bests,
                                small[:, 28:36].unsqueeze(2).to_broadcast([P, HEADS, TOPK]), ALU.mult).then_inc(tab_ok, 1)

            def onehot_group(L, q, i=0):
                if q >= 4 or not isinstance(i, int):
                    v.wait_ge(g_out, GROUPS * L + q - 3 + i * 4)
                tok = ds(i * (4 * GROUP) + q * GROUP, GROUP)
                shape = [P, GROUP, NKEYS]
                for side in (0, 1):
                    ins = v.tensor_tensor(onehots[:, q % 4, side], iota.unsqueeze(1).to_broadcast(shape),
                                          tabT[:, side, tok].unsqueeze(2).to_broadcast(shape), ALU.is_equal)
                ins.then_inc(eq_ok, 1)

            def gate_group(L, q, i=0):
                v.wait_ge(g_out, GROUPS * L + q + 1 + i * 4)
                g = gates[:, ds(i * (4 * GROUP) + q * GROUP, GROUP), 0:AHEAD]
                v.tensor_tensor(g, g, acc[q % 4][:, :].rearrange("p (t j) -> p t j", t=GROUP)[:, :, 0:AHEAD],
                                ALU.mult).then_inc(g_mul, 1)

            v.wait_ge(s_load, 16 * 6)
            step(v.tensor_tensor(lvp, lv[:, :, 0, :], lv[:, :, 1, :], ALU.mult))
            v.tensor_reduce(lam[:, 0:2], lvp, AX.X, ALU.add).then_inc(lam_sum, 1)
            v.wait_ge(t5_out, 1)
            for L in layers:
                ins = v.tensor_tensor(rowb[0:HEADS, L], px[0][0:HEADS, 0:REL], rowc[0:HEADS, 1 + L], ALU.add)
            ins.then_inc(rowb_ok, 1)
            v.wait_ge(lam_exp, 1)
            step(v.scalar_tensor_tensor(lam[:, 0:1], lam[:, 3:4], LAMBDA_INIT, lam[:, 2:3], ALU.subtract, ALU.subtract))

            for L in layers:
                split_rows(3 * L)
                v.wait_ge(s_cload, 64 * (L + 1))
                v.wait_ge(s_bias, 32 * (L + 1))
                if L == 1:
                    v.tensor_copy(wf_hi, wf).then_inc(wf_hi_ok, 1)
                    v.wait_ge(wf_hi_ok, 1)
                    v.tensor_tensor(wf_lo, wf, wf_hi.bitcast(F32), ALU.subtract).then_inc(wf_ok, 1)
                    v.wait_ge(f_out, 1)
                    step(v.tensor_tensor(fgx, px[0][:, 0:2 * HEADS].rearrange("p (t h) -> p t h", t=2),
                                         bfr.unsqueeze(1).to_broadcast([P, 2, HEADS]), ALU.add))
                    v.scalar_tensor_tensor(fga, fgx, -1.0, fgx, ALU.mult, ALU.min).then_inc(f_abs, 1)
                    v.wait_ge(f_log, 1)
                    v.scalar_tensor_tensor(logf, fgx, 0.0, fga, ALU.min, ALU.subtract).then_inc(logf_ok, 1)
                units = [range(0, SOFT_A), range(SOFT_A, SOFT_A + SOFT_C)][L]
                for i in range(len(units) + 2):
                    if i < len(units):
                        maps(units[i])
                    if 1 <= i <= len(units):
                        weights(units[i - 1])
                    if i >= 2:
                        outputs(units[i - 2])
                if L == 0:
                    oa = o[:, :, 0:HEADS * HD]
                    heads = lambda t: t.rearrange("p t (h d) -> p t h d", d=HD)
                    rv = rms.rearrange("p (t h) -> p t h", t=2)

                    def mean_squares():
                        v.wait_ge(pv_read, SOFT_A)
                        step(v.tensor_tensor(sq, oa, oa, ALU.mult))
                        step(v.tensor_reduce(rv, heads(sq), AX.X, ALU.add))
                        v.tensor_scalar(rms, rms, 1.0 / HD, LN_EPS, ALU.mult, ALU.add).then_inc(rms_sum, 1)
                        mark(v.tensor_scalar(subr, subr, 1.0 - LAMBDA_INIT, None, ALU.mult))

                    def rms_scaled(t):
                        if t == 0:
                            v.wait_ge(rms_sd, 1)
                            step(v.reciprocal(rms, rms))
                        step(v.tensor_tensor(heads(oa)[:, t], heads(oa)[:, t],
                                             rv[:, t].unsqueeze(2).to_broadcast([P, HEADS, HD]), ALU.mult))
                        return mark(v.tensor_tensor(heads(oa)[:, t], heads(oa)[:, t],
                                                    subr.unsqueeze(1).to_broadcast([P, HEADS, HD]), ALU.mult))

                    for i in range(HEADS + 4):
                        if i < HEADS:
                            b = i % NZ
                            z = zbank[b][:, 0:W3]
                            v.wait_ge(sp_log_ok, i + 1)
                            if i >= NZ:
                                v.wait_ge(cum_out, i - NZ + 1)
                            step(v.scalar_tensor_tensor(z_abs[b], z, 0.0, z_abs[b], ALU.max, ALU.add))
                            v.tensor_tensor(rem[b], z_abs[b], stick_neg, ALU.mult).then_inc(rem_ok, 1)
                        if i == 1:
                            mean_squares()
                        if i in (6, 7):
                            n = rms_scaled(i - 6)
                        m = i - 1
                        if 0 <= m < HEADS:
                            v.wait_ge(cum_out, m + 1)
                            if m >= NZ:
                                v.wait_ge(w_stick_ok, m - NZ + 1)
                            v.tensor_tensor(z_cum[m % NZ], zbank[m % NZ][:, 0:W3], past_mask, ALU.add).then_inc(z_cum_ok, 1)
                        m = i - 4
                        if m >= 0:
                            v.wait_ge(pv_out, SOFT_A + m + 1)
                            c = HEADS * HD + m * HD
                            v.tensor_copy(o[:, :, c:c + HD], acc[2 + m % 2][:, 0:2 * HD].rearrange("p (t d) -> p t d", t=2)
                                          ).then_inc(pv_read, 1)
                    v.wait_ge(pv_read, 2 * HEADS)
                    after(n)
                else:
                    v.wait_ge(fcum_out, 1)
                    v.tensor_copy(fcum, px[1][:, 0:2 * HEADS].rearrange("p (t h) -> p t h", t=2)).then_inc(fcum_ok, 1)
                    v.wait_ge(fcum_ok, 1)
                    units = range(SOFT_A + SOFT_C, SOFT_A + SOFT_C + SOFT_D)
                    for i in range(len(units) + 2):
                        if i < len(units):
                            maps(units[i])
                        if 1 <= i <= len(units):
                            weights(units[i - 1])
                        if i >= 2:
                            outputs(units[i - 2])
                    v.wait_ge(pv_read, 2 * HEADS + SOFT_C + SOFT_D)
                v.engine_nop().then_inc(rows_ok, 4)
                split_rows(3 * L + 1)
                for n in range(0, OUT_ITEMS, 2):
                    v.wait_ge(u_used[1], item(L, N_OUT + n) + 2)
                    for tb in range(TB):
                        part = h[:, tb, n * P:(n + 2) * P]
                        ins = v.scalar_tensor_tensor(part, part, ALPHA, acc[n % 4 + tb][:, 0:2 * P], ALU.mult, ALU.add)
                    ins.then_inc(mixed, 2)
                v.wait_ge(mixed, OUT_ITEMS * (L + 1))
                norm(2 * L)
                split_rows(3 * L + 2)

                topk_first(L)
                for tb in range(TB):
                    topk_second(L, tb)
                for tb in range(TB):
                    gate_weights(L, tb)
                v.wait_ge(tabT_ok, TB * (L + 1))
                v.wait_ge(evac, evacs(L, N_U + AHEAD - 1))
                for q in range(GATE_LAG):
                    onehot_group(L, q)
                for q in range(4):
                    onehot_group(L, q + GATE_LAG)
                    gate_group(L, q)
                with v.Fori(1, GROUPS // 4 - 1) as i:
                    for q in range(4):
                        onehot_group(L, q + GATE_LAG, i)
                        gate_group(L, q, i)
                for q in range(GROUPS - 4, GROUPS):
                    if q + GATE_LAG < GROUPS:
                        onehot_group(L, q + GATE_LAG)
                    gate_group(L, q)
                v.wait_ge(g_mul, GROUPS * (L + 1))
                v.wait_ge(g_copied, GROUPS * (L + 1))

                def low_v_half(r, f, i=0, period=2):
                    j = E_ * L + r
                    v.wait_ge(v_hi_ok, 2 * j + f + 1 + i * (2 * period))
                    half = slice(f * 512, (f + 1) * 512)
                    v.tensor_tensor(v_lo[:, j % 2, half], v_raw[:, j % 2, half], v_hi[:, j % 2, half].bitcast(F32),
                                    ALU.subtract).then_inc(v_lo_ok, 1)

                def split_w(r, i=0, period=2):
                    j = E_ * L + r
                    if j >= 2:
                        v.wait_ge(v_used, 2 * (j - 2) + 2 + i * (2 * period))
                    col = gates[:, :, ds(i * period + r, 1)].rearrange("p t o -> p (t o)")
                    v.tensor_copy(w_hi[:, j % 2], col).then_inc(w_hi_ok, 1)
                    v.wait_ge(w_hi_ok, j + 1 + i * period)
                    v.tensor_tensor(w_lo[:, j % 2], col, w_hi[:, j % 2].bitcast(F32), ALU.subtract).then_inc(w_ok, 1)

                def gate_item(r, i=0):
                    v.wait_ge(evac, evacs(L, N_U + AHEAD + LATE + r) + i * RAW)
                    col = gates[:, :, ds(i * RAW + AHEAD + LATE + r, 1)].rearrange("p t o -> p (t o)")
                    v.tensor_tensor(col, col, act[:, r % 2], ALU.mult).then_inc(gated, 1)

                v.wait_ge(evac, evacs(L, N_U + AHEAD + LATE - 1))
                for m in range(LATE):
                    col = gates[:, :, AHEAD + m]
                    v.tensor_tensor(col, col, late[:, m], ALU.mult).then_inc(late_gated, 1)
                v.wait_ge(late_gated, LATE * (L + 1))
                n = REST
                assert AHEAD >= 2 * RAW

                def main_step(s, i=0):
                    split_w(s, i, RAW)
                    low_v_half(s, 0, i, RAW)
                    low_v_half(s, 1, i, RAW)
                    gate_item(s, i)

                for s in range(RAW):
                    main_step(s)
                with v.Fori(0, n // RAW - 1) as i:
                    v.wait_ge(gated, n * L + RAW + i * RAW)
                    for s in range(RAW, 2 * RAW):
                        main_step(s, i)
                v.wait_ge(gated, n * (L + 1))
                with v.Fori(0, (E_ - n) // 2) as i:
                    for r in range(2):
                        low_v_half(n + r, 0, i)
                        split_w(n + r, i)
                        low_v_half(n + r, 1, i)
                v.wait_ge(v_used, 2 * E_ * (L + 1))
                norm(2 * L + 1)

        @block.tensor
        def _(pe):
            def passes(out_ap, lhs, rhs, start, stop):
                (lh, ll), (rh, rl) = lhs, rhs
                pe.matmul(out_ap, lh, rh, start=start, stop=False)
                pe.matmul(out_ap, lh, rl, start=False, stop=False)
                return pe.matmul(out_ap, ll, rh, start=False, stop=stop)

            def item_columns(k, bank, i=0, period=2):
                for f in range(2):
                    half_columns(k, f, bank, i, period)

            def half_columns(k, f, bank, i, period):
                pe.wait_ge(u_lo_ok[f], k + 1 + i * period)
                for c in range(f * DC // 2, (f + 1) * DC // 2):
                    ins = passes(bank[:, 0:SEQ], (u_hi[:, k % 2, c], u_lo[:, k % 2, c]),
                                 (xT_hi[:, c, :], xT_lo[:, c, :]), c == 0, c == DC - 1)
                ins.then_inc(u_used[f], 1)

            def pair_tokens(k, banks):
                for f in range(2):
                    pe.wait_ge(u_lo_ok[f], k + 2)
                    for c in range(f * DC // 2, (f + 1) * DC // 2):
                        for tb in range(TB):
                            t = slice(tb * P, (tb + 1) * P)
                            ins = passes(banks[tb][:, 0:2 * P], (xT_hi[:, c, t], xT_lo[:, c, t]),
                                         (u_hi[:, :, c], u_lo[:, :, c]), c == 0, c == DC - 1)
                    ins.then_inc(u_used[f], 2)

            def in_item(L, n):
                if n >= 2:
                    pe.wait_ge(evac, evacs(L, n - 2))
                item_columns(item(L, n), pu[n % 2])

            def transpose_rows(s, src):
                for g in range(4):
                    tb, half = g // 2, g % 2
                    if s == 0:
                        pe.wait_ge(s_load, 16 * 6)
                        if g == 0:
                            pe.wait_ge(rowb_ok, 1)
                    else:
                        pe.wait_ge(rows_ok, 4 * (s - 1) + g + 1)
                    if 4 * s + g >= 2:
                        pe.wait_ge(xT_ok, 4 * s + g - 1)
                    for c in range(4):
                        at = (4 * half + c) * P
                        ins = pe.transpose(px[g % 2][:, c * P:(c + 1) * P], src[:, tb, at:at + P], ident)
                    ins.then_inc(tr_out, 1)
                pe.wait_ge(xT_ok, 4 * s + 4)

            def head(tiles, hh, m=None):
                base = (hh % 2) * HD + (0 if m is None else 32 * m)
                n = HD if m is None else 32
                return qkT[base:base + n, tiles + hh // 2, :]

            def products(su):
                if su > SOFT_A + SOFT_C:
                    pe.wait_ge(s_read, su - 1)
                elif su >= 1:
                    pe.wait_ge(s_read, su)
                for m in range(2):
                    if su < SOFT_A:
                        q, k = head(0, su, m), head(4, su, m)
                    elif su < SOFT_A + SOFT_C:
                        hh = 2 * (su - SOFT_A) + m
                        q, k = head(0, hh), head(4, hh)
                    else:
                        hh = 2 * (su - SOFT_A - SOFT_C) + m
                        q, k = head(8, hh), head(12, hh)
                    forget = su >= SOFT_A + SOFT_C
                    S = score_bank(su, m)
                    ins = pe.matmul(S[:, 0:2 * P], q[:, P:2 * P], k[:, 0:2 * P], start=True, stop=True)
                    if forget:
                        f0 = logf[:, 0, hh:hh + 1].to_broadcast([P, P])
                        f1 = logf[:, 1, hh:hh + 1].to_broadcast([P, P])
                        pe.matmul(S[:, 0:P], f0, ntri_le, start=False, stop=True, skip_group_check=True)
                        pe.matmul(S[:, P:2 * P], f0, nones, start=False, stop=True, skip_group_check=True)
                        pe.matmul(S[:, P:2 * P], f1, ntri_le, start=False, stop=True, skip_group_check=True)
                    ins = pe.matmul(S[:, 2 * P:W3], q[:, 0:P], k[:, 0:P], start=True, stop=True)
                    if forget:
                        ins = pe.matmul(S[:, 2 * P:W3], f0, ntri_le, start=False, stop=True, skip_group_check=True)
                ins.then_inc(s_out, 1)

            def weights_T(su):
                b = su % 2
                if su < SOFT_A:
                    pe.wait_ge(w_diff_ok, su + 1)
                    if su >= 2:
                        pe.wait_ge(wT_ok, su - 1)
                    for blk in range(3):
                        ins = pe.transpose(px[b][:, blk * P:(blk + 1) * P], diffw[b][:, blk * P:(blk + 1) * P], ident)
                    ins.then_inc(wT_out, 1)
                else:
                    pe.wait_ge(exp_ok, su + 1)
                    for m in range(2):
                        n = SOFT_A + 2 * (su - SOFT_A) + m
                        pe.wait_ge(wT_ok, n - 1)
                        for blk in range(3):
                            ins = pe.transpose(px[m][:, blk * P:(blk + 1) * P], logits[b][:, m, blk * P:(blk + 1) * P], ident)
                        ins.then_inc(wT_out, 1)

            def weigh(out_ap, wT, col):
                v0, v1 = vals[:, 0, col:col + HD], vals[:, 1, col:col + HD]
                pe.matmul(out_ap[:, 0:HD], wT[2], v0, start=True, stop=True)
                pe.matmul(out_ap[:, HD:2 * HD], wT[0], v0, start=True, stop=False)
                return pe.matmul(out_ap[:, HD:2 * HD], wT[1], v1, start=False, stop=True)

            def attend(su):
                b = su % 2
                reads = su if su < SOFT_A else su + HEADS
                if reads >= 2:
                    pe.wait_ge(pv_read, reads - 1)
                if su < SOFT_A:
                    pe.wait_ge(wT_ok, su + 1)
                    T = [probsT[b][:, 0, k * P:(k + 1) * P] for k in range(3)]
                    weigh(acc[2 + b][:, 0:2 * HD], T, su * HD).then_inc(pv_out, 1)
                else:
                    for m in range(2):
                        pe.wait_ge(wT_ok, SOFT_A + 2 * (su - SOFT_A) + m + 1)
                        T = [probsT[b][:, m, k * P:(k + 1) * P] for k in range(3)]
                        ins = weigh(acc[2 + b][:, m * 2 * HD:(m + 1) * 2 * HD], T, (2 * (su - SOFT_A) + m) * HD)
                    ins.then_inc(pv_out, 1)

            def run_units(units, L=None, per=0):
                for i in range(len(units) + 2):
                    if i < len(units):
                        products(units[i])
                        for n in range(16 + per * i, 16 + per * i + per):
                            in_item(L, n)
                    if 1 <= i <= len(units):
                        weights_T(units[i - 1])
                    if i >= 2:
                        attend(units[i - 2])

            pe.wait_ge(s_load, 16 * 6)
            pe.matmul(px[0][0:HEADS, 0:REL], t5s[0:32, :], rowc[0:32, 0, :], start=True, stop=True).then_inc(t5_out, 1)
            for L in layers:
                transpose_rows(3 * L, h)
                for n in range(V_FIRST):
                    in_item(L, n)
                for m in range(0, V_ITEMS, 2):
                    if m >= 4:
                        pe.wait_ge(evac, evacs(L, V_FIRST + m - 3))
                    pair_tokens(item(L, V_FIRST + m), acc[m % 4:m % 4 + 2])
                if L == 1:
                    pe.wait_ge(wf_ok, 1)
                    for tb in range(TB):
                        t = slice(tb * P, (tb + 1) * P)
                        for c in range(DC):
                            ins = passes(px[0][:, tb * HEADS:(tb + 1) * HEADS], (xT_hi[:, c, t], xT_lo[:, c, t]),
                                         (wf_hi[:, c], wf_lo[:, c]), c == 0, c == DC - 1)
                    ins.then_inc(f_out, 1)
                pe.wait_ge(evac, evacs(L, 15))
                pe.wait_ge(s_cload, 64 * (L + 1))
                if L == 0:
                    run_units(range(0, SOFT_A), L, 1)
                    pe.wait_ge(evac, evacs(L, 23))
                    for i in range(HEADS + 4):
                        if i < HEADS:
                            if i >= NZ:
                                pe.wait_ge(z_cum_ok, i - NZ + 1)
                            elif i == 0:
                                pe.wait_ge(s_read, SOFT_A)
                            z = zbank[i % NZ]
                            q, k = head(8, i), head(12, i)
                            pe.matmul(z[:, 0:2 * P], k[:, 0:P], q[:, 0:2 * P], start=True, stop=False)
                            pe.matmul(z[:, 2 * P:W3], k[:, P:2 * P], q[:, P:2 * P], start=False, stop=True).then_inc(z_out, 1)
                        m = i - 2
                        if 0 <= m < HEADS:
                            pe.wait_ge(rem_ok, m + 1)
                            z, r = zbank[m % NZ], rem[m % NZ]
                            kw = dict(start=False, skip_group_check=True)
                            pe.matmul(z[:, 0:2 * P], tri_ge, r[:, 0:2 * P], stop=True, **kw)
                            pe.matmul(z[:, P:2 * P], ones, r[:, 2 * P:W3], stop=True, **kw)
                            pe.matmul(z[:, 2 * P:W3], tri_ge, r[:, 2 * P:W3], stop=True, **kw).then_inc(cum_out, 1)
                        m = i - 4
                        if m >= 0:
                            pe.wait_ge(w_stick_ok, m + 1)
                            pe.wait_ge(pv_read, SOFT_A + m - 1)
                            w = w_stick[m % NZ]
                            T = [w[:, P:2 * P], w[:, 2 * P:W3], w[:, 0:P]]
                            weigh(acc[2 + m % 2][:, 0:2 * HD], T, (HEADS + m) * HD).then_inc(pv_out, 1)
                else:
                    pe.wait_ge(f_abs, 1)
                    run_units(range(SOFT_A, SOFT_A + SOFT_C), L, 2)
                    pe.wait_ge(logf_ok, 1)
                    pe.wait_ge(wT_ok, SOFT_A + 2 * SOFT_C)
                    for tb in range(TB):
                        F = px[1][:, tb * HEADS:(tb + 1) * HEADS]
                        if tb == 0:
                            pe.matmul(F, tri_le, logf[:, 0, :], start=True, stop=True)
                        else:
                            pe.matmul(F, ones, logf[:, 0, :], start=True, stop=False)
                            pe.matmul(F, tri_le, logf[:, 1, :], start=False, stop=True).then_inc(fcum_out, 1)
                    pe.wait_ge(fcum_ok, 1)
                    pe.wait_ge(evac, evacs(L, 23))
                    run_units(range(SOFT_A + SOFT_C, SOFT_A + SOFT_C + SOFT_D))
                transpose_rows(3 * L + 1, o)
                for n in range(0, OUT_ITEMS, 2):
                    if n >= 4:
                        pe.wait_ge(mixed, OUT_ITEMS * L + n - 2)
                    pair_tokens(item(L, N_OUT + n), acc[n % 4:n % 4 + 2])
                transpose_rows(3 * L + 2, h)
                pe.wait_ge(s_keys, 16 * (L + 1))
                for e in range(Q_ITEMS + 1):
                    if e < Q_ITEMS:
                        if e >= 2:
                            pe.wait_ge(evac, evacs(L, N_Q + e - 2))
                        item_columns(item(L, N_Q + e), pu[e % 2])
                    if e > 0:
                        b = e - 1
                        pe.wait_ge(evac, evacs(L, N_Q + b))
                        if b % 4 == 0 and b > 0:
                            pe.wait_ge(sc_ok, 8 * L + 2 * (b // 4))
                        for tb in range(TB):
                            ins = pe.matmul(px[tb][:, (b % 4) * P:(b % 4 + 1) * P], qrow[:, b % 2, tb * P:(tb + 1) * P],
                                            keysT[:, b, :], start=True, stop=True)
                        ins.then_inc(q_out, 1)
                with pe.Fori(0, AHEAD // 2) as i:
                    for r in range(2):
                        pe.wait_ge(evac, evacs(L, N_U + r - 2) + i * 2)
                        item_columns(item(L, N_U + r), pu[r], i)
                for tb in range(TB):
                    pe.wait_ge(sc_ok, 8 * (L + 1))
                    pe.wait_ge(tab_ok, TB * L + tb + 1)
                    for n in range(3):
                        ins = pe.transpose(px[tb][:, n * P:(n + 1) * P], sc[:, tb, (n + 1) * P:(n + 2) * P], ident)
                    ins.then_inc(tabT_out, 1)

                def gates_group(q, i=0):
                    if q % 4 == 3:
                        pe.wait_ge(oh_ok_act, GROUPS // 4 * L + q // 4 + 1 + i * 4)
                    else:
                        pe.wait_ge(oh_ok, GROUPS // 4 * 3 * L + q // 4 * 3 + q % 4 + 1 + i * 12)
                    if q >= 4:
                        pe.wait_ge(g_copied, GROUPS * L + q - 3 + i * 16)
                    for t in range(GROUP):
                        ins = pe.matmul(acc[q % 4][:, t * NKEYS:(t + 1) * NKEYS], onehots[:, q % 4, 0, t],
                                        onehots[:, q % 4, 1, t], start=True, stop=True)
                    ins.then_inc(g_out, 1)

                def groups_and_item(r, i=0):
                    k = item(L, N_U + AHEAD + r)
                    for f in range(2):
                        gates_group(4 * r + 2 * f, i)
                        gates_group(4 * r + 2 * f + 1, i)
                        if f == 0:
                            pe.wait_ge(evac, evacs(L, N_U + AHEAD + r - 2) + i * RAW)
                        half_columns(k, f, pu[r % 2], i, RAW)

                for r in range(RAW):
                    groups_and_item(r)
                with pe.Fori(0, LATE // RAW - 1) as i:
                    for r in range(RAW, 2 * RAW):
                        groups_and_item(r, i)

                def v_item(r, i=0, first=False, last=False):
                    j = E_ * L + r
                    pe.wait_ge(w_ok, j + 1 + i * 2)
                    for f in range(2):
                        pe.wait_ge(v_lo_ok, 2 * j + f + 1 + i * 4)
                        half = slice(f * 512, (f + 1) * 512)
                        for tb in range(TB):
                            t = slice(tb * P, (tb + 1) * P)
                            ins = passes(acc[2 * tb + f][:, :], (w_hi[:, j % 2, t], w_lo[:, j % 2, t]),
                                         (v_hi[:, j % 2, half], v_lo[:, j % 2, half]), first, last)
                        ins.then_inc(v_used, 1)

                def u_item(r, i=0):
                    pe.wait_ge(evac, evacs(L, N_U + AHEAD + LATE + r - 2) + i * 2)
                    item_columns(item(L, N_U + AHEAD + LATE + r), pu[r % 2], i)

                u_item(0)
                u_item(1)
                pe.wait_ge(g_copied, GROUPS * (L + 1))
                for r in range(2):
                    v_item(r, first=(r == 0))
                    u_item(2 + r)
                n = REST
                with pe.Fori(0, n // 2 - 2) as i:
                    for r in range(2):
                        v_item(2 + r, i)
                        u_item(4 + r, i)
                with pe.Fori(0, (E_ - n) // 2) as i:
                    for r in range(2):
                        v_item(n - 2 + r, i)
                v_item(E_ - 2)
                v_item(E_ - 1, last=True)


def tables():
    p, f = np.arange(P)[:, None], np.arange(P)[None, :]
    ident = (p == f)
    iota = np.broadcast_to(f, (P, P))
    ge, le = (p >= f), (p <= f)
    one = np.ones((P, P))
    q3 = np.concatenate([np.arange(256), np.arange(128)])[None, :]
    past = q3 > p
    k3 = np.concatenate([np.arange(256) - 128, np.arange(128)])[None, :]
    causal = k3 <= p
    cols = [ident, iota, ge, le, -1.0 * le, one, -one, -1.0 * past, np.where(past, 0, NEG), np.where(causal, 0, NEG)]
    consts = np.concatenate([np.asarray(c, np.float32) for c in cols], axis=1)
    dist = 255 - np.arange(REL)
    n = np.maximum(dist, 0)
    nf = np.maximum(n, 1).astype(np.float32)
    large = 16 + (np.log(nf / np.float32(16)) / np.float32(np.log(8.0)) * np.float32(16)).astype(np.int32)
    bucket = np.where(n < 16, n, np.minimum(large, 31))
    onehot = (np.arange(32)[:, None] == bucket[None, :]).astype(np.float32)
    times = sum(((n % dil == 0) & (n <= win)).astype(np.int32) for win, dil in ((128, 1), (512, 4), (2048, 16)))
    dil = np.where((dist >= 0) & (times > 0), np.log(np.maximum(times, 1)), NEG)
    full = np.where(dist >= 0, 0.0, NEG)
    relmask = np.broadcast_to(np.stack([full, dil])[None], (HEADS, 2, REL)).astype(np.float32)
    return consts, onehot, np.ascontiguousarray(relmask)


def lay_out(x, t5_bias, ab_w_in, ab_lambda, ab_subln_g, ab_w_out, cd_w_in, cd_b_f, cd_w_out,
            peer_w_q, peer_sub_keys, peer_u, peer_v, ln_g, ln_b):
    a = {k: np.asarray(v) for k, v in dict(
        x=x, t5=t5_bias, ab_in=ab_w_in, lam=ab_lambda, sub=ab_subln_g, ab_out=ab_w_out, cd_in=cd_w_in, bf=cd_b_f,
        cd_out=cd_w_out, wq=peer_w_q, keys=peer_sub_keys, u=peer_u, v=peer_v, g=ln_g, b=ln_b).items()}

    def tiles(w):
        return w.reshape(DC, P, -1, P).transpose(2, 1, 0, 3).reshape(-1, P, D)

    stream = []
    for L, (w_in, w_out) in enumerate(((a["ab_in"][0], a["ab_out"][0]), (a["cd_in"][0], a["cd_out"][0]))):
        t = tiles(w_in[:, :IN_ITEMS * P])
        stream += [t[0:12], t[20:24], t[12:20], tiles(w_out), tiles(a["wq"][L])]
        u = a["u"][L].reshape(P, NKEYS, DC, P).transpose(1, 3, 2, 0).reshape(NKEYS, P, D)
        stream.append(u)
    consts, onehot, relmask = tables()
    return {
        "x": a["x"][0],
        "u_stream": np.concatenate(stream),
        "v_stream": np.ascontiguousarray(a["v"].reshape(LAYERS, P, NKEYS, D).transpose(0, 2, 1, 3).reshape(-1, P, D)),
        "keys": np.ascontiguousarray(a["keys"].transpose(0, 4, 1, 2, 3).reshape(LAYERS, P, Q_ITEMS, NKEYS)),
        "t5": a["t5"], "onehot": onehot, "relmask": relmask,
        "lam_vecs": a["lam"].reshape(-1), "subln": a["sub"].reshape(-1),
        "w_f": np.ascontiguousarray(a["cd_in"][0][:, IN_ITEMS * P:].reshape(DC, P, HEADS).transpose(1, 0, 2).reshape(P, -1)),
        "b_f": a["bf"].reshape(-1),
        "ln_g": a["g"].reshape(2 * LAYERS, D), "ln_b": a["b"].reshape(2 * LAYERS, D),
        "consts": consts,
    }


def kernel(**inputs):
    import concourse.bacc as bacc
    from concourse.bass_utils import run_bass_kernel_spmd

    arrays = {k: np.ascontiguousarray(v) for k, v in lay_out(**inputs).items()}
    nc = bacc.Bacc("TRN2", target_bir_lowering=False, num_devices=1, dynamic_dma_scratch_size=1024)
    aps = {k: nc.dram_tensor(f"in_{k}", v.shape, mybir.dt.from_np(v.dtype), kind="ExternalInput").ap()
           for k, v in arrays.items()}
    result = nc.dram_tensor("result", (SEQ, D), F32, kind="ExternalOutput").ap()
    build_program(nc, out=result, **aps)
    r = run_bass_kernel_spmd(nc, [{f"in_{k}": v for k, v in arrays.items()}], core_ids=[0])
    return r.results[0]["result"].reshape(1, SEQ, D)
```

```python
from contextlib import ExitStack

import numpy as np

import concourse.bass as bass
from concourse import mybir

F32 = mybir.dt.float32
F32R = mybir.dt.float32r
U32 = mybir.dt.uint32
ALU = mybir.AluOpType
ACT = mybir.ActivationFunctionType
AX = mybir.AxisListType
ds = bass.ds

P = 128
SEQ = 256
TB = SEQ // P
D = 1024
DC = D // P
LAYERS = 2
HEADS = 8
HD = 64
NKEYS = 128
TOPK = 16
EXPERT_ITEMS = NKEYS
IN_ITEMS = 24
OUT_ITEMS = 8
Q_ITEMS = 16
V_FIRST, V_ITEMS = 8, 8
N_OUT = IN_ITEMS
N_Q = N_OUT + OUT_ITEMS
N_U = N_Q + Q_ITEMS
ITEMS = N_U + EXPERT_ITEMS
EVACS = ITEMS - OUT_ITEMS
RAW = 4
AHEAD = 32
LATE = 16
POOL_CHUNKS = 2
T5_AFTER = 2
NZ = 4
REST = EXPERT_ITEMS - AHEAD - LATE
GROUP = 4
GATE_LAG = 3
ALPHA = (2 * LAYERS) ** 0.25
LN_EPS = 1e-5
LAMBDA_INIT = 0.2
NEG = -1.0e30
LOWEST = -3.0e38
REL = 384
W3 = 384

C_KEEP = 2 * P
(C_GE, C_LE, C_NLE, C_ONE, C_NONE, C_STICK, C_PAST, C_CAUSAL) = (
    0, P, 2 * P, 3 * P, 4 * P, 5 * P, 5 * P + W3, 5 * P + 2 * W3)
C_COLS = 5 * P + 3 * W3
SOFT_A, SOFT_C, SOFT_D = 8, 4, 4


def build_program(nc, x, u_stream, v_stream, keys, t5, onehot, relmask, lam_vecs, subln, w_f, b_f,
                  ln_g, ln_b, consts, out):
    scratch = nc.dram_tensor("bias_rows", [LAYERS, HEADS, P, REL], F32, kind="Internal").ap()

    with ExitStack() as ctx:
        def sb(name, shape, dt=F32):
            return ctx.enter_context(nc.sbuf_tensor(name, shape, dt))

        def sem(name):
            return ctx.enter_context(nc.semaphore(name))

        gates = sb("gates", [P, SEQ, NKEYS])
        flat = gates[:, :, :].rearrange("p t j -> p (t j)")
        used = [0]

        def carve(*shape):
            n = int(np.prod(shape))
            a = flat[:, used[0]:used[0] + n]
            used[0] += n
            assert used[0] <= SEQ * NKEYS
            if len(shape) == 2:
                return a.rearrange("p (a b) -> p a b", a=shape[0])
            if len(shape) == 3:
                return a.rearrange("p (a b c) -> p a b c", a=shape[0], b=shape[1])
            return a

        u_raw = sb("u_raw", [P, RAW, DC, P])
        u_hi = sb("u_hi", [P, 2, DC, P], F32R)
        u_lo = sb("u_lo", [P, 2, DC, P], F32R)
        v_hi_at = nc.sbuf_base
        v_hi = sb("v_hi", [P, 2, D], F32R)
        v_lo = sb("v_lo", [P, 2, D], F32R)
        late_at = nc.sbuf_base
        v_raw = sb("v_raw", [P, 2, D])
        w_hi_at = nc.sbuf_base
        w_hi = sb("w_hi", [P, 2, SEQ], F32R)
        w_lo = sb("w_lo", [P, 2, SEQ], F32R)
        gain_at = nc.sbuf_base
        top_s = sb("top_s", [P, TB, 2 * HEADS, TOPK])
        top_i = sb("top_i", [P, TB, 2 * HEADS, TOPK], U32)
        xT_hi = sb("xT_hi", [P, DC, SEQ], F32R)
        xT_lo = sb("xT_lo", [P, DC, SEQ], F32R)
        h = sb("h", [P, TB, D])
        shift_at = nc.sbuf_base
        act = sb("act", [P, 2, SEQ])
        wf_hi, wf_lo = (w_hi[:, b, 0:DC * HEADS].rearrange("p (c k) -> p c k", c=DC) for b in range(2))
        tabT = sb("tabT", [P, 3, SEQ])
        keep = sb("keep", [P, C_KEEP])
        ident, iota = keep[:, 0:P], keep[:, P:2 * P]
        small = sb("small", [P, 64])
        sc = nc.alloc_sbuf_tensor_at("scores", [P, TB, 2 * HEADS * NKEYS], F32, offset=v_hi_at)
        tmp = nc.alloc_sbuf_tensor_at("tmp", [P, 8, P], F32, offset=w_hi_at)
        tmpu = nc.alloc_sbuf_tensor_at("tmpu", [P, 8, P], U32, offset=w_hi_at)
        qrow = tmp[:, 0:4, :].rearrange("p (e t) k -> p e (t k)", e=2)
        onehots = nc.alloc_sbuf_tensor_at("onehots", [P, 4, 2, GROUP, NKEYS], F32, offset=v_hi_at)
        gain = nc.alloc_sbuf_tensor_at("gain", [P, D], F32, offset=gain_at)
        shift = nc.alloc_sbuf_tensor_at("shift", [P, D], F32, offset=shift_at)
        late = nc.alloc_sbuf_tensor_at("late", [P, LATE, SEQ], F32, offset=late_at)
        keysT = v_raw[:, :, :].rearrange("p a (e k) -> p (a e) k", k=NKEYS)

        qkT = carve(16, SEQ)
        vals = carve(TB, 2 * HEADS * HD)
        o = carve(TB, 2 * HEADS * HD)
        bias = carve(HEADS, W3)
        cst = carve(C_COLS)
        logits = [carve(2, W3) for _ in range(2)]
        diffw = [carve(W3) for _ in range(2)]
        probsT = [carve(2, W3) for _ in range(2)]
        z_abs, rem, z_cum, w_stick = ([carve(W3) for _ in range(NZ)] for _ in range(4))
        sq = carve(TB, HEADS * HD)
        wf = carve(DC, HEADS)
        bfr = carve(HEADS)
        subr = carve(HD)
        lv = carve(2, 2, 32)
        lvp = carve(2, 32)
        t5s = carve(HEADS)
        rowc = carve(3, REL)
        rowb = carve(2, REL)
        ssum = [carve(4) for _ in range(2)]
        nmax = [carve(4) for _ in range(2)]
        rsum = [carve(4) for _ in range(2)]
        fneg = [carve(2) for _ in range(2)]
        lam = carve(4)
        rms = carve(2 * HEADS)
        fgx = carve(2, HEADS)
        fga = carve(2, HEADS)
        logf = carve(2, HEADS)
        fcum = carve(2, HEADS)
        tri_ge, tri_le, ntri_le = (cst[:, a:a + P] for a in (C_GE, C_LE, C_NLE))
        ones, nones = cst[:, C_ONE:C_ONE + P], cst[:, C_NONE:C_NONE + P]
        stick_neg, past_mask, causal = (cst[:, a:a + W3] for a in (C_STICK, C_PAST, C_CAUSAL))

        acc = [ctx.enter_context(nc.psum_tensor(f"acc{i}", [P, 512], F32)) for i in range(4)]
        pu = [ctx.enter_context(nc.psum_tensor(f"pu{i}", [P, 512], F32)) for i in range(2)]
        px = [ctx.enter_context(nc.psum_tensor(f"px{i}", [P, 512], F32)) for i in range(2)]

        zbank = [pu[0], pu[1], acc[0], acc[1]]

        s_x = sem("s_x")
        s_load = sem("s_load")
        s_bias = sem("s_bias")
        s_cload = sem("s_cload")
        s_lnload = sem("s_lnload")
        s_keys = sem("s_keys")
        s_rows = sem("s_rows")
        u_in = [sem(f"u_in{i}") for i in range(RAW)]
        v_in = [[sem(f"v_in{f}_{i}") for i in range(2)] for f in range(2)]
        u_hi_ok = [sem(f"u_hi_ok{f}") for f in range(2)]
        u_lo_ok = [sem(f"u_lo_ok{f}") for f in range(2)]
        pair_lo_ok = [sem(f"pair_lo_ok{f}") for f in range(2)]
        u_used = [sem(f"u_used{f}") for f in range(2)]
        evac = sem("evac")
        mixed = sem("mixed")
        v_hi_ok = sem("v_hi_ok")
        v_lo_ok = sem("v_lo_ok")
        v_used = sem("v_used")
        w_hi_ok = sem("w_hi_ok")
        w_ok = sem("w_ok")
        gated = sem("gated")
        rows_ok = sem("rows_ok")
        tr_out = sem("tr_out")
        xT_hi_ok = sem("xT_hi_ok")
        xT_ok = sem("xT_ok")
        s_out = sem("s_out")
        s_read = sem("s_read")
        nmax_ok = sem("nmax_ok")
        exp_ok = sem("exp_ok")
        w_diff_ok = sem("w_diff_ok")
        wT_out = sem("wT_out")
        wT_ok = sem("wT_ok")
        pv_out = sem("pv_out")
        pv_read = sem("pv_read")
        z_out = sem("z_out")
        sp_log_ok = sem("sp_log_ok")
        rem_ok = sem("rem_ok")
        cum_out = sem("cum_out")
        z_cum_ok = sem("z_cum_ok")
        w_stick_ok = sem("w_stick_ok")
        var_ok = sem("var_ok")
        sd_ok = sem("sd_ok")
        t5_out = sem("t5_out")
        rowb_ok = sem("rowb_ok")
        lam_sum = sem("lam_sum")
        lam_exp = sem("lam_exp")
        rms_sum = sem("rms_sum")
        rms_sd = sem("rms_sd")
        wf_hi_ok = sem("wf_hi_ok")
        wf_ok = sem("wf_ok")
        f_out = sem("f_out")
        f_abs = sem("f_abs")
        f_log = sem("f_log")
        logf_ok = sem("logf_ok")
        fcum_out = sem("fcum_out")
        fcum_ok = sem("fcum_ok")
        q_out = sem("q_out")
        sc_ok = sem("sc_ok")
        gsub = sem("gsub")
        gexp = sem("gexp")
        tab_ok = sem("tab_ok")
        tabT_out = sem("tabT_out")
        tabT_ok = sem("tabT_ok")
        eq_ok = sem("eq_ok")
        oh_ok = sem("oh_ok")
        oh_ok_act = sem("oh_ok_act")
        g_out = sem("g_out")
        late_gated = sem("late_gated")
        g_mul = sem("g_mul")
        g_copied = sem("g_copied")
        act_step = sem("act_step")
        dve_step = sem("dve_step")
        stored = sem("stored")

        GROUPS = SEQ // GROUP
        layers = range(LAYERS)
        E_ = EXPERT_ITEMS

        def item(L, n):
            return L * ITEMS + n

        def evacs(L, n):
            return L * EVACS + n + 1 - (OUT_ITEMS if n >= N_Q else 0)

        def pairs_done(L, n):
            return (V_ITEMS + OUT_ITEMS) * L + (n - V_FIRST + 1 if n < N_OUT else V_ITEMS + n - N_OUT + 1)

        def shares(f):
            return slice(4 * f, 4 * f + POOL_CHUNKS), slice(4 * f + POOL_CHUNKS, 4 * f + 4)

        def score_bank(su, m):
            return (acc, pu)[su % 2 if su >= SOFT_A + SOFT_C else 0][m]

        def layer_units(L):
            return (range(0, SOFT_A), 1) if L == 0 else (range(SOFT_A, SOFT_A + SOFT_C + SOFT_D), 2)

        block = ctx.enter_context(nc.Block())

        @block.sync
        def _(sp):
            def load_item(k, i=0):
                if k >= RAW:
                    sp.wait_ge(u_lo_ok[1], k - RAW + 1 + i * RAW)
                    L, n = divmod(k - RAW, ITEMS)
                    if V_FIRST <= n < V_FIRST + V_ITEMS or N_OUT <= n < N_Q:
                        sp.wait_ge(pair_lo_ok[1], pairs_done(L, n))
                src = u_stream[k] if isinstance(i, int) else u_stream[ds(i * RAW + k, 1)].rearrange("o p f -> (o p) f")
                sp.dma_start(u_raw[:, k % RAW].rearrange("p c k -> p (c k)"), src).then_inc(u_in[k % RAW], 16)

            def load_v(j, i=0, step=2):
                src = v_stream[j] if isinstance(i, int) else v_stream[ds(i * step + j, 1)].rearrange("o p f -> (o p) f")
                for f in range(2):
                    if j >= 2:
                        sp.wait_ge(v_lo_ok, (j - 2) * 2 + f + 1 + i * (2 * step))
                    half = slice(f * 512, (f + 1) * 512)
                    sp.dma_start(v_raw[:, j % 2, half], src[:, half]).then_inc(v_in[f][j % 2], 16)

            def load_consts(L):
                sp.dma_start(cst, consts[:, C_KEEP:]).then_inc(s_cload, 16)
                sp.dma_start(wf.rearrange("p c k -> p (c k)"), w_f).then_inc(s_cload, 16)
                sp.dma_start(bfr, b_f.partition_broadcast(P)).then_inc(s_cload, 16)
                sp.dma_start(subr, subln.partition_broadcast(P)).then_inc(s_cload, 16)

            def load_bias(L):
                at = L * HEADS * P * REL + P - 1
                sp.dma_start(bias[:, :, 0:2 * P], bass.AP(scratch.tensor, at, [[REL - 1, P], [P * REL, HEADS], [1, 2 * P]])
                             ).then_inc(s_bias, 16)
                sp.dma_start(bias[:, :, 2 * P:W3], bass.AP(scratch.tensor, at + P, [[REL - 1, P], [P * REL, HEADS], [1, P]])
                             ).then_inc(s_bias, 16)

            def store_rows(L):
                sp.dma_start(scratch[L], rowb[0:HEADS, L, :].unsqueeze(1).to_broadcast([HEADS, P, REL])
                             ).then_inc(s_rows, 16)

            def load_norm(q):
                sp.dma_start(gain[:, :], ln_g[q].partition_broadcast(P)).then_inc(s_lnload, 16)
                sp.dma_start(shift[:, :], ln_b[q].partition_broadcast(P)).then_inc(s_lnload, 16)

            sp.dma_start(h[:, :, :], x.rearrange("(t p) d -> p t d", p=P)).then_inc(s_x, 16)
            sp.dma_start(keep[:, :], consts[:, 0:C_KEEP]).then_inc(s_x, 16)
            for k in range(RAW):
                load_item(k)
            sp.dma_start(t5s[0:32, :], t5).then_inc(s_load, 16)
            sp.dma_start(rowc[0:32, 0, :], onehot).then_inc(s_load, 16)
            sp.dma_start(rowc[0:HEADS, 1:3, :], relmask).then_inc(s_load, 16)
            sp.dma_start(lv.rearrange("p a b c -> p (a b c)"), lam_vecs.partition_broadcast(P)).then_inc(s_load, 16)
            for L in layers:
                if L > 0:
                    sp.wait_ge(w_ok, E_ * L)
                for n in range(RAW, N_OUT):
                    if L == 0 and n == T5_AFTER + RAW + 2:
                        sp.wait_ge(rowb_ok, 1)
                        store_rows(0)
                    if n == V_FIRST + 2:
                        sp.wait_ge(s_rows, 16 * (L + 1))
                        load_bias(L)
                    if n == (V_FIRST + V_ITEMS if L == 0 else V_FIRST + 2):
                        load_consts(L)
                    load_item(item(L, n))
                if L > 0:
                    sp.wait_ge(rows_ok, 4 * 3 * L)
                load_norm(2 * L)
                for n in range(N_OUT, N_OUT + 4):
                    load_item(item(L, n))
                if L == 0:
                    for m in range(1, LAYERS):
                        store_rows(m)
                if L > 0:
                    sp.wait_ge(v_lo_ok, 2 * E_ * L)
                sp.dma_start(keysT, keys[L]).then_inc(s_keys, 16)
                for n in range(N_OUT + 4, N_OUT + 8):
                    load_item(item(L, n))
                first = item(L, N_OUT + 8)
                with sp.Fori(0, (OUT_ITEMS - 8 + Q_ITEMS + AHEAD + LATE + 4) // RAW) as i:
                    for r in range(RAW):
                        load_item(first + r, i)
                for r in range(2):
                    sp.wait_ge(late_gated, LATE * L + 4 * (r + 1))
                    load_v(E_ * L + r)
                first = item(L, N_U + AHEAD + LATE + 4)
                if L + 1 < LAYERS:
                    pairs = REST
                else:
                    pairs = REST - 4
                with sp.Fori(0, pairs // RAW) as i:
                    for r in range(RAW):
                        load_item(first + r, i)
                        load_v(E_ * L + 2 + r, i, RAW)
                for r in range(8):
                    load_v(E_ * L + 2 + pairs + r)
                sp.wait_ge(gated, REST * (L + 1))
                load_norm(2 * L + 1)
                with sp.Fori(0, (E_ - 10 - pairs) // 2) as i:
                    for r in range(2):
                        load_v(E_ * L + 10 + pairs + r, i)
            for g in range(4):
                tb, c = g % 2, slice(g // 2 * 512, (g // 2 + 1) * 512)
                sp.wait_ge(rows_ok, 4 * (3 * LAYERS - 1) + g + 1)
                sp.dma_start(out[tb * P:(tb + 1) * P, c], h[:, tb, c]).then_inc(stored, 16)
            sp.wait_ge(stored, 16 * 4)

        @block.gpsimd
        def _(pool):
            def low(k, f, i=0, paired=False):
                pool.wait_ge(u_hi_ok[f], k + 1 + i * RAW)
                half = shares(f)[0] if paired else slice(f * DC // 2, (f + 1) * DC // 2)
                pool.tensor_tensor(u_lo[:, k % 2, half], u_raw[:, k % RAW, half],
                                   u_hi[:, k % 2, half].bitcast(F32), ALU.subtract).then_inc(u_lo_ok[f], 1)

            def lows(k, n):
                with pool.Fori(0, n // RAW) as i:
                    for r in range(RAW):
                        for f in range(2):
                            low(k + r, f, i)
                for r in range(n // RAW * RAW, n):
                    for f in range(2):
                        low(k + r, f)

            def low_pairs(k, n):
                with pool.Fori(0, n // RAW) as i:
                    for r in range(0, RAW, 2):
                        for f in range(2):
                            low(k + r, f, i, paired=True)
                            low(k + r + 1, f, i, paired=True)

            def weigh_onehots(L, q, i=0):
                pool.wait_ge(eq_ok, GROUPS * L + q + 1 + i * 16)
                tok = ds(i * (16 * GROUP) + q * GROUP, GROUP)
                pool.tensor_tensor(onehots[:, q % 4, 1], onehots[:, q % 4, 1],
                                   tabT[:, 2, tok].unsqueeze(2).to_broadcast([P, GROUP, NKEYS]), ALU.mult
                                   ).then_inc(oh_ok, 1)

            for L in layers:
                lows(item(L, 0), V_FIRST)
                low_pairs(item(L, V_FIRST), V_ITEMS)
                lows(item(L, V_FIRST + V_ITEMS), N_OUT - V_FIRST - V_ITEMS)
                low_pairs(item(L, N_OUT), OUT_ITEMS)
                lows(item(L, N_Q), Q_ITEMS + AHEAD)
                weigh_onehots(L, 0)
                weigh_onehots(L, 1)
                low(item(L, N_U + AHEAD), 0)
                weigh_onehots(L, 2)
                low(item(L, N_U + AHEAD), 1)
                for f in range(2):
                    low(item(L, N_U + AHEAD + 1), f)

                def beside(r, i=0, last=False):
                    k = item(L, N_U + AHEAD + 2 + r)
                    low(k, 0, i)
                    if not last:
                        weigh_onehots(L, 4 * r + 4, i)
                        weigh_onehots(L, 4 * r + 5, i)
                    low(k, 1, i)
                    if not last:
                        weigh_onehots(L, 4 * r + 6, i)

                with pool.Fori(0, LATE // RAW - 1) as i:
                    for r in range(RAW):
                        beside(r, i)
                for r in range(LATE - RAW, LATE):
                    beside(r, last=(r == LATE - 1))
                lows(item(L, N_U + AHEAD + LATE + 2), REST - 2)

        @block.scalar
        def _(a):
            steps = [0]

            def step(ins):
                ins.then_inc(act_step, 1)
                steps[0] += 1
                a.wait_ge(act_step, steps[0])

            def round_item(k, i=0, period=RAW):
                a.wait_ge(u_in[k % RAW], 16 * (k // RAW + 1) + i * (16 * period // RAW))
                for f in range(2):
                    round_half(k, f, i, period)

            def round_half(k, f, i=0, period=RAW):
                if k >= 2:
                    a.wait_ge(u_used[f], k - 1 + i * period)
                half = slice(f * DC // 2, (f + 1) * DC // 2)
                a.activation(u_hi[:, k % 2, half], u_raw[:, k % RAW, half], ACT.Copy).then_inc(u_hi_ok[f], 1)

            def round_pair(k):
                for n in (k, k + 1):
                    a.wait_ge(u_in[n % RAW], 16 * (n // RAW + 1))
                for f in range(2):
                    round_half(k, f)
                    round_half(k + 1, f)

            def round_v(j, i=0, period=2):
                for f in range(2):
                    a.wait_ge(v_in[f][j % 2], 16 * (j // 2 + 1) + i * (16 * period // 2))
                    if j >= 2:
                        a.wait_ge(v_used, 2 * (j - 2) + f + 1 + i * (2 * period))
                    half = slice(f * 512, (f + 1) * 512)
                    a.activation(v_hi[:, j % 2, half], v_raw[:, j % 2, half], ACT.Copy).then_inc(v_hi_ok, 1)

            def next_item(k):
                if k + 2 < LAYERS * ITEMS:
                    round_item(k + 2)

            def split_rows(s):
                for g in range(4):
                    half, tb = g // 2, g % 2
                    a.wait_ge(tr_out, 4 * s + g + 1)
                    a.activation(xT_hi[:, 4 * half:4 * half + 4, tb * P:(tb + 1) * P],
                                 px[g % 2][:, :].rearrange("p (c t) -> p c t", c=4), ACT.Copy).then_inc(xT_hi_ok, 1)

            def norm_sd(q):
                a.wait_ge(var_ok, q + 1)
                a.activation(small[:, 16:18], small[:, 14:16], ACT.Sqrt).then_inc(sd_ok, 1)

            def take_in(L, n):
                a.wait_ge(u_used[1], item(L, n) + 1)
                tile = n if n < V_FIRST else n - V_ITEMS
                query = n < 4 or 16 <= n < 20
                scale = HD ** -0.5 if query and not (L == 0 and n < 4) else 1.0
                a.activation(qkT[:, tile, :], pu[n % 2][:, 0:SEQ], ACT.Copy, scale=scale).then_inc(evac, 1)

            def take_values(L, n):
                a.wait_ge(u_used[1], item(L, n) + 2)
                m = n - V_FIRST
                for tb in range(TB):
                    ins = a.activation(vals[:, tb, m * P:(m + 2) * P], acc[m % 4 + tb][:, 0:2 * P], ACT.Copy)
                ins.then_inc(evac, 2)

            def exps(su):
                b = su % 2
                a.wait_ge(nmax_ok, su + 1)
                for m in range(2):
                    a.activation(logits[b][:, m, 0:2 * P], logits[b][:, m, 0:2 * P], ACT.Exp,
                                 bias=nmax[b][:, m:m + 1], accum_out=ssum[b][:, 2 * m + 1:2 * m + 2])
                    ins = a.activation(logits[b][:, m, 2 * P:W3], logits[b][:, m, 2 * P:W3], ACT.Exp,
                                       bias=nmax[b][:, 2 + m:3 + m], accum_out=ssum[b][:, 2 * m:2 * m + 1])
                ins.then_inc(exp_ok, 1)

            def take_T(su):
                b = su % 2
                if su < SOFT_A:
                    a.wait_ge(wT_out, su + 1)
                    a.activation(probsT[b][:, 0, :], px[b][:, 0:W3], ACT.Copy).then_inc(wT_ok, 1)
                else:
                    for m in range(2):
                        n = SOFT_A + 2 * (su - SOFT_A) + m + 1
                        a.wait_ge(wT_out, n)
                        a.activation(probsT[b][:, m, :], px[m][:, 0:W3], ACT.Copy).then_inc(wT_ok, 1)

            a.preload_act_table_set("natural_log_exp_and_others")
            for L in layers:
                if L == 0:
                    round_item(0)
                    round_item(1)
                split_rows(3 * L)
                n0 = V_FIRST + V_ITEMS
                for n in range(V_FIRST):
                    next_item(item(L, n))
                    take_in(L, n)
                    if L == 0 and n == T5_AFTER:
                        a.wait_ge(lam_sum, 1)
                        a.activation(lam[:, 2:4], lam[:, 0:2], ACT.Exp).then_inc(lam_exp, 1)
                for n in range(V_FIRST, n0, 2):
                    round_pair(item(L, n + 2))
                    take_values(L, n)
                if L == 1:
                    a.preload_act_table_set("natural_log_exp_and_others")
                    a.wait_ge(f_abs, 1)
                    step(a.activation(fga, fga, ACT.Exp))
                    a.activation(fga, fga, ACT.Ln, bias=1.0).then_inc(f_log, 1)
                units, per = layer_units(L)
                for i in range(len(units) + 1):
                    if i < len(units):
                        first = n0 + per * i
                        for n in range(first, min(first + per, N_OUT)):
                            next_item(item(L, n))
                            take_in(L, n)
                            if n == first:
                                exps(units[i])
                        if first >= N_OUT:
                            exps(units[i])
                    if i > 0:
                        take_T(units[i - 1])
                if L == 0:
                    for i in range(HEADS + 3):
                        if i < HEADS:
                            b = i % NZ
                            a.wait_ge(z_out, i + 1)
                            if i >= NZ:
                                a.wait_ge(rem_ok, i - NZ + 1)
                            a.activation(z_abs[b], zbank[b][:, 0:W3], ACT.Abs).then_inc(act_step, 1)
                            steps[0] += 1
                        if i == 4:
                            a.wait_ge(rms_sum, 1)
                            a.activation(rms, rms, ACT.Sqrt).then_inc(rms_sd, 1)
                            a.preload_act_table_set("natural_log_exp_and_others")
                        m = i - 3
                        if m >= 0:
                            a.wait_ge(z_cum_ok, m + 1)
                            if m >= NZ:
                                a.wait_ge(pv_out, SOFT_A + m - NZ + 1)
                            a.activation(w_stick[m % NZ], z_cum[m % NZ], ACT.Exp).then_inc(w_stick_ok, 1)
                        if i < HEADS:
                            a.wait_ge(act_step, steps[0])
                            step(a.activation(z_abs[b], z_abs[b], ACT.Exp, scale=-1.0))
                            a.activation(z_abs[b], z_abs[b], ACT.Ln, bias=1.0).then_inc(sp_log_ok, 1)
                split_rows(3 * L + 1)
                a.preload_act_table(ACT.Sqrt)
                for n in range(N_OUT, N_Q, 2):
                    round_pair(item(L, n + 2))
                norm_sd(2 * L)
                split_rows(3 * L + 2)
                for e in range(Q_ITEMS + 1):
                    if e < Q_ITEMS:
                        k = item(L, N_Q + e)
                        next_item(k)
                        a.wait_ge(u_used[1], k + 1)
                        if e >= 2:
                            a.wait_ge(q_out, Q_ITEMS * L + e - 1)
                        a.activation(qrow[:, e % 2, :], pu[e % 2][:, 0:SEQ], ACT.Copy).then_inc(evac, 1)
                    if e > 0 and e % 4 == 0:
                        a.wait_ge(q_out, Q_ITEMS * L + e)
                        for tb in range(TB):
                            a.activation(sc[:, tb, (e - 4) * P:e * P], px[tb][:, :], ACT.Copy).then_inc(sc_ok, 1)
                a.wait_ge(s_rows, 16 * LAYERS)
                def ahead(r, i=0):
                    k = item(L, N_U + r)
                    round_item(k + 2, i)
                    a.wait_ge(u_used[1], k + 1 + i * RAW)
                    a.activation(gates[:, :, ds(i * RAW + r, 1)].rearrange("p t o -> p (t o)"),
                                 pu[r % 2][:, 0:SEQ], ACT.Gelu).then_inc(evac, 1)

                a.preload_act_table(ACT.Gelu)
                with a.Fori(0, AHEAD // RAW - 1) as i:
                    for r in range(RAW):
                        ahead(r, i)
                for tb in range(TB):
                    a.wait_ge(gsub, TB * L + tb + 1)
                    a.activation(top_s[:, tb, 0:8, :], top_s[:, tb, 0:8, :], ACT.Exp).then_inc(gexp, 1)
                ahead(AHEAD - 4)
                ahead(AHEAD - 3)
                for tb in range(TB):
                    a.wait_ge(tabT_out, TB * L + tb + 1)
                    a.activation(tabT[:, :, tb * P:(tb + 1) * P],
                                 px[tb][:, 0:3 * P].rearrange("p (a t) -> p a t", a=3), ACT.Copy).then_inc(tabT_ok, 1)
                ahead(AHEAD - 2)
                ahead(AHEAD - 1)

                def copy_gates(q, i):
                    a.wait_ge(g_mul, GROUPS * L + q + 1 + i * 16)
                    a.activation(gates[:, ds(i * (16 * GROUP) + q * GROUP, GROUP), AHEAD:NKEYS],
                                 acc[q % 4][:, :].rearrange("p (t j) -> p t j", t=GROUP)[:, :, AHEAD:NKEYS],
                                 ACT.Copy).then_inc(g_copied, 1)

                def weigh_onehots(q, i):
                    a.wait_ge(eq_ok, GROUPS * L + q + 1 + i * 16)
                    for t in range(GROUP):
                        row = onehots[:, q % 4, 1, t]
                        tok = ds(i * (16 * GROUP) + q * GROUP + t, 1)
                        ins = a.activation(row, row, ACT.Copy, scale=tabT[:, 2, tok])
                    ins.then_inc(oh_ok_act, 1)

                a.preload_act_table(ACT.Gelu)
                with a.Fori(0, LATE // RAW) as i:
                    for r in range(RAW):
                        k = item(L, N_U + AHEAD + r)
                        copy_gates(4 * r, i)
                        weigh_onehots(4 * r + 3, i)
                        copy_gates(4 * r + 1, i)
                        a.wait_ge(u_in[(k + 2) % RAW], 16 * ((k + 2) // RAW + 1) + i * 16)
                        round_half(k + 2, 0, i)
                        copy_gates(4 * r + 2, i)
                        copy_gates(4 * r + 3, i)
                        round_half(k + 2, 1, i)
                        a.wait_ge(u_used[1], k + 1 + i * RAW)
                        a.activation(late[:, ds(i * RAW + r, 1)].rearrange("p o t -> p (o t)"),
                                     pu[r % 2][:, 0:SEQ], ACT.Gelu).then_inc(evac, 1)

                def both(i, s, last=False):
                    k = item(L, N_U + AHEAD + LATE + s)
                    if s >= 2:
                        round_v(E_ * L + s, i, RAW)
                    if not last:
                        round_item(k + 2, i)
                    a.wait_ge(u_used[1], k + 1 + i * RAW)
                    if L > 0 or s >= 2:
                        a.wait_ge(gated, REST * L + s - 1 + i * RAW)
                    a.activation(act[:, s % 2, :], pu[s % 2][:, 0:SEQ], ACT.Gelu).then_inc(evac, 1)
                    if s < 2:
                        round_v(E_ * L + s)

                n = REST
                for r in range(RAW):
                    both(0, r)
                with a.Fori(0, n // RAW - 2) as i:
                    for r in range(RAW):
                        both(i, RAW + r)
                for r in range(RAW):
                    both(0, n - RAW + r, last=(L == LAYERS - 1 and r >= 2))
                a.preload_act_table(ACT.Sqrt)
                with a.Fori(0, (E_ - n) // 2) as i:
                    for r in range(2):
                        round_v(E_ * L + n + r, i)
                norm_sd(2 * L + 1)

        @block.vector
        def _(v):
            steps = [0]

            def mark(ins):
                ins.then_inc(dve_step, 1)
                steps[0] += 1
                return steps[0]

            def after(n):
                v.wait_ge(dve_step, n)

            def step(ins):
                after(mark(ins))

            def split_group(s, g):
                half, tb = g // 2, g % 2
                v.wait_ge(xT_hi_ok, 4 * s + g + 1)
                part = (slice(None), slice(4 * half, 4 * half + 4), slice(tb * P, (tb + 1) * P))
                v.tensor_tensor(xT_lo[part], px[g % 2][:, :].rearrange("p (c t) -> p c t", c=4),
                                xT_hi[part].bitcast(F32), ALU.subtract).then_inc(xT_ok, 1)

            def split_rows(s):
                for g in range(4):
                    split_group(s, g)

            def low_pair(L, n):
                for f in range(2):
                    for k in (item(L, n), item(L, n + 1)):
                        v.wait_ge(u_hi_ok[f], k + 1)
                        part = shares(f)[1]
                        v.tensor_tensor(u_lo[:, k % 2, part], u_raw[:, k % RAW, part],
                                        u_hi[:, k % 2, part].bitcast(F32), ALU.subtract).then_inc(pair_lo_ok[f], 1)

            def half_stats(f):
                for tb in range(TB):
                    at = 40 + 12 * tb + 6 * f
                    n = mark(v.bn_stats(small[:, at:at + 6], h[:, tb, 512 * f:512 * f + 512]))
                return n

            def norm(q, stats_done):
                after(stats_done)
                for tb in range(TB):
                    n = mark(v.bn_aggr(small[:, 36 + 2 * tb:38 + 2 * tb],
                                       small[:, 40 + 12 * tb:52 + 12 * tb].rearrange("p (a b) -> p a b", a=2)))
                after(n)
                mv = small[:, 36:40].rearrange("p (t m) -> p t m", t=TB)
                v.tensor_scalar(small[:, 14:16].unsqueeze(2), mv[:, :, 1:2], LN_EPS, None, ALU.add).then_inc(var_ok, 1)
                v.wait_ge(s_lnload, 32 * (q + 1))
                v.wait_ge(sd_ok, q + 1)
                step(v.reciprocal(small[:, 18:20], small[:, 16:18]))
                groups = [(slice(512 * (g // 2), 512 * (g // 2) + 512), g % 2) for g in range(4)]
                s = 3 * (q // 2) + 2 + q % 2
                last = s == 3 * LAYERS

                def centred(g):
                    c, tb = groups[g]
                    return mark(v.scalar_tensor_tensor(h[:, tb, c], h[:, tb, c], mv[:, tb, 0:1], gain[:, c],
                                                       ALU.subtract, ALU.mult))

                def scaled(g, n):
                    c, tb = groups[g]
                    after(n)
                    v.scalar_tensor_tensor(h[:, tb, c], h[:, tb, c], small[:, 18 + tb:19 + tb], shift[:, c],
                                           ALU.mult, ALU.add).then_inc(rows_ok, 1)

                n = [centred(0), centred(1)]
                scaled(0, n[0])
                scaled(1, n[1])
                n += [centred(2), centred(3)]
                for g in (2, 3):
                    if not last:
                        split_group(s, g - 2)
                    scaled(g, n[g])
                v.wait_ge(rows_ok, 4 * s)
                if not last:
                    split_group(s, 2)
                    split_group(s, 3)

            def maps(su):
                b = su % 2
                v.wait_ge(s_out, su + 1)
                if su >= 2:
                    v.wait_ge(wT_out, su - 1 if su - 2 < SOFT_A else SOFT_A + 2 * (su - 1 - SOFT_A))
                for m in range(2):
                    S = score_bank(su, m)[:, 0:W3]
                    if su < SOFT_A:
                        ins = v.scalar_tensor_tensor(logits[b][:, m, :], S, 32.0 ** -0.5, bias[:, su, :],
                                                     ALU.mult, ALU.add)
                    elif su < SOFT_A + SOFT_C:
                        ins = v.tensor_tensor(logits[b][:, m, :], S, bias[:, 2 * (su - SOFT_A) + m, :], ALU.add)
                    else:
                        hh = 2 * (su - SOFT_A - SOFT_C) + m
                        v.scalar_tensor_tensor(logits[b][:, m, 0:2 * P], S[:, 0:2 * P], fcum[:, 1, hh:hh + 1],
                                               causal[:, 0:2 * P], ALU.add, ALU.add)
                        ins = v.scalar_tensor_tensor(logits[b][:, m, 2 * P:W3], S[:, 2 * P:W3],
                                                     fcum[:, 0, hh:hh + 1], causal[:, 2 * P:W3], ALU.add, ALU.add)
                ins.then_inc(s_read, 1)
                v.wait_ge(s_read, su + 1)
                v.tensor_reduce(nmax[b][:, 0:2], logits[b][:, :, 0:2 * P], AX.X, ALU.max, negate=True)
                v.tensor_reduce(nmax[b][:, 2:4], logits[b][:, :, 2 * P:W3], AX.X, ALU.max, negate=True
                                ).then_inc(nmax_ok, 1)

            def weights(su):
                b = su % 2
                v.wait_ge(exp_ok, su + 1)
                if su >= 2:
                    v.wait_ge(pv_read, PV[su - 2])
                step(v.reciprocal(rsum[b], ssum[b]))
                if su < SOFT_A:
                    step(v.scalar_tensor_tensor(fneg[b], ssum[b][:, 0:2], lam[:, 0:1], rsum[b][:, 2:4],
                                                ALU.mult, ALU.mult))
                    v.scalar_tensor_tensor(diffw[b][:, 0:2 * P], logits[b][:, 1, 0:2 * P], fneg[b][:, 1:2],
                                           logits[b][:, 0, 0:2 * P], ALU.mult, ALU.add)
                    v.scalar_tensor_tensor(diffw[b][:, 2 * P:W3], logits[b][:, 1, 2 * P:W3], fneg[b][:, 0:1],
                                           logits[b][:, 0, 2 * P:W3], ALU.mult, ALU.add).then_inc(w_diff_ok, 1)

            def outputs(su):
                b = su % 2
                v.wait_ge(pv_out, PV[su])
                if su < SOFT_A:
                    res = acc[2 + b][:, 0:2 * HD].rearrange("p (t d) -> p t d", t=2)
                    v.tensor_tensor(o[:, :, su * HD:(su + 1) * HD], res,
                                    rsum[b][:, 0:2].unsqueeze(2).to_broadcast([P, 2, HD]), ALU.mult).then_inc(pv_read, 1)
                else:
                    c = (su - SOFT_A) * 2 * HD
                    for m in range(2):
                        res = acc[2 + b][:, m * 2 * HD:(m + 1) * 2 * HD].rearrange("p (t d) -> p t d", t=2)
                        ins = v.tensor_tensor(o[:, :, c + m * HD:c + (m + 1) * HD], res,
                                              rsum[b][:, 2 * m:2 * m + 2].unsqueeze(2).to_broadcast([P, 2, HD]), ALU.mult)
                    ins.then_inc(pv_read, 1)

            PV = [su + 1 if su < SOFT_A else su + 1 + HEADS for su in range(SOFT_A + SOFT_C + SOFT_D)]

            def topk_first(L):
                for grp in range(4):
                    for tb in range(TB):
                        v.wait_ge(sc_ok, 2 * 4 * L + 2 * grp + tb + 1)
                        es = range(4 * grp, 4 * grp + 4)
                        row = {e: sc[:, tb, e * P:(e + 1) * P] for e in es}
                        best = lambda e, f: top_s[:, tb, e, 8 * f:8 * f + 8]
                        n = {e: mark(v.max(best(e, 0), row[e])) for e in es}
                        for f in range(2):
                            for e in es:
                                after(n[e])
                                n[e] = mark(v.max_index(top_i[:, tb, e, 8 * f:8 * f + 8], best(e, f), row[e]))
                            if f == 0:
                                for e in es:
                                    after(n[e])
                                    n[e] = mark(v.match_replace(row[e], best(e, 0), row[e], LOWEST))
                                for e in es:
                                    after(n[e])
                                    n[e] = mark(v.max(best(e, 1), row[e]))
                after(steps[0])

            def topk_second(L, tb):
                cand = sc[:, tb, :].rearrange("p (h a b) -> p h a b", h=HEADS, a=TOPK)
                ts = top_s[:, tb].rearrange("p (h c) k -> p h c k", c=2)
                step(v.tensor_tensor(cand, ts[:, :, 0, :].unsqueeze(3).to_broadcast([P, HEADS, TOPK, TOPK]),
                                     ts[:, :, 1, :].unsqueeze(2).to_broadcast([P, HEADS, TOPK, TOPK]), ALU.add))
                bests = top_s[:, tb, 0:8, :]
                pos = tmpu[:, 0, :].rearrange("p (h k) -> p h k", h=HEADS)
                for g in range(2):
                    hs = range(4 * g, 4 * g + 4)
                    row = {q: sc[:, tb, q * 2 * P:(q + 1) * 2 * P] for q in hs}
                    best = lambda q, f: bests[:, q, 8 * f:8 * f + 8]
                    n = {q: mark(v.max(best(q, 0), row[q])) for q in hs}
                    for f in range(2):
                        for q in hs:
                            after(n[q])
                            n[q] = mark(v.max_index(pos[:, q, 8 * f:8 * f + 8], best(q, f), row[q]))
                        if f == 0:
                            for q in hs:
                                after(n[q])
                                n[q] = mark(v.match_replace(row[q], best(q, 0), row[q], LOWEST))
                            for q in hs:
                                after(n[q])
                                n[q] = mark(v.max(best(q, 1), row[q]))
                after(steps[0])
                v.tensor_single_scalar(tmpu[:, 1, :], tmpu[:, 0, :], 4, ALU.logical_shift_right)
                step(v.tensor_single_scalar(tmpu[:, 2, :], tmpu[:, 0, :], TOPK - 1, ALU.bitwise_and))
                v.tensor_copy(tmp[:, 3, :], tmpu[:, 1, :])
                step(v.tensor_copy(tmp[:, 4, :], tmpu[:, 2, :]))
                work = sc[:, tb, :].rearrange("p (s a) -> p s a", a=TOPK)
                work4 = sc[:, tb, :].rearrange("p (h k a) -> p h k a", h=HEADS, k=TOPK)
                ti = top_i[:, tb].rearrange("p (h c) k -> p h c k", c=2)
                for side in range(2):
                    step(v.tensor_tensor(work, tmp[:, 3 + side, :].unsqueeze(2).to_broadcast([P, P, TOPK]),
                                         iota[:, 0:TOPK].unsqueeze(1).to_broadcast([P, P, TOPK]), ALU.is_equal))
                    step(v.tensor_tensor(work4, work4,
                                         ti[:, :, side, :].unsqueeze(2).to_broadcast([P, HEADS, TOPK, TOPK]), ALU.mult))
                    step(v.tensor_reduce(tmp[:, 5 + side, :], work, AX.X, ALU.add))
                sub = sc[:, tb, 0:P].rearrange("p (h k) -> p h k", h=HEADS)
                step(v.tensor_tensor(sub, bests, bests[:, :, 0:1].to_broadcast([P, HEADS, TOPK]), ALU.subtract))
                v.tensor_copy(bests, sub).then_inc(gsub, 1)
                dst = sc[:, tb, P:3 * P].rearrange("p (a s) -> p a s", a=2)
                step(v.tensor_copy(dst, tmp[:, 5:7, :]))

            def gate_weights(L, tb):
                bests = top_s[:, tb, 0:8, :]
                v.wait_ge(gexp, TB * L + tb + 1)
                step(v.tensor_reduce(small[:, 20:28], bests, AX.X, ALU.add))
                step(v.reciprocal(small[:, 28:36], small[:, 20:28]))
                v.tensor_tensor(sc[:, tb, 3 * P:4 * P].rearrange("p (h k) -> p h k", h=HEADS), bests,
                                small[:, 28:36].unsqueeze(2).to_broadcast([P, HEADS, TOPK]), ALU.mult).then_inc(tab_ok, 1)

            def onehot_group(L, q, i=0):
                if q >= 4 or not isinstance(i, int):
                    v.wait_ge(g_out, GROUPS * L + q - 3 + i * 4)
                tok = ds(i * (4 * GROUP) + q * GROUP, GROUP)
                shape = [P, GROUP, NKEYS]
                for side in (0, 1):
                    ins = v.tensor_tensor(onehots[:, q % 4, side], iota.unsqueeze(1).to_broadcast(shape),
                                          tabT[:, side, tok].unsqueeze(2).to_broadcast(shape), ALU.is_equal)
                ins.then_inc(eq_ok, 1)

            def gate_group(L, q, i=0):
                v.wait_ge(g_out, GROUPS * L + q + 1 + i * 4)
                g = gates[:, ds(i * (4 * GROUP) + q * GROUP, GROUP), 0:AHEAD]
                v.tensor_tensor(g, g, acc[q % 4][:, :].rearrange("p (t j) -> p t j", t=GROUP)[:, :, 0:AHEAD],
                                ALU.mult).then_inc(g_mul, 1)

            for L in layers:
                if L == 0:
                    split_rows(0)
                    v.wait_ge(s_load, 16 * 4)
                    step(v.tensor_tensor(lvp, lv[:, :, 0, :], lv[:, :, 1, :], ALU.mult))
                    v.tensor_reduce(lam[:, 0:2], lvp, AX.X, ALU.add).then_inc(lam_sum, 1)
                    v.wait_ge(t5_out, 1)
                    for m in layers:
                        ins = v.tensor_tensor(rowb[0:HEADS, m], px[0][0:HEADS, 0:REL], rowc[0:HEADS, 1 + m], ALU.add)
                    ins.then_inc(rowb_ok, 1)
                    v.wait_ge(lam_exp, 1)
                    step(v.scalar_tensor_tensor(lam[:, 0:1], lam[:, 3:4], LAMBDA_INIT, lam[:, 2:3], ALU.subtract, ALU.subtract))
                for n in range(V_FIRST, V_FIRST + V_ITEMS, 2):
                    low_pair(L, n)
                v.wait_ge(s_bias, 32 * (L + 1))
                if L > 0:
                    v.wait_ge(s_cload, 64 * (L + 1))
                if L == 1:
                    v.tensor_copy(wf_hi, wf).then_inc(wf_hi_ok, 1)
                    v.wait_ge(wf_hi_ok, 1)
                    v.tensor_tensor(wf_lo, wf, wf_hi.bitcast(F32), ALU.subtract).then_inc(wf_ok, 1)
                    v.wait_ge(f_out, 1)
                    step(v.tensor_tensor(fgx, px[0][:, 0:2 * HEADS].rearrange("p (t h) -> p t h", t=2),
                                         bfr.unsqueeze(1).to_broadcast([P, 2, HEADS]), ALU.add))
                    v.scalar_tensor_tensor(fga, fgx, -1.0, fgx, ALU.mult, ALU.min).then_inc(f_abs, 1)
                    v.wait_ge(f_log, 1)
                    v.scalar_tensor_tensor(logf, fgx, 0.0, fga, ALU.min, ALU.subtract).then_inc(logf_ok, 1)
                units, _ = layer_units(L)
                for i in range(len(units) + 2):
                    if 1 <= i <= len(units):
                        weights(units[i - 1])
                    if L == 1 and i == SOFT_C + 1:
                        low_pair(L, N_OUT)
                    if L == 1 and i == SOFT_C:
                        v.wait_ge(fcum_out, 1)
                        v.tensor_copy(fcum, pu[0][:, 0:2 * HEADS].rearrange("p (t h) -> p t h", t=2)).then_inc(fcum_ok, 1)
                        v.wait_ge(fcum_ok, 1)
                    if i < len(units):
                        maps(units[i])
                    if i >= 2:
                        outputs(units[i - 2])
                if L == 0:
                    v.wait_ge(s_cload, 64)
                    oa = o[:, :, 0:HEADS * HD]
                    heads = lambda t: t.rearrange("p t (h d) -> p t h d", d=HD)
                    rv = rms.rearrange("p (t h) -> p t h", t=2)

                    def mean_squares():
                        v.wait_ge(pv_read, SOFT_A)
                        step(v.tensor_tensor(sq, oa, oa, ALU.mult))
                        step(v.tensor_reduce(rv, heads(sq), AX.X, ALU.add))
                        v.tensor_scalar(rms, rms, 1.0 / HD, LN_EPS, ALU.mult, ALU.add).then_inc(rms_sum, 1)
                        mark(v.tensor_scalar(subr, subr, 1.0 - LAMBDA_INIT, None, ALU.mult))

                    def rms_scaled(t):
                        if t == 0:
                            v.wait_ge(rms_sd, 1)
                            step(v.reciprocal(rms, rms))
                        step(v.tensor_tensor(heads(oa)[:, t], heads(oa)[:, t],
                                             rv[:, t].unsqueeze(2).to_broadcast([P, HEADS, HD]), ALU.mult))
                        return mark(v.tensor_tensor(heads(oa)[:, t], heads(oa)[:, t],
                                                    subr.unsqueeze(1).to_broadcast([P, HEADS, HD]), ALU.mult))

                    for i in range(HEADS + 4):
                        if i < HEADS:
                            b = i % NZ
                            z = zbank[b][:, 0:W3]
                            v.wait_ge(sp_log_ok, i + 1)
                            if i >= NZ:
                                v.wait_ge(cum_out, i - NZ + 1)
                            step(v.scalar_tensor_tensor(z_abs[b], z, 0.0, z_abs[b], ALU.max, ALU.add))
                            v.tensor_tensor(rem[b], z_abs[b], stick_neg, ALU.mult).then_inc(rem_ok, 1)
                        if i == 1:
                            mean_squares()
                        if i == 3:
                            low_pair(L, N_OUT)
                        if i in (6, 7):
                            n = rms_scaled(i - 6)
                        m = i - 1
                        if 0 <= m < HEADS:
                            v.wait_ge(cum_out, m + 1)
                            if m >= NZ:
                                v.wait_ge(w_stick_ok, m - NZ + 1)
                            v.tensor_tensor(z_cum[m % NZ], zbank[m % NZ][:, 0:W3], past_mask, ALU.add).then_inc(z_cum_ok, 1)
                        m = i - 4
                        if m >= 0:
                            v.wait_ge(pv_out, SOFT_A + m + 1)
                            c = HEADS * HD + m * HD
                            v.tensor_copy(o[:, :, c:c + HD], acc[2 + m % 2][:, 0:2 * HD].rearrange("p (t d) -> p t d", t=2)
                                          ).then_inc(pv_read, 1)
                    v.wait_ge(pv_read, 2 * HEADS)
                    after(n)
                else:
                    v.wait_ge(pv_read, 2 * HEADS + SOFT_C + SOFT_D)
                v.engine_nop().then_inc(rows_ok, 4)
                split_rows(3 * L + 1)
                for n in range(0, OUT_ITEMS, 2):
                    if n + 2 < OUT_ITEMS:
                        low_pair(L, N_OUT + n + 2)
                    v.wait_ge(u_used[1], item(L, N_OUT + n) + 2)
                    for tb in range(TB):
                        part = h[:, tb, n * P:(n + 2) * P]
                        ins = v.scalar_tensor_tensor(part, part, ALPHA, acc[n % 4 + tb][:, 0:2 * P], ALU.mult, ALU.add)
                    ins.then_inc(mixed, 2)
                    if n % 4 == 2:
                        v.wait_ge(mixed, OUT_ITEMS * L + n + 2)
                        stats_done = half_stats(n // 4)
                norm(2 * L, stats_done)

                topk_first(L)
                for tb in range(TB):
                    topk_second(L, tb)
                for tb in range(TB):
                    gate_weights(L, tb)
                v.wait_ge(tabT_ok, TB * (L + 1))
                for q in range(GATE_LAG):
                    onehot_group(L, q)
                v.wait_ge(evac, evacs(L, N_U + AHEAD - 1))
                for q in range(4):
                    onehot_group(L, q + GATE_LAG)
                    gate_group(L, q)
                with v.Fori(1, GROUPS // 4 - 1) as i:
                    for q in range(4):
                        onehot_group(L, q + GATE_LAG, i)
                        gate_group(L, q, i)
                for q in range(GROUPS - 4, GROUPS):
                    if q + GATE_LAG < GROUPS:
                        onehot_group(L, q + GATE_LAG)
                    gate_group(L, q)
                v.wait_ge(g_mul, GROUPS * (L + 1))
                v.wait_ge(g_copied, GROUPS * (L + 1))

                def low_v_half(r, f, i=0, period=2):
                    j = E_ * L + r
                    v.wait_ge(v_hi_ok, 2 * j + f + 1 + i * (2 * period))
                    half = slice(f * 512, (f + 1) * 512)
                    v.tensor_tensor(v_lo[:, j % 2, half], v_raw[:, j % 2, half], v_hi[:, j % 2, half].bitcast(F32),
                                    ALU.subtract).then_inc(v_lo_ok, 1)

                def split_w(r, i=0, period=2):
                    j = E_ * L + r
                    if j >= 2:
                        v.wait_ge(v_used, 2 * (j - 2) + 2 + i * (2 * period))
                    col = gates[:, :, ds(i * period + r, 1)].rearrange("p t o -> p (t o)")
                    v.tensor_copy(w_hi[:, j % 2], col).then_inc(w_hi_ok, 1)
                    v.wait_ge(w_hi_ok, j + 1 + i * period)
                    v.tensor_tensor(w_lo[:, j % 2], col, w_hi[:, j % 2].bitcast(F32), ALU.subtract).then_inc(w_ok, 1)

                def gate_item(r, i=0):
                    v.wait_ge(evac, evacs(L, N_U + AHEAD + LATE + r) + i * RAW)
                    col = gates[:, :, ds(i * RAW + AHEAD + LATE + r, 1)].rearrange("p t o -> p (t o)")
                    v.tensor_tensor(col, col, act[:, r % 2], ALU.mult).then_inc(gated, 1)

                v.wait_ge(evac, evacs(L, N_U + AHEAD + LATE - 1))
                n = REST
                lead = 12

                def gate_late(first, end):
                    for m in range(first, end):
                        col = gates[:, :, AHEAD + m]
                        v.tensor_tensor(col, col, late[:, m], ALU.mult).then_inc(late_gated, 1)
                    v.wait_ge(late_gated, LATE * L + end)

                assert AHEAD >= 2 * RAW

                def main_step(s, i=0):
                    split_w(s, i, RAW)
                    low_v_half(s, 0, i, RAW)
                    low_v_half(s, 1, i, RAW)
                    gate_item(s, i)

                gate_late(0, lead)
                main_step(0)
                gate_late(lead, LATE)
                for s in range(1, RAW):
                    main_step(s)
                with v.Fori(0, n // RAW - 1) as i:
                    v.wait_ge(gated, n * L + RAW + i * RAW)
                    for s in range(RAW, 2 * RAW):
                        main_step(s, i)
                v.wait_ge(gated, n * (L + 1))
                with v.Fori(0, (E_ - n) // 2) as i:
                    for r in range(2):
                        low_v_half(n + r, 0, i)
                        split_w(n + r, i)
                        low_v_half(n + r, 1, i)
                for f in range(2):
                    v.wait_ge(v_used, 2 * E_ * (L + 1) - 1 + f)
                    for tb in range(TB):
                        part = h[:, tb, f * 512:f * 512 + 512]
                        n = mark(v.scalar_tensor_tensor(part, part, ALPHA, acc[2 * tb + f][:, :], ALU.mult, ALU.add))
                    after(n)
                    stats_done = half_stats(f)
                norm(2 * L + 1, stats_done)

        @block.tensor
        def _(pe):
            def passes(out_ap, lhs, rhs, start, stop):
                (lh, ll), (rh, rl) = lhs, rhs
                pe.matmul(out_ap, lh, rh, start=start, stop=False)
                pe.matmul(out_ap, lh, rl, start=False, stop=False)
                return pe.matmul(out_ap, ll, rh, start=False, stop=stop)

            right = [0]

            def wait_right():
                if right[0]:
                    pe.wait_ge(xT_ok, right[0])
                    right[0] = 0

            def item_columns(k, bank, i=0, period=2):
                for f in range(2):
                    half_columns(k, f, bank, i, period)

            def half_columns(k, f, bank, i, period):
                pe.wait_ge(u_lo_ok[f], k + 1 + i * period)
                if f == 1:
                    wait_right()
                for c in range(f * DC // 2, (f + 1) * DC // 2):
                    ins = passes(bank[:, 0:SEQ], (u_hi[:, k % 2, c], u_lo[:, k % 2, c]),
                                 (xT_hi[:, c, :], xT_lo[:, c, :]), c == 0, c == DC - 1)
                ins.then_inc(u_used[f], 1)

            def pair_tokens(L, n, banks):
                for f in range(2):
                    pe.wait_ge(u_lo_ok[f], item(L, n) + 2)
                    pe.wait_ge(pair_lo_ok[f], pairs_done(L, n + 1))
                    if f == 1:
                        wait_right()
                    for c in range(f * DC // 2, (f + 1) * DC // 2):
                        for tb in range(TB):
                            t = slice(tb * P, (tb + 1) * P)
                            ins = passes(banks[tb][:, 0:2 * P], (xT_hi[:, c, t], xT_lo[:, c, t]),
                                         (u_hi[:, :, c], u_lo[:, :, c]), c == 0, c == DC - 1)
                    ins.then_inc(u_used[f], 2)

            def in_item(L, n):
                if n >= 2:
                    pe.wait_ge(evac, evacs(L, n - 2))
                item_columns(item(L, n), pu[n % 2])

            def transpose_rows(s, src):
                for g in range(4):
                    half, tb = g // 2, g % 2
                    if s == 0:
                        pe.wait_ge(s_x, 16 * 2)
                    else:
                        pe.wait_ge(rows_ok, 4 * (s - 1) + g + 1)
                    if 4 * s + g >= 2:
                        pe.wait_ge(xT_ok, 4 * s + g - 1)
                    for c in range(4):
                        at = (4 * half + c) * P
                        ins = pe.transpose(px[g % 2][:, c * P:(c + 1) * P], src[:, tb, at:at + P], ident)
                    ins.then_inc(tr_out, 1)
                pe.wait_ge(xT_ok, 4 * s + 2)
                right[0] = 4 * s + 4

            def head(tiles, hh, m=None):
                base = (hh % 2) * HD + (0 if m is None else 32 * m)
                n = HD if m is None else 32
                return qkT[base:base + n, tiles + hh // 2, :]

            def products(su):
                if su > SOFT_A + SOFT_C:
                    pe.wait_ge(s_read, su - 1)
                    pe.wait_ge(fcum_ok, 1)
                elif su >= 1:
                    pe.wait_ge(s_read, su)
                for m in range(2):
                    if su < SOFT_A:
                        q, k = head(0, su, m), head(4, su, m)
                    elif su < SOFT_A + SOFT_C:
                        hh = 2 * (su - SOFT_A) + m
                        q, k = head(0, hh), head(4, hh)
                    else:
                        hh = 2 * (su - SOFT_A - SOFT_C) + m
                        q, k = head(8, hh), head(12, hh)
                    forget = su >= SOFT_A + SOFT_C
                    S = score_bank(su, m)
                    ins = pe.matmul(S[:, 0:2 * P], q[:, P:2 * P], k[:, 0:2 * P], start=True, stop=True)
                    if forget:
                        f0 = logf[:, 0, hh:hh + 1].to_broadcast([P, P])
                        f1 = logf[:, 1, hh:hh + 1].to_broadcast([P, P])
                        pe.matmul(S[:, 0:P], f0, ntri_le, start=False, stop=True, skip_group_check=True)
                        pe.matmul(S[:, P:2 * P], f0, nones, start=False, stop=True, skip_group_check=True)
                        pe.matmul(S[:, P:2 * P], f1, ntri_le, start=False, stop=True, skip_group_check=True)
                    ins = pe.matmul(S[:, 2 * P:W3], q[:, 0:P], k[:, 0:P], start=True, stop=True)
                    if forget:
                        ins = pe.matmul(S[:, 2 * P:W3], f0, ntri_le, start=False, stop=True, skip_group_check=True)
                ins.then_inc(s_out, 1)

            def weights_T(su):
                b = su % 2
                if su < SOFT_A:
                    pe.wait_ge(w_diff_ok, su + 1)
                    if su >= 2:
                        pe.wait_ge(wT_ok, su - 1)
                    for blk in range(3):
                        ins = pe.transpose(px[b][:, blk * P:(blk + 1) * P], diffw[b][:, blk * P:(blk + 1) * P], ident)
                    ins.then_inc(wT_out, 1)
                else:
                    pe.wait_ge(exp_ok, su + 1)
                    for m in range(2):
                        n = SOFT_A + 2 * (su - SOFT_A) + m
                        pe.wait_ge(wT_ok, n - 1)
                        for blk in range(3):
                            ins = pe.transpose(px[m][:, blk * P:(blk + 1) * P], logits[b][:, m, blk * P:(blk + 1) * P], ident)
                        ins.then_inc(wT_out, 1)

            def weigh(out_ap, wT, col):
                v0, v1 = vals[:, 0, col:col + HD], vals[:, 1, col:col + HD]
                pe.matmul(out_ap[:, 0:HD], wT[2], v0, start=True, stop=True)
                pe.matmul(out_ap[:, HD:2 * HD], wT[0], v0, start=True, stop=False)
                return pe.matmul(out_ap[:, HD:2 * HD], wT[1], v1, start=False, stop=True)

            def attend(su):
                b = su % 2
                reads = su if su < SOFT_A else su + HEADS
                if reads >= 2:
                    pe.wait_ge(pv_read, reads - 1)
                if su < SOFT_A:
                    pe.wait_ge(wT_ok, su + 1)
                    T = [probsT[b][:, 0, k * P:(k + 1) * P] for k in range(3)]
                    weigh(acc[2 + b][:, 0:2 * HD], T, su * HD).then_inc(pv_out, 1)
                else:
                    for m in range(2):
                        pe.wait_ge(wT_ok, SOFT_A + 2 * (su - SOFT_A) + m + 1)
                        T = [probsT[b][:, m, k * P:(k + 1) * P] for k in range(3)]
                        ins = weigh(acc[2 + b][:, m * 2 * HD:(m + 1) * 2 * HD], T, (2 * (su - SOFT_A) + m) * HD)
                    ins.then_inc(pv_out, 1)

            def stick_scores(i):
                if i >= NZ:
                    pe.wait_ge(z_cum_ok, i - NZ + 1)
                elif i == 2:
                    pe.wait_ge(s_read, SOFT_A)
                z = zbank[i % NZ]
                q, k = head(8, i), head(12, i)
                pe.matmul(z[:, 0:2 * P], k[:, 0:P], q[:, 0:2 * P], start=True, stop=False)
                pe.matmul(z[:, 2 * P:W3], k[:, P:2 * P], q[:, P:2 * P], start=False, stop=True).then_inc(z_out, 1)

            def log_sums():
                pe.wait_ge(evac, evacs(1, N_OUT - 1))
                pe.wait_ge(logf_ok, 1)
                for tb in range(TB):
                    F = pu[0][:, tb * HEADS:(tb + 1) * HEADS]
                    if tb == 0:
                        pe.matmul(F, tri_le, logf[:, 0, :], start=True, stop=True)
                    else:
                        pe.matmul(F, ones, logf[:, 0, :], start=True, stop=False)
                        pe.matmul(F, tri_le, logf[:, 1, :], start=False, stop=True).then_inc(fcum_out, 1)

            def run_units(L):
                units, per = layer_units(L)
                for i in range(len(units) + 2):
                    if i < len(units):
                        if L == 1 and i == SOFT_C:
                            log_sums()
                        products(units[i])
                        for n in range(16 + per * i, min(16 + per * i + per, N_OUT)):
                            in_item(L, n)
                    if L == 0 and i == len(units):
                        pe.wait_ge(evac, evacs(L, N_OUT - 1))
                        stick_scores(0)
                        stick_scores(1)
                        pe.wait_ge(s_cload, 64)
                    if 1 <= i <= len(units):
                        weights_T(units[i - 1])
                    if i >= 2:
                        attend(units[i - 2])

            for L in layers:
                transpose_rows(3 * L, h)
                for n in range(V_FIRST):
                    in_item(L, n)
                    if L == 0 and n == T5_AFTER:
                        pe.wait_ge(s_load, 16 * 4)
                        pe.matmul(px[0][0:HEADS, 0:REL], t5s[0:32, :], rowc[0:32, 0, :], start=True, stop=True
                                  ).then_inc(t5_out, 1)
                for m in range(0, V_ITEMS, 2):
                    if m >= 4:
                        pe.wait_ge(evac, evacs(L, V_FIRST + m - 3))
                    pair_tokens(L, V_FIRST + m, acc[m % 4:m % 4 + 2])
                if L == 1:
                    pe.wait_ge(wf_ok, 1)
                    for tb in range(TB):
                        t = slice(tb * P, (tb + 1) * P)
                        for c in range(DC):
                            ins = passes(px[0][:, tb * HEADS:(tb + 1) * HEADS], (xT_hi[:, c, t], xT_lo[:, c, t]),
                                         (wf_hi[:, c], wf_lo[:, c]), c == 0, c == DC - 1)
                    ins.then_inc(f_out, 1)
                pe.wait_ge(evac, evacs(L, 15))
                if L > 0:
                    pe.wait_ge(s_cload, 64 * (L + 1))
                if L == 0:
                    pe.wait_ge(rowb_ok, 1)
                    run_units(L)
                    for i in range(HEADS + 4):
                        if 2 <= i < HEADS:
                            stick_scores(i)
                        m = i - 2
                        if 0 <= m < HEADS:
                            pe.wait_ge(rem_ok, m + 1)
                            z, r = zbank[m % NZ], rem[m % NZ]
                            kw = dict(start=False, skip_group_check=True)
                            pe.matmul(z[:, 0:2 * P], tri_ge, r[:, 0:2 * P], stop=True, **kw)
                            pe.matmul(z[:, P:2 * P], ones, r[:, 2 * P:W3], stop=True, **kw)
                            pe.matmul(z[:, 2 * P:W3], tri_ge, r[:, 2 * P:W3], stop=True, **kw).then_inc(cum_out, 1)
                        m = i - 4
                        if m >= 0:
                            pe.wait_ge(w_stick_ok, m + 1)
                            pe.wait_ge(pv_read, SOFT_A + m - 1)
                            w = w_stick[m % NZ]
                            T = [w[:, P:2 * P], w[:, 2 * P:W3], w[:, 0:P]]
                            weigh(acc[2 + m % 2][:, 0:2 * HD], T, (HEADS + m) * HD).then_inc(pv_out, 1)
                else:
                    pe.wait_ge(f_abs, 1)
                    run_units(L)
                transpose_rows(3 * L + 1, o)
                for n in range(0, OUT_ITEMS, 2):
                    if n >= 4:
                        pe.wait_ge(mixed, OUT_ITEMS * L + n - 2)
                    pair_tokens(L, N_OUT + n, acc[n % 4:n % 4 + 2])
                transpose_rows(3 * L + 2, h)
                pe.wait_ge(s_keys, 16 * (L + 1))
                for e in range(Q_ITEMS + 1):
                    if e < Q_ITEMS:
                        if e >= 2:
                            pe.wait_ge(evac, evacs(L, N_Q + e - 2))
                        item_columns(item(L, N_Q + e), pu[e % 2])
                    if e > 0:
                        b = e - 1
                        pe.wait_ge(evac, evacs(L, N_Q + b))
                        if b % 4 == 0 and b > 0:
                            pe.wait_ge(sc_ok, 8 * L + 2 * (b // 4))
                        for tb in range(TB):
                            ins = pe.matmul(px[tb][:, (b % 4) * P:(b % 4 + 1) * P], qrow[:, b % 2, tb * P:(tb + 1) * P],
                                            keysT[:, b, :], start=True, stop=True)
                        ins.then_inc(q_out, 1)
                def ahead(r, i=0):
                    pe.wait_ge(evac, evacs(L, N_U + r - 2) + i * 2)
                    item_columns(item(L, N_U + r), pu[r % 2], i)

                with pe.Fori(0, AHEAD // 2 - 1) as i:
                    for r in range(2):
                        ahead(r, i)
                for tb in range(TB):
                    pe.wait_ge(sc_ok, 8 * (L + 1))
                    pe.wait_ge(tab_ok, TB * L + tb + 1)
                    for n in range(3):
                        ins = pe.transpose(px[tb][:, n * P:(n + 1) * P], sc[:, tb, (n + 1) * P:(n + 2) * P], ident)
                    ins.then_inc(tabT_out, 1)
                ahead(AHEAD - 2)
                ahead(AHEAD - 1)

                def gates_group(q, i=0):
                    if q % 4 == 3:
                        pe.wait_ge(oh_ok_act, GROUPS // 4 * L + q // 4 + 1 + i * 4)
                    else:
                        pe.wait_ge(oh_ok, GROUPS // 4 * 3 * L + q // 4 * 3 + q % 4 + 1 + i * 12)
                    if q >= 4:
                        pe.wait_ge(g_copied, GROUPS * L + q - 3 + i * 16)
                    for t in range(GROUP):
                        ins = pe.matmul(acc[q % 4][:, t * NKEYS:(t + 1) * NKEYS], onehots[:, q % 4, 0, t],
                                        onehots[:, q % 4, 1, t], start=True, stop=True)
                    ins.then_inc(g_out, 1)

                def groups_and_item(r, i=0):
                    k = item(L, N_U + AHEAD + r)
                    for f in range(2):
                        gates_group(4 * r + 2 * f, i)
                        gates_group(4 * r + 2 * f + 1, i)
                        if f == 0:
                            pe.wait_ge(evac, evacs(L, N_U + AHEAD + r - 2) + i * RAW)
                        half_columns(k, f, pu[r % 2], i, RAW)

                for r in range(RAW):
                    groups_and_item(r)
                with pe.Fori(0, LATE // RAW - 1) as i:
                    for r in range(RAW, 2 * RAW):
                        groups_and_item(r, i)

                def v_item(r, i=0, first=False, last=False):
                    j = E_ * L + r
                    pe.wait_ge(w_ok, j + 1 + i * 2)
                    for f in range(2):
                        pe.wait_ge(v_lo_ok, 2 * j + f + 1 + i * 4)
                        half = slice(f * 512, (f + 1) * 512)
                        for tb in range(TB):
                            t = slice(tb * P, (tb + 1) * P)
                            ins = passes(acc[2 * tb + f][:, :], (w_hi[:, j % 2, t], w_lo[:, j % 2, t]),
                                         (v_hi[:, j % 2, half], v_lo[:, j % 2, half]), first, last)
                        ins.then_inc(v_used, 1)

                def u_item(r, i=0):
                    pe.wait_ge(evac, evacs(L, N_U + AHEAD + LATE + r - 2) + i * 2)
                    item_columns(item(L, N_U + AHEAD + LATE + r), pu[r % 2], i)

                u_item(0)
                u_item(1)
                pe.wait_ge(g_copied, GROUPS * (L + 1))
                for r in range(2):
                    v_item(r, first=(r == 0))
                    u_item(2 + r)
                n = REST
                with pe.Fori(0, n // 2 - 2) as i:
                    for r in range(2):
                        v_item(2 + r, i)
                        u_item(4 + r, i)
                with pe.Fori(0, (E_ - n) // 2) as i:
                    for r in range(2):
                        v_item(n - 2 + r, i)
                v_item(E_ - 2)
                v_item(E_ - 1, last=True)


def tables():
    p, f = np.arange(P)[:, None], np.arange(P)[None, :]
    ident = (p == f)
    iota = np.broadcast_to(f, (P, P))
    ge, le = (p >= f), (p <= f)
    one = np.ones((P, P))
    q3 = np.concatenate([np.arange(256), np.arange(128)])[None, :]
    past = q3 > p
    k3 = np.concatenate([np.arange(256) - 128, np.arange(128)])[None, :]
    causal = k3 <= p
    cols = [ident, iota, ge, le, -1.0 * le, one, -one, -1.0 * past, np.where(past, 0, NEG), np.where(causal, 0, NEG)]
    consts = np.concatenate([np.asarray(c, np.float32) for c in cols], axis=1)
    dist = 255 - np.arange(REL)
    n = np.maximum(dist, 0)
    nf = np.maximum(n, 1).astype(np.float32)
    large = 16 + (np.log(nf / np.float32(16)) / np.float32(np.log(8.0)) * np.float32(16)).astype(np.int32)
    bucket = np.where(n < 16, n, np.minimum(large, 31))
    onehot = (np.arange(32)[:, None] == bucket[None, :]).astype(np.float32)
    times = sum(((n % dil == 0) & (n <= win)).astype(np.int32) for win, dil in ((128, 1), (512, 4), (2048, 16)))
    dil = np.where((dist >= 0) & (times > 0), np.log(np.maximum(times, 1)), NEG)
    full = np.where(dist >= 0, 0.0, NEG)
    relmask = np.broadcast_to(np.stack([full, dil])[None], (HEADS, 2, REL)).astype(np.float32)
    return consts, onehot, np.ascontiguousarray(relmask)


def lay_out(x, t5_bias, ab_w_in, ab_lambda, ab_subln_g, ab_w_out, cd_w_in, cd_b_f, cd_w_out,
            peer_w_q, peer_sub_keys, peer_u, peer_v, ln_g, ln_b):
    a = {k: np.asarray(v) for k, v in dict(
        x=x, t5=t5_bias, ab_in=ab_w_in, lam=ab_lambda, sub=ab_subln_g, ab_out=ab_w_out, cd_in=cd_w_in, bf=cd_b_f,
        cd_out=cd_w_out, wq=peer_w_q, keys=peer_sub_keys, u=peer_u, v=peer_v, g=ln_g, b=ln_b).items()}

    def tiles(w):
        return w.reshape(DC, P, -1, P).transpose(2, 1, 0, 3).reshape(-1, P, D)

    stream = []
    for L, (w_in, w_out) in enumerate(((a["ab_in"][0], a["ab_out"][0]), (a["cd_in"][0], a["cd_out"][0]))):
        t = tiles(w_in[:, :IN_ITEMS * P])
        stream += [t[0:12], t[20:24], t[12:20], tiles(w_out), tiles(a["wq"][L])]
        u = a["u"][L].reshape(P, NKEYS, DC, P).transpose(1, 3, 2, 0).reshape(NKEYS, P, D)
        stream.append(u)
    consts, onehot, relmask = tables()
    return {
        "x": a["x"][0],
        "u_stream": np.concatenate(stream),
        "v_stream": np.ascontiguousarray(a["v"].reshape(LAYERS, P, NKEYS, D).transpose(0, 2, 1, 3).reshape(-1, P, D)),
        "keys": np.ascontiguousarray(a["keys"].transpose(0, 4, 1, 2, 3).reshape(LAYERS, P, Q_ITEMS, NKEYS)),
        "t5": a["t5"], "onehot": onehot, "relmask": relmask,
        "lam_vecs": a["lam"].reshape(-1), "subln": a["sub"].reshape(-1),
        "w_f": np.ascontiguousarray(a["cd_in"][0][:, IN_ITEMS * P:].reshape(DC, P, HEADS).transpose(1, 0, 2).reshape(P, -1)),
        "b_f": a["bf"].reshape(-1),
        "ln_g": a["g"].reshape(2 * LAYERS, D), "ln_b": a["b"].reshape(2 * LAYERS, D),
        "consts": consts,
    }


def kernel(**inputs):
    import concourse.bacc as bacc
    from concourse.bass_utils import run_bass_kernel_spmd

    arrays = {k: np.ascontiguousarray(v) for k, v in lay_out(**inputs).items()}
    nc = bacc.Bacc("TRN2", target_bir_lowering=False, num_devices=1, dynamic_dma_scratch_size=1024)
    aps = {k: nc.dram_tensor(f"in_{k}", v.shape, mybir.dt.from_np(v.dtype), kind="ExternalInput").ap()
           for k, v in arrays.items()}
    result = nc.dram_tensor("result", (SEQ, D), F32, kind="ExternalOutput").ap()
    build_program(nc, out=result, **aps)
    r = run_bass_kernel_spmd(nc, [{f"in_{k}": v for k, v in arrays.items()}], core_ids=[0])
    return r.results[0]["result"].reshape(1, SEQ, D)
```
